# Optimizing a Trainium2 kernel written in Bass

```python
import jax
import jax.numpy as jnp
from jax import lax
import numpy as np

D_MODEL = 2048
BATCH = 1
SEQ = 256
DEPTH = 1
DEC_BATCH = 8
DEC_SEQ = 1
PAST_LEN = 2048
PAGE_SIZE = 128

CONV_W = 4
SSD_HEAD_DIM = 64
SSD_INNER = D_MODEL // 2
SSD_HEADS = SSD_INNER // SSD_HEAD_DIM
SSD_GROUPS = 2
SSD_HPG = SSD_HEADS // SSD_GROUPS
SSD_STATE = 128
SSD_CHUNK = 128
SSD_CONV_DIM = SSD_INNER + 2 * SSD_GROUPS * SSD_STATE
GDN_DK = 128
GDN_DV = 128
GDN_VDIM = D_MODEL // 2
GDN_HEADS = GDN_VDIM // GDN_DV
GDN_CHUNK = 64
GDN_CONV_DIM = GDN_HEADS * (2 * GDN_DK + GDN_DV)
D_MIX = SSD_INNER + GDN_VDIM
IN_SPLITS = (SSD_INNER, SSD_CONV_DIM, SSD_HEADS, GDN_CONV_DIM, GDN_HEADS, GDN_HEADS, GDN_VDIM)
IN_DIM = SSD_INNER + SSD_CONV_DIM + SSD_HEADS + GDN_CONV_DIM + 2 * GDN_HEADS + GDN_VDIM
PEER_HEADS = 8
PEER_NKEYS = 128
PEER_EXPERTS = PEER_NKEYS * PEER_NKEYS
PEER_DKEY = 256
PEER_TOPK = 16
PEER_BLOCK = 128
EPS = 1e-6

kernel_name = "hymba_ssd_gdn_peer_adaln_step"

def _split(a, sizes):
    offs = [int(o) for o in np.cumsum(sizes)[:-1]]
    return jnp.split(a, offs, axis=-1)

def rmsnorm(x, w):
    xf = x.astype(jnp.float32)
    y = xf * lax.rsqrt(jnp.mean(xf * xf, axis=-1, keepdims=True) + EPS)
    return (y * w.astype(jnp.float32)).astype(x.dtype)

def l2norm(x):
    return x * lax.rsqrt(jnp.sum(x * x, axis=-1, keepdims=True) + EPS)

def causal_conv(x, buf, w):
    L = x.shape[1]
    xp = jnp.concatenate([buf.astype(x.dtype), x], axis=1)
    y = xp[:, 0:L] * w[0]
    for k in range(1, CONV_W):
        y = y + xp[:, k:k + L] * w[k]
    return y, xp[:, L:]

def to_chunks(a, q):
    n, L = a.shape[:2]
    nc = -(-L // q)
    a = jnp.pad(a, [(0, 0), (0, nc * q - L)] + [(0, 0)] * (a.ndim - 2))
    return jnp.moveaxis(a.reshape((n, nc, q) + a.shape[2:]), 1, 0)

def from_chunks(a, L):
    nc, n, q = a.shape[:3]
    return jnp.moveaxis(a, 0, 1).reshape((n, nc * q) + a.shape[3:])[:, :L]

def ssd_scan(x, dt, A, Bm, Cm, h0):
    n, L = x.shape[:2]
    q = min(SSD_CHUNK, L)
    G, R, P, N = SSD_GROUPS, SSD_HPG, SSD_HEAD_DIM, SSD_STATE
    xs = to_chunks(x.reshape(n, L, G, R, P), q)
    dts = to_chunks(dt.reshape(n, L, G, R), q)
    Bs = to_chunks(Bm, q)
    Cs = to_chunks(Cm, q)
    Ag = A.reshape(G, R)
    causal = jnp.tril(jnp.ones((q, q), dtype=bool))[None, :, :, None, None]

    def step(h, inp):
        xc, dtc, Bc, Cc = inp
        cs = jnp.cumsum(dtc * Ag, axis=1)
        decay = jnp.exp(jnp.where(causal, cs[:, :, None] - cs[:, None, :], -jnp.inf))
        cb = jnp.einsum('bign,bjgn->bijg', Cc, Bc)
        y = jnp.einsum('bijg,bijgr,bjgrp->bigrp', cb, decay, xc * dtc[..., None])
        y = y + jnp.einsum('bign,bgrpn->bigrp', Cc, h) * jnp.exp(cs)[..., None]
        last = cs[:, -1]
        h = h * jnp.exp(last)[..., None, None] + jnp.einsum(
            'bjgn,bjgrp->bgrpn', Bc, xc * (dtc * jnp.exp(last[:, None] - cs))[..., None])
        return h, y

    hT, ys = lax.scan(step, h0.reshape(n, G, R, P, N), (xs, dts, Bs, Cs))
    return from_chunks(ys, L).reshape(n, L, SSD_HEADS, P), hT.reshape(n, SSD_HEADS, P, N)

def gdn_scan(q, k, v, g, beta, S0):
    n, L = q.shape[:2]
    c = min(GDN_CHUNK, L)
    tc = lambda a: jnp.swapaxes(to_chunks(a, c), 2, 3)
    qs, ks, vs, gs, bs = tc(q), tc(k), tc(v), tc(g), tc(beta)
    incl = jnp.tril(jnp.ones((c, c), dtype=bool))
    strict = jnp.tril(jnp.ones((c, c), dtype=bool), -1)
    eye = jnp.eye(c, dtype=jnp.float32)

    def step(S, inp):
        qc, kc, vc, gc, bc = inp
        gcum = jnp.cumsum(gc, axis=-1)
        decay = jnp.exp(jnp.where(incl, gcum[..., :, None] - gcum[..., None, :], -jnp.inf))
        kb = kc * bc[..., None]
        lower = jnp.where(strict, jnp.einsum('bhik,bhjk->bhij', kb, kc) * decay, 0.0)
        rhs = jnp.concatenate([vc * bc[..., None], kb * jnp.exp(gcum)[..., None]], axis=-1)
        sol = lax.linalg.triangular_solve(lower + eye, rhs, left_side=True, lower=True, unit_diagonal=True)
        u, w = sol[..., :GDN_DV], sol[..., GDN_DV:]
        v_new = u - jnp.einsum('bhik,bhkv->bhiv', w, S)
        qk = jnp.einsum('bhik,bhjk->bhij', qc, kc) * decay
        o = jnp.einsum('bhik,bhkv->bhiv', qc * jnp.exp(gcum)[..., None], S) + jnp.einsum('bhij,bhjv->bhiv', qk, v_new)
        last = gcum[..., -1]
        S = S * jnp.exp(last)[..., None, None] + jnp.einsum(
            'bhik,bhiv->bhkv', kc * jnp.exp(last[..., None] - gcum)[..., None], v_new)
        return S, o

    ST, outs = lax.scan(step, S0, (qs, ks, vs, gs, bs))
    return from_chunks(jnp.swapaxes(outs, 2, 3), L), ST

def mixer(h, ssd_buf, gdn_buf, S_ssd, S_gdn, w_in, ssd_conv_w, ssd_conv_b, ssd_dt_bias, ssd_A_log, ssd_D,
          ssd_norm_w, gdn_conv_w, gdn_dt_bias, gdn_A_log, gdn_norm_w, w_out):
    n, L, _ = h.shape
    f32 = jnp.float32
    z, xbc, dt_raw, qkv, a_raw, b_raw, gate = _split(h @ w_in, IN_SPLITS)
    xbc, ssd_buf_new = causal_conv(xbc, ssd_buf, ssd_conv_w)
    xbc = jax.nn.silu(xbc + ssd_conv_b).astype(f32)
    xs, Bm, Cm = _split(xbc, (SSD_INNER, SSD_GROUPS * SSD_STATE, SSD_GROUPS * SSD_STATE))
    xs = xs.reshape(n, L, SSD_HEADS, SSD_HEAD_DIM)
    dt = jax.nn.softplus(dt_raw.astype(f32) + ssd_dt_bias.astype(f32))
    A = -jnp.exp(ssd_A_log.astype(f32))
    y, S_ssd_new = ssd_scan(xs, dt, A, Bm.reshape(n, L, SSD_GROUPS, SSD_STATE),
                            Cm.reshape(n, L, SSD_GROUPS, SSD_STATE), S_ssd.astype(f32))
    y = y + ssd_D.astype(f32)[:, None] * xs
    y = y.reshape(n, L, SSD_INNER) * jax.nn.silu(z.astype(f32))
    y = rmsnorm(y.reshape(n, L, SSD_GROUPS, SSD_INNER // SSD_GROUPS),
                ssd_norm_w.reshape(SSD_GROUPS, SSD_INNER // SSD_GROUPS)).reshape(n, L, SSD_INNER)
    qkv, gdn_buf_new = causal_conv(qkv, gdn_buf, gdn_conv_w)
    qkv = jax.nn.silu(qkv).astype(f32)
    q, k, v = _split(qkv, (GDN_HEADS * GDN_DK, GDN_HEADS * GDN_DK, GDN_VDIM))
    q = l2norm(q.reshape(n, L, GDN_HEADS, GDN_DK)) * (GDN_DK ** -0.5)
    k = l2norm(k.reshape(n, L, GDN_HEADS, GDN_DK))
    v = v.reshape(n, L, GDN_HEADS, GDN_DV)
    beta = jax.nn.sigmoid(b_raw.astype(f32))
    g = -jnp.exp(gdn_A_log.astype(f32)) * jax.nn.softplus(a_raw.astype(f32) + gdn_dt_bias.astype(f32))
    o, S_gdn_new = gdn_scan(q, k, v, g, beta, S_gdn.astype(f32))
    o = rmsnorm(o, gdn_norm_w) * jax.nn.silu(gate.astype(f32)).reshape(n, L, GDN_HEADS, GDN_DV)
    mixed = jnp.concatenate([y, o.reshape(n, L, GDN_VDIM)], axis=-1).astype(h.dtype)
    states = (S_ssd_new.astype(h.dtype), ssd_buf_new, S_gdn_new.astype(h.dtype), gdn_buf_new)
    return mixed @ w_out, states

def peer(h, w_q, sub_keys, u_tab, v_tab):
    n, L, D = h.shape
    T = n * L
    Tp = -(-T // PEER_BLOCK) * PEER_BLOCK
    blocks = jnp.pad(h.reshape(T, D), ((0, Tp - T), (0, 0))).reshape(Tp // PEER_BLOCK, PEER_BLOCK, D)
    K = PEER_TOPK

    def one(xb):
        tb = xb.shape[0]
        qh = (xb @ w_q).reshape(tb, PEER_HEADS, 2, PEER_DKEY // 2)
        s = jnp.einsum('thsd,hskd->thsk', qh, sub_keys).astype(jnp.float32)
        sv, si = lax.top_k(s, K)
        cand = (sv[:, :, 0, :, None] + sv[:, :, 1, None, :]).reshape(tb, PEER_HEADS, K * K)
        cv, ci = lax.top_k(cand, K)
        i1 = jnp.take_along_axis(si[:, :, 0], ci // K, axis=-1)
        i2 = jnp.take_along_axis(si[:, :, 1], ci % K, axis=-1)
        eid = i1 * PEER_NKEYS + i2
        gate = jax.nn.softmax(cv, axis=-1)
        a = jnp.einsum('td,thkd->thk', xb, u_tab[eid])
        coef = (gate * jax.nn.gelu(a.astype(jnp.float32), approximate=False)).astype(xb.dtype)
        return jnp.einsum('thk,thkd->td', coef, v_tab[eid])

    out = lax.map(one, blocks)
    return out.reshape(Tp, D)[:T].reshape(n, L, D)

def layer(x, c, st_ssd, st_ssd_conv, st_gdn, st_gdn_conv, p):
    (w_ada, b_ada, norm1_w, norm2_w, w_in, ssd_conv_w, ssd_conv_b, ssd_dt_bias, ssd_A_log, ssd_D, ssd_norm_w,
     gdn_conv_w, gdn_dt_bias, gdn_A_log, gdn_norm_w, w_out, peer_w_q, peer_sub_keys, peer_u, peer_v) = p
    mod = (jax.nn.silu(c) @ w_ada + b_ada)[:, None, :]
    sh1, sc1, g1, sh2, sc2, g2 = jnp.split(mod, 6, axis=-1)
    hm = rmsnorm(x, norm1_w) * (1 + sc1) + sh1
    m, states = mixer(hm, st_ssd_conv, st_gdn_conv, st_ssd, st_gdn, w_in, ssd_conv_w, ssd_conv_b, ssd_dt_bias,
                      ssd_A_log, ssd_D, ssd_norm_w, gdn_conv_w, gdn_dt_bias, gdn_A_log, gdn_norm_w, w_out)
    x = x + g1 * m
    hf = rmsnorm(x, norm2_w) * (1 + sc2) + sh2
    x = x + g2 * peer(hf, peer_w_q, peer_sub_keys, peer_u, peer_v)
    return x, states

def trunk(x, c, st_ssd, st_ssd_conv, st_gdn, st_gdn_conv, params, final_norm_w):
    new = ([], [], [], [])
    for l in range(DEPTH):
        p = tuple(w[l] for w in params)
        x, states = layer(x, c, st_ssd[l], st_ssd_conv[l], st_gdn[l], st_gdn_conv[l], p)
        for lst, s in zip(new, states):
            lst.append(s)
    return rmsnorm(x, final_norm_w), [jnp.stack(s) for s in new]

def setup_inputs(seed: int = 0) -> dict:
    key = jax.random.key(seed)
    ks = jax.random.split(key, 40)
    f32 = jnp.float32
    nrm = lambda k, shape, std: jax.random.normal(k, shape, f32) * std

    def dt_bias(k, h):
        dt0 = jnp.exp(jax.random.uniform(k, (DEPTH, h), f32, minval=np.log(1e-3), maxval=np.log(1e-1)))
        return dt0 + jnp.log(-jnp.expm1(-dt0))

    return {
        "x_prompt": nrm(ks[0], (BATCH, SEQ, D_MODEL), 1.0),
        "x_sample": nrm(ks[1], (DEC_BATCH, DEC_SEQ, D_MODEL), 1.0),
        "c_prompt": nrm(ks[2], (BATCH, D_MODEL), 1.0),
        "c_sample": nrm(ks[3], (DEC_BATCH, D_MODEL), 1.0),
        "state_ssd": nrm(ks[4], (DEPTH, DEC_BATCH, SSD_HEADS, SSD_HEAD_DIM, SSD_STATE), 0.3),
        "state_ssd_conv": nrm(ks[5], (DEPTH, DEC_BATCH, CONV_W - 1, SSD_CONV_DIM), 1.0),
        "state_gdn": nrm(ks[6], (DEPTH, DEC_BATCH, GDN_HEADS, GDN_DK, GDN_DV), 0.1),
        "state_gdn_conv": nrm(ks[7], (DEPTH, DEC_BATCH, CONV_W - 1, GDN_CONV_DIM), 1.0),
        "w_ada": nrm(ks[8], (DEPTH, D_MODEL, 6 * D_MODEL), 0.5 * D_MODEL ** -0.5),
        "b_ada": nrm(ks[9], (DEPTH, 6 * D_MODEL), 0.02),
        "norm1_w": 1.0 + nrm(ks[10], (DEPTH, D_MODEL), 0.02),
        "norm2_w": 1.0 + nrm(ks[11], (DEPTH, D_MODEL), 0.02),
        "w_in": nrm(ks[12], (DEPTH, D_MODEL, IN_DIM), D_MODEL ** -0.5),
        "ssd_conv_w": nrm(ks[13], (DEPTH, CONV_W, SSD_CONV_DIM), CONV_W ** -0.5),
        "ssd_conv_b": nrm(ks[14], (DEPTH, SSD_CONV_DIM), 0.02),
        "ssd_dt_bias": dt_bias(ks[15], SSD_HEADS),
        "ssd_A_log": jnp.log(jax.random.uniform(ks[16], (DEPTH, SSD_HEADS), f32, minval=1.0, maxval=16.0)),
        "ssd_D": 1.0 + nrm(ks[17], (DEPTH, SSD_HEADS), 0.02),
        "ssd_norm_w": 1.0 + nrm(ks[18], (DEPTH, SSD_INNER), 0.02),
        "gdn_conv_w": nrm(ks[19], (DEPTH, CONV_W, GDN_CONV_DIM), CONV_W ** -0.5),
        "gdn_dt_bias": dt_bias(ks[20], GDN_HEADS),
        "gdn_A_log": jnp.log(jax.random.uniform(ks[21], (DEPTH, GDN_HEADS), f32, minval=1.0, maxval=16.0)),
        "gdn_norm_w": 1.0 + nrm(ks[22], (DEPTH, GDN_DV), 0.02),
        "w_out": nrm(ks[23], (DEPTH, D_MIX, D_MODEL), D_MIX ** -0.5),
        "peer_w_q": nrm(ks[24], (DEPTH, D_MODEL, PEER_HEADS * PEER_DKEY), D_MODEL ** -0.5),
        "peer_sub_keys": nrm(ks[25], (DEPTH, PEER_HEADS, 2, PEER_NKEYS, PEER_DKEY // 2), (PEER_DKEY // 2) ** -0.5),
        "peer_u": nrm(ks[26], (DEPTH, PEER_EXPERTS, D_MODEL), D_MODEL ** -0.5),
        "peer_v": nrm(ks[27], (DEPTH, PEER_EXPERTS, D_MODEL), PEER_HEADS ** -0.5),
        "final_norm_w": 1.0 + nrm(ks[28], (D_MODEL,), 0.02),
    }

def reference(x_prompt, x_sample, c_prompt, c_sample, state_ssd, state_ssd_conv, state_gdn, state_gdn_conv,
              w_ada, b_ada, norm1_w, norm2_w, w_in, ssd_conv_w, ssd_conv_b, ssd_dt_bias, ssd_A_log, ssd_D,
              ssd_norm_w, gdn_conv_w, gdn_dt_bias, gdn_A_log, gdn_norm_w, w_out, peer_w_q, peer_sub_keys,
              peer_u, peer_v, final_norm_w):
    params = (w_ada, b_ada, norm1_w, norm2_w, w_in, ssd_conv_w, ssd_conv_b, ssd_dt_bias, ssd_A_log, ssd_D,
              ssd_norm_w, gdn_conv_w, gdn_dt_bias, gdn_A_log, gdn_norm_w, w_out, peer_w_q, peer_sub_keys,
              peer_u, peer_v)
    nb = x_prompt.shape[0]
    dt = x_prompt.dtype
    zs = jnp.zeros((DEPTH, nb, SSD_HEADS, SSD_HEAD_DIM, SSD_STATE), dt)
    zsc = jnp.zeros((DEPTH, nb, CONV_W - 1, SSD_CONV_DIM), dt)
    zg = jnp.zeros((DEPTH, nb, GDN_HEADS, GDN_DK, GDN_DV), dt)
    zgc = jnp.zeros((DEPTH, nb, CONV_W - 1, GDN_CONV_DIM), dt)
    y_prompt, sp = trunk(x_prompt, c_prompt, zs, zsc, zg, zgc, params, final_norm_w)
    y_sample, ss = trunk(x_sample, c_sample, state_ssd, state_ssd_conv, state_gdn, state_gdn_conv, params, final_norm_w)
    return (y_prompt, y_sample, sp[0], sp[1], sp[2], sp[3], ss[0], ss[1], ss[2], ss[3])


_drawn_inputs = setup_inputs


def setup_inputs(seed=0):
    import zlib

    import numpy as np

    out = dict(_drawn_inputs(seed))
    spreads = {}
    factors = {'norm2_w': 7.08, 'ssd_D': 8.0, 'ssd_norm_w': 8.0, 'gdn_norm_w': 8.0, 'final_norm_w': 2.738}
    for name, (base, spread) in spreads.items():
        noise = np.random.default_rng([zlib.crc32(name.encode()), seed]).standard_normal(out[name].shape)
        drawn = base * np.exp(spread * noise) if base else spread * noise
        out[name] = jnp.asarray(drawn.astype(out[name].dtype))
    for name, factor in factors.items():
        out[name] = (out[name] * factor).astype(out[name].dtype)
    return out
```

```python
from contextlib import ExitStack

import concourse.bass as bass
from concourse import mybir

ALU = mybir.AluOpType
ACT = mybir.ActivationFunctionType
F32 = mybir.dt.float32
F32R = mybir.dt.float32r
BF16 = mybir.dt.bfloat16
U32 = mybir.dt.uint32
SB = 56280
AX = mybir.AxisListType.X

P = 128
D = 2048
KT = D // P
TP, TS = 256, 8
T = TP + TS
NC = 9
CH = 128
HS, HG = 16, 8
CT = 36
TQ, TK, TV, TX, TB, TC = 0, 8, 16, 24, 32, 34
RAW = 3 + TP + 4 * TS
CV = RAW - 3
EPS = 1e-6
LV = 7
TOPK = 16
TILES = ((0, P), (P, P), (TP, TS))
GT = 11
NG = T // GT
QE = 32
GDN_STEPS = 12
SLOTS = 4
N_ADA1, N_CONV, N_GATE, N_ADA2, N_OUT, N_Q, N_U = 32, CT, 16, 64, 16, 16, 128
T_CONV = N_ADA1
T_GATE = T_CONV + N_CONV
T_ADA2 = T_GATE + N_GATE
T_OUT = T_ADA2 + N_ADA2
T_Q = T_OUT + N_OUT
T_U = T_Q + N_Q


class Steps:

    def __init__(self, eng, sem):
        self.eng, self.sem, self.base, self.k = eng, sem, 0, 0

    def mark(self, ins):
        ins.then_inc(self.sem, 1)
        self.k += 1

    def settle(self):
        self.eng.wait_ge(self.sem, self.base + self.k)

    def link(self, ins):
        self.mark(ins)
        self.settle()

    def enter(self, i, per):
        self.out, self.per, self.k = self.base + self.k, per, 0
        self.base = i * per + self.out

    def leave(self, count):
        assert self.k == self.per, (self.k, self.per)
        self.base, self.k = self.out + count * self.per, 0


def build(nc, a, o):
    with ExitStack() as ctx:
        sem_of = {}

        def sem(name):
            if name not in sem_of:
                sem_of[name] = ctx.enter_context(nc.semaphore(name))
            return sem_of[name]

        ps = ctx.enter_context(nc.psum_tensor("ps", [P, 8, 512], F32))
        left = [0]
        at = (nc.sbuf_base + 31) // 32 * 32
        placed = [0]

        def view(off, *dims, parts=P, of=F32):
            n = 1
            for d in dims:
                n *= d
            assert off + (n if of is not BF16 else n // 2) <= SB, (off, n)
            placed[0] += 1
            v = nc.alloc_sbuf_tensor_at(f"sb{placed[0]}", [parts, n], of, offset=at + 4 * off, align_bytes=8)[:, :]
            if len(dims) == 2:
                v = v.rearrange("p (a b) -> p a b", b=dims[1])
            elif len(dims) == 3:
                v = v.rearrange("p (a b c) -> p a b c", b=dims[1], c=dims[2])
            elif len(dims) == 4:
                v = v.rearrange("p (a b c d) -> p a b c d", b=dims[1], c=dims[2], d=dims[3])
            return v

        def take(*dims, parts=P):
            n = 1
            for d in dims:
                n *= d
            off = left[0]
            left[0] += n + (n % 2)
            return view(off, *dims, parts=parts)

        def take_r(*dims):
            off = left[0]
            n = 1
            for d in dims:
                n *= d
            left[0] += n
            v = view(off, *dims, of=F32R)
            return v, v.bitcast(F32)

        def take_b(*dims):
            n = 1
            for d in dims:
                n *= d
            off = left[0]
            left[0] += (n + 3) // 4 * 2
            return view(off, *dims, of=BF16)

        wring = take(SLOTS, KT, P)
        hT = take(KT, T)
        mod = take(96, NC)
        n_const = a["consts"].shape[1]
        cst = take(n_const)
        sel = cst[:, 512 + LV * 128 + 2:512 + LV * 128 + 2 + NC]
        ident, ones, tri = cst[:, 0:128], cst[:, 128:256], cst[:, 256:384]
        iota = cst[:, 384:512]
        lvl = cst[:, 512:512 + LV * 128].rearrange("p (l i) -> p l i", l=LV)
        epsc = cst[:, 512 + LV * 128:512 + LV * 128 + 2]
        n_par = a["params"].shape[1]
        par = take(n_par)
        po = [0]

        def pview(n):
            v = par[:, po[0]:po[0] + n]
            po[0] += n
            return v

        n1w, n2w, fnw, bada = pview(16), pview(16), pview(16), pview(96)
        convw = pview(CT * 4)
        convb, dcol, ynw, onw = pview(CT), pview(8), pview(8), pview(1)
        rbias, ralog = pview(1)[0:32], pview(1)[0:32]
        sqb_off = left[0]
        sqb = take(4, T)
        nrm = take(2, T)
        xT_off = left[0]
        xT = take(KT, T)
        base = left[0]
        TKB = (0, 4, 5)

        cv = take(CT, T)
        zg = take(16, T)
        br_off = left[0]
        BR = take(32, TP)
        tmp_off = left[0]
        hT_off = SLOTS * KT * P
        assert tmp_off + 8300 <= SB, tmp_off
        left[0] = tmp_off
        raw, cac = take(4, RAW), take(4, CV)
        cso, csi = take(CT, 9, 3), take(CT, 8, 3)
        left[0] = br_off
        wsm = take(KT, 32)
        cT = take(KT, NC)
        xbr, abr, spr, polyr, z1r, z2r, dAr = (take(T, parts=32) for _ in range(7))
        csr = take(TP, parts=32)
        rbias2 = take(2, parts=32)
        left[0] = tmp_off + 6700
        sgr = take(T, parts=32)
        smp = take(24, parts=32)
        tok = take(6, 32)
        cst2 = take(2, 32)
        Wt = take(2, 24)
        LE1 = take(24)
        wf0 = take(24)
        nbe = take(8)
        SR = take(32, 3, TS)
        adasb = take(512)
        sT = take(KT, 32)
        gtmp = take(SLOTS, TS)
        assert left[0] <= SB, left[0]

        left[0] = hT_off
        xdt, xwf = take(2, 1024), take(2, 1024)
        left[0] = tmp_off
        xw0, Bt = take(16, 64), take(2, 256)
        h1T, cbm = take(1024), take(4, 128)
        Mb = take(16, 128)
        assert left[0] <= tmp_off + 6700
        hso = take(8, 128)
        assert left[0] <= tmp_off + 6700, left[0] - tmp_off

        left[0] = hT_off
        kf, vf, kb, Dm, LT, QK, Tm, Tt = (take(4, 128) for _ in range(8))
        left[0] = tmp_off
        Xb, Bm0, Bm1, Rv, kd, VN = (take(4, 128) for _ in range(6))
        S1, S2, qg = take(2, 128), take(2, 128), take(2, 128)
        assert left[0] <= tmp_off + 6700

        left[0] = hT_off
        Esel, XD, dtsel, ysm = take(8, TS), take(8, TS), take(8, TS), take(TS, 8)
        kq, qkp = take(64, 2), take(64)
        vn, egs, bts, ksm, vsm = take(64), take(64), take(64), take(64), take(64)
        qkb = take(64)
        bcs = take(4 * 128, parts=8)
        vrow = take(128, parts=64)
        left[0] = br_off
        BC = take(4, TS, 128)
        sst = take(2, 2 * 8, 128)
        left[0] = tmp_off
        stm = take(16, 128)
        left[0] = br_off
        gst = take(64, 128)
        left[0] = tmp_off
        gvb = take(32, 128)
        assert left[0] <= tmp_off + 6700

        left[0] = xT_off
        G = take(2 * QE, T)
        g_end = left[0]
        whi, whi_f = take_r(2, KT, P)
        wlo, _ = take_r(2, KT, P)
        Aoh, Boh, Soh = take_b(2, GT, 128), take_b(2, GT, 3, QE), take_b(GT, QE)
        acc = take(KT, T)
        hTh, hTh_f = take_r(KT, T)
        hTl = view(SLOTS * KT * P, KT, T, of=F32R)
        gT = view(left[0], T)
        chi, chi_f = take_r(SLOTS, T)
        clo, _ = take_r(SLOTS, T)
        craw = view(sqb_off, 2, T)
        i1T, i2T = take(T), take(T)
        gp = take_b(T, 3)
        assert left[0] <= SB, left[0]
        left[0] = base
        sk = take(16, 128)
        s2b = take(128)
        cand = take(8, 256)
        c2b = take(256)
        oh = take(128, 16)
        sv, sif = take(16, 16), take(16, 16)
        siu = take(16, 16).bitcast(U32)
        cvv = take(8, 16)
        ciu, rcu = take(8, 16).bitcast(U32), take(8, 16).bitcast(U32)
        rcf = take(8, 16)
        gsum = take(8)
        assert left[0] <= g_end
        tkI1, tkI2, tkG = (view(off, 128) for off in (left[0], left[0] + 128, left[0] + 256))
        left[0] += 384
        assert left[0] <= g_end
        qT = acc

        block = ctx.enter_context(nc.Block())

        ssd_p = o["ssd_state_p"].rearrange("(t q) d n -> (q d) t n", q=2)
        ssd_s_in = a["state_ssd"].rearrange("b (t q) d n -> (q d) b t n", q=2)
        ssd_s_out = o["ssd_state_s"].rearrange("b (t q) d n -> (q d) b t n", q=2)
        gdn_s_in = a["state_gdn"].rearrange("b h k v -> k h b v")
        gdn_s_out = o["gdn_state_s"].rearrange("b h k v -> k h b v")
        gdn_p = o["gdn_state_p"].rearrange("h k v -> k h v")

        @block.sync
        def _(sp):
            landed = [sem(f"w_landed{s}") for s in range(SLOTS)]
            gemm_done = sem("gemm_done")

            sp.dma_start(cT, a["condT"]).then_inc(sem("ld_cond"), 16)

            def tiles(src, n0, count, t0=0, first=0):
                with sp.Fori(first, count // SLOTS) as i:
                    for s in range(SLOTS):
                        sp.wait_ge(gemm_done, i * SLOTS + (n0 + s - SLOTS + 1))
                        sp.dma_start(wring[:, s, :, :], src[i * SLOTS + (t0 + s)]).then_inc(landed[s], 16)

            for s in range(SLOTS):
                sp.dma_start(wring[:, s, :, :], a["w_ada"][s]).then_inc(landed[s], 16)
                if s == 0:
                    sp.dma_start(cst, a["consts"]).then_inc(sem("ld_const"), 16)
                    sp.dma_start(par, a["params"]).then_inc(sem("ld_par"), 16)
                if s == 1:
                    sp.dma_start(xT, a["xT"]).then_inc(sem("ld_x"), 16)
                if s == 2:
                    sp.dma_start(wsm, a["w_small"]).then_inc(sem("ld_wsm"), 16)
                    sp.dma_start(csi, a["conv_state"]).then_inc(sem("ld_csi"), 16)
            tiles(a["w_ada"], 0, N_ADA1, first=1)
            tiles(a["w_in"], T_CONV, N_CONV + N_GATE)
            tiles(a["w_ada"], T_ADA2, N_ADA2, t0=N_ADA1)
            tiles(a["w_out"], T_OUT, N_OUT)
            tiles(a["w_q"], T_Q, N_Q)

            lo_ready = sem("lo_ready")
            for s in range(SLOTS):
                sp.wait_ge(gemm_done, T_U + s - SLOTS + 1)
                sp.dma_start(wring[:, s, :, :], a["peer_u"][s]).then_inc(landed[s], 16)
            for s in range(SLOTS):
                sp.wait_ge(lo_ready, s + 1)
                sp.dma_start(wring[:, s, :, :], a["peer_v"][s]).then_inc(landed[s], 16)
            with sp.Fori(1, N_U // SLOTS) as i:
                for half, src in enumerate((a["peer_u"], a["peer_v"])):
                    for s in range(SLOTS):
                        sp.wait_ge(lo_ready, i * (2 * SLOTS) + (SLOTS * half + s - SLOTS + 1))
                        sp.dma_start(wring[:, s, :, :], src[i * SLOTS + s]).then_inc(landed[s], 16)
            sp.wait_ge(sem("coef_ready"), N_U + 2)
            sp.wait_ge(sem("x1_stored"), 16)
            sp.dma_start(xT, a["x1_dram"]).then_inc(sem("x1_back"), 16)
            sp.wait_ge(sem("y_ready"), 1)
            sp.dma_start(o["yT"], hT).then_inc(sem("y_stored"), 16)
            sp.wait_ge(sem("y_stored"), 16)

        @block.tensor
        def _(pe):
            landed = [sem(f"w_landed{s}") for s in range(SLOTS)]
            gemm_done = sem("gemm_done")
            sq_n = [0]
            norms = [0]

            def mm(out, l, r, start=True, stop=True):
                return pe.matmul(out, l, r, start=start, stop=stop)

            def tr(out, in_):
                return pe.transpose(out, in_, ident[0:in_.shape[0], 0:in_.shape[0]])

            def tile(out, s, rhs):
                for k in range(KT):
                    last = mm(out, wring[:, s, k, :], rhs(k), k == 0, k == KT - 1)
                last.then_inc(gemm_done, 1)

            def norm(count):
                k = norms[0]
                norms[0] += 1
                if k >= 2:
                    pe.wait_ge(sem("norm_sqrt"), k - 1)
                for j in range(count):
                    n = sq_n[0]
                    sq_n[0] += 1
                    pe.wait_ge(sem("sq_ready"), n + 1)
                    mm(ps[:, 4 + k % 2, 0:T], ones, sqb[:, n % 4, :], j == 0, j == count - 1
                       ).then_inc(sem("sq_used"), 1)

            pe.sem_inc(sem("v_done"), 1)
            pe.sem_inc(sem("g_ps"), 2)
            pe.wait_ge(sem("cond_ready"), 1)
            pe.wait_ge(sem("ld_const"), 16)

            def ada_part(s):
                for j in range(4):
                    last = pe.matmul(ps[32 * j:32 * j + 32, 6, :], sT[:, 4 * s + j, :],
                                     wring[:, s, :, :].rearrange("p (k c) n -> p k (c n)", k=4)[:, j, :],
                                     start=s == 0, stop=s == SLOTS - 1, tile_position=(0, 32 * j))
                last.then_inc(gemm_done, 1)

            def ada_turn(n, col):
                pe.wait_ge(sem("ada_sb"), n)
                for j in range(4):
                    last = mm(ps[:, 7, bass.ds(col + j * NC, NC)], adasb[:, j * P:(j + 1) * P], sel)
                last.then_inc(sem("ada_ps"), 1)

            with pe.Fori(0, N_ADA1 // SLOTS) as i:
                for s in range(SLOTS):
                    pe.wait_ge(landed[s], i * 16 + 16)
                    ada_part(s)
                ada_turn(i + 1, i * (SLOTS * NC))
            norm(KT)
            pe.wait_ge(sem("h_ready"), 1)
            pe.wait_ge(sem("ld_wsm"), 16)
            for k in range(KT):
                last = mm(ps[0:32, 6, 0:T], wsm[:, k, :], hT[:, k, :], k == 0, k == KT - 1)
            last.then_inc(sem("small_done"), 1)
            with pe.Fori(0, N_CONV // SLOTS) as i:
                for s in range(SLOTS):
                    pe.wait_ge(landed[s], i * 16 + (T_CONV // SLOTS * 16 + 16))
                    pe.wait_ge(sem("raw_ready"), i * (3 * SLOTS) + 3 * (s + 1))
                    tile(ps[:, s, 0:T], s, lambda k: hT[:, k, :])
            pe.wait_ge(sem("raw_ready"), 3 * (N_CONV + SLOTS))
            with pe.Fori(0, N_GATE // SLOTS) as i:
                for s in range(SLOTS):
                    pe.wait_ge(landed[s], i * 16 + (T_GATE // SLOTS * 16 + 16))
                    pe.wait_ge(sem("zg_ready"), i * SLOTS + s + 1)
                    tile(ps[:, s, 0:T], s, lambda k: hT[:, k, :])
            pe.wait_ge(sem("small_rows"), 1)
            for j, row in enumerate((dAr, spr, sgr)):
                for c in range(2):
                    last = tr(ps[:, 6, (2 * j + c) * 32:(2 * j + c + 1) * 32], row[:, c * CH:(c + 1) * CH])
            last.then_inc(sem("tok_ps"), 1)
            pe.wait_ge(sem("tok_ready"), 1)
            for c in range(2):
                mm(ps[0:32, 7, c * CH:(c + 1) * CH], tok[:, c, :], tri)
                last = mm(ps[:, 7, 256 + 32 * c:288 + 32 * c], tri, tok[:, c, :])
            last.then_inc(sem("cs_ps"), 1)
            for h in range(16):
                norm(1)

            pe.wait_ge(sem("zg_ready"), N_GATE + SLOTS)
            pe.wait_ge(sem("cv_ready"), 2 * CT + 8)
            for c in range(2):
                for j in range(8):
                    tr(ps[:, 2 * c + j // 4, (j % 4) * 128:(j % 4 + 1) * 128], cv[:, TX + j, c * CH:(c + 1) * CH]
                       ).then_inc(sem("xt_ps"), 1)
            pe.wait_ge(sem("cs_ready"), 1)
            for c in range(2):
                for g in range(2):
                    last = tr(ps[:, 7, (2 * c + g) * 128:(2 * c + g + 1) * 128], cv[:, TB + g, c * CH:(c + 1) * CH])
            last.then_inc(sem("bt_ps"), 1)
            for c in range(2):
                for g in range(2):
                    s = slice(c * CH, (c + 1) * CH)
                    last = mm(ps[:, 6, (2 * c + g) * 128:(2 * c + g + 1) * 128], cv[:, TB + g, s], cv[:, TC + g, s])
            last.then_inc(sem("cb_ps"), 1)
            pe.wait_ge(sem("bt_ready"), 1)
            pe.wait_ge(sem("xw_ready"), 1)
            for g in range(2):
                last = mm(ps[:, g, :], Bt[:, 0, g * 128:(g + 1) * 128],
                          xw0[:, g * 8:(g + 1) * 8, :])
            last.then_inc(sem("h1_ps"), 1)
            pe.wait_ge(sem("xw_ready"), 3)
            for hp in range(8):
                for c in range(2):
                    last = mm(ps[:, 2 + hp // 4, (hp % 4) * 128:(hp % 4 + 1) * 128],
                              xwf[:, c, hp * 128:(hp + 1) * 128], Bt[:, c, (hp // 4) * 128:(hp // 4 + 1) * 128],
                              c == 0, c == 1)
            last.then_inc(sem("hf_ps"), 1)
            pe.wait_ge(sem("norm_sqrt"), 17)
            pe.wait_ge(sem("h1_ready"), 1)
            for c in range(2):
                pe.wait_ge(sem("m_ready"), c + 1)
                if c == 1:
                    pe.wait_ge(sem("y_evac"), 8)
                for h in range(HS):
                    hp, q = h // 2, h % 2
                    out = ps[64 * q:64 * q + 64, 4 + hp // 4, (hp % 4) * 128:(hp % 4 + 1) * 128]
                    last = pe.matmul(out, xdt[:, c, h * 64:(h + 1) * 64], Mb[:, h, :], start=True, stop=c == 0,
                                     skip_group_check=True)
                    if c == 0:
                        if h % 2:
                            last.then_inc(sem("y_ps"), 1)
                if c == 1:
                    last.then_inc(sem("m_used"), 1)
            pe.wait_ge(sem("ce_ready"), 1)
            for h in range(HS):
                hp, q = h // 2, h % 2
                out = ps[64 * q:64 * q + 64, 6 + hp // 4, (hp % 4) * 128:(hp % 4 + 1) * 128]
                last = pe.matmul(out, h1T[:, h * 64:(h + 1) * 64], Mb[:, h, :], start=True, stop=True,
                                 skip_group_check=True)
                if h % 2:
                    last.then_inc(sem("y_ps"), 1)

            def ada(i, j):
                s, n = j % SLOTS, j // SLOTS
                pe.wait_ge(landed[s], i * 64 + (T_ADA2 // SLOTS * 16 + 16 * n + 16))
                if s == 0 and n:
                    ada_turn(i * 4 + (N_ADA1 // SLOTS + n), (n - 1) * (SLOTS * NC))
                ada_part(s)

            pe.wait_ge(sem("y_evac"), 24)
            pe.wait_ge(sem("hso_ready"), 2)
            with pe.Fori(0, 4) as i:
                pe.wait_ge(sem("kf_ready"), i * 2 + 2)
                pe.wait_ge(sem("kb_ready"), i + 1)
                pe.wait_ge(sem("gdn_free"), i + 1)
                for p in range(4):
                    h, c = p // 2, p % 2
                    mm(ps[:, 0, p * 128:(p + 1) * 128], kf[:, p, :], kb[:, p, :])
                for p in range(4):
                    last = mm(ps[:, 1, p * 128:(p + 1) * 128], kf[:, p, :], cv[:, i * 2 + (TQ + p // 2), (p % 2) * CH:(p % 2 + 1) * CH])
                last.then_inc(sem("kk_ps"), 1)
                for p in range(4):
                    last = tr(ps[:, 2, p * 128:(p + 1) * 128], vf[:, p, :])
                last.then_inc(sem("vt_ps"), 1)
                for p in range(4):
                    last = tr(ps[:, 3, p * 128:(p + 1) * 128], kf[:, p, :])
                last.then_inc(sem("kt_ps"), 1)
                ada(i, 0)
                ada(i, 1)
                pe.wait_ge(sem("lt_ready"), i + 1)
                for p in range(4):
                    last = tr(ps[:, 0, p * 128:(p + 1) * 128], Bm0[:, p, :])
                last.then_inc(sem("x_ps"), 1)
                ada(i, 2)
                for l in range(1, LV):
                    Bm = (Bm0, Bm1)[l % 2]
                    pe.wait_ge(sem("b_ready"), i * (LV - 1) + l)
                    pe.wait_ge(sem("t_ready"), i * (2 * LV) + 2 * l)
                    for p in range(4):
                        last = mm(ps[:, 0, p * 128:(p + 1) * 128], Bm[:, p, :], Tm[:, p, :])
                    last.then_inc(sem("x_ps"), 1)
                    ada(i, 2 * l + 1)
                    pe.wait_ge(sem("x_ready"), i * (LV - 1) + l)
                    if l < LV - 1:
                        for p in range(4):
                            mm(ps[:, 4, p * 128:(p + 1) * 128], Tt[:, p, :], Xb[:, p, :])
                    for p in range(4):
                        last = mm(ps[:, 1, p * 128:(p + 1) * 128], Xb[:, p, :], Tt[:, p, :])
                    last.then_inc(sem("tt_ps"), 1)
                    ada(i, 2 * l + 2)
                pe.wait_ge(sem("t_ready"), i * (2 * LV) + 2 * LV)
                pe.wait_ge(sem("rv_ready"), i * 2 + 1)
                for h in range(2):
                    last = mm(ps[:, 0, h * 128:(h + 1) * 128], Tt[:, 2 * h, :], Rv[:, 2 * h, :])
                last.then_inc(sem("vn_ps"), 1)
                ada(i, 15)
                ada_turn(i * 4 + (N_ADA1 // SLOTS + 4), 3 * SLOTS * NC)
                pe.wait_ge(sem("vn_ready"), i * 2 + 1)
                for h in range(2):
                    last = mm(ps[:, 1, h * 128:(h + 1) * 128], kd[:, 2 * h, :], VN[:, 2 * h, :])
                last.then_inc(sem("s_ps"), 1)
                for h in range(2):
                    mm(ps[:, 5, (2 * h) * 128:(2 * h + 1) * 128], VN[:, 2 * h, :], QK[:, 2 * h, :])
                pe.wait_ge(sem("s_ready"), i + 1)
                for h in range(2):
                    last = mm(ps[:, 0, 256 + h * 128:256 + (h + 1) * 128], kf[:, 2 * h + 1, :], S1[:, h, :])
                last.then_inc(sem("ks_ps"), 1)
                pe.wait_ge(sem("rv_ready"), i * 2 + 2)
                for h in range(2):
                    last = mm(ps[:, 0, h * 128:(h + 1) * 128], Tt[:, 2 * h + 1, :], Rv[:, 2 * h + 1, :])
                last.then_inc(sem("vn_ps"), 1)
                pe.wait_ge(sem("vn_ready"), i * 2 + 2)
                for h in range(2):
                    out = ps[:, 5, (2 * h + 1) * 128:(2 * h + 2) * 128]
                    mm(out, S1[:, h, :], qg[:, h, :], True, False)
                    last = mm(out, VN[:, 2 * h + 1, :], QK[:, 2 * h + 1, :], False, True)
                last.then_inc(sem("o_ps"), 1)
                for h in range(2):
                    last = mm(ps[:, 1, h * 128:(h + 1) * 128], kd[:, 2 * h + 1, :], VN[:, 2 * h + 1, :])
                last.then_inc(sem("s_ps"), 1)

            pe.wait_ge(sem("gdn_free"), 5)
            for j in range(4):
                tr(ps[0:8, 0, j * 128:(j + 1) * 128], cv[:, TB + j, TP:T]).then_inc(sem("bc_ps"), 1)
            pe.wait_ge(sem("qkp_ready"), 1)
            mm(ps[:, 1, 0:64], ones, qkp).then_inc(sem("qk_ps"), 1)
            pe.wait_ge(sem("kq_ready"), 1)
            pe.wait_ge(sem("ld_gst"), 128)
            for j in range(64):
                last = mm(ps[:, 2, 2 * j:2 * j + 2], gst[:, j, :], kq[:, j, :])
            last.then_inc(sem("skq_ps"), 1)
            pe.wait_ge(sem("vns_ready"), 1)
            tr(ps[0:64, 3, 0:128], vn).then_inc(sem("vrow_ps"), 1)

            norm(4)
            norm(4)
            for h in range(HG):
                norm(1)

            pe.wait_ge(sem("mix_ready"), 1)
            with pe.Fori(0, N_OUT // SLOTS) as i:
                for s in range(SLOTS):
                    pe.wait_ge(landed[s], i * 16 + (T_OUT // SLOTS * 16 + 16))
                    pe.wait_ge(sem("x1_done"), i * SLOTS + s + 1)
                    tile(ps[:, s, 0:T], s, lambda k: cv[:, TX + k, :] if k < 8 else cv[:, TQ + k - 8, :])
            norm(KT)
            pe.wait_ge(sem("h_ready"), 2)
            with pe.Fori(0, N_Q // SLOTS) as i:
                for s in range(SLOTS):
                    pe.wait_ge(landed[s], i * 16 + (T_Q // SLOTS * 16 + 16))
                    pe.wait_ge(sem("q_ready"), i * SLOTS + s + 1)
                    tile(ps[:, s, 0:T], s, lambda k: hT[:, k, :])
            pe.wait_ge(sem("q_ready"), N_Q + SLOTS)
            pe.wait_ge(sem("ld_sk"), 16)
            pe.wait_ge(sem("norm_sqrt"), norms[0])
            def scores(t):
                t0, n = TILES[t]
                for j in range(16):
                    last = mm(ps[0:n, 4 * (t % 2) + j // 4, (j % 4) * 128:(j % 4 + 1) * 128],
                              qT[:, j, t0:t0 + n], sk[:, j, :])
                last.then_inc(sem("score_ps"), 1)

            scores(0)
            scores(1)
            for t in range(3):
                n = TILES[t][1]
                pe.wait_ge(sem("top_done"), t + 1)
                for j, v in enumerate((tkI1, tkI2, tkG)):
                    last = tr(ps[:, TKB[t], j * 128:j * 128 + n], v[0:n, :])
                last.then_inc(sem("tk_ps"), 1)
                if t == 0:
                    pe.wait_ge(sem("tk_ready"), 3)
                    scores(2)

            def gate_group(n):
                b = n["b"]
                pe.wait_ge(sem("oh_ready"), n["n"] + 2)
                pe.wait_ge(sem("g_copied"), n["n"] + 1)
                for j in range(GT):
                    for part in range(3):
                        last = mm(ps[:, 6 + b, j * QE:(j + 1) * QE], Aoh[:, b, j, :], Boh[:, b, j, part, :],
                                  part == 0, part == 2)
                last.then_inc(sem("g_ps"), 1)

            with pe.Fori(0, NG // 2) as i:
                for b in range(2):
                    gate_group({"b": b, "n": i * 2 + b})

            def expert_step(i, gates, g0):
                for s in range(SLOTS):
                    b, m = s % 2, i * (2 * SLOTS) + s
                    out = ps[:, b, 0:T]
                    pe.wait_ge(sem("hi_ready"), m + 1)
                    pe.wait_ge(sem("gelu_done"), i * SLOTS + s + 1)
                    for k in range(KT):
                        mm(out, whi[:, b, k, :], hTh[:, k, :], k == 0, False)
                        mm(out, whi[:, b, k, :], hTl[:, k, :], False, False)
                    pe.wait_ge(sem("lo_ready"), m + 1)
                    for k in range(KT):
                        last = mm(out, wlo[:, b, k, :], hTh[:, k, :], False, k == KT - 1)
                    last.then_inc(gemm_done, 1)
                    if gates and s:
                        gate_group({"b": (gates[s - 1]) % 2, "n": g0 + gates[s - 1]})
                for q in range(4):
                    b, m = q % 2, i * (2 * SLOTS) + (SLOTS + q)
                    pe.wait_ge(sem("hi_ready"), m + 1)
                    for e in range(SLOTS):
                        if q == 0:
                            pe.wait_ge(sem("coef_ready"), i * SLOTS + (e + 3))
                        for d in range(4):
                            if e == 0:
                                pe.wait_ge(sem("v_added"), i * KT + (4 * q + d + 1))
                            mm(ps[:, 2 + d, 0:T], whi[:, b, 4 * e + d, :], chi[:, e, :], e == 0, False)
                            mm(ps[:, 2 + d, 0:T], whi[:, b, 4 * e + d, :], clo[:, e, :], False, False)
                    pe.wait_ge(sem("lo_ready"), m + 1)
                    for d in range(4):
                        for e in range(SLOTS):
                            last = mm(ps[:, 2 + d, 0:T], wlo[:, b, 4 * e + d, :], chi[:, e, :], False, e == SLOTS - 1)
                        last.then_inc(sem("v_done"), 1)

            with pe.Fori(0, 12) as i2:
                expert_step(i2 * 2, (0, 1, 2), i2 * 6 + NG)
                expert_step(i2 * 2 + 1, (3, 4, 5), i2 * 6 + NG)
            with pe.Fori(24, 32) as i:
                expert_step(i, None, None)
            norm(KT)

        @block.scalar
        def _(act):
            gemm_done = sem("gemm_done")
            sq_n = [0]
            norms = [0]
            s_act = Steps(act, sem("act_steps"))

            def square(src):
                n = sq_n[0]
                sq_n[0] += 1
                if n >= 4:
                    act.wait_ge(sem("sq_used"), n - 3)
                act.activation(sqb[:, n % 4, :], src, ACT.Square).then_inc(sem("sq_ready"), 1)

            def root(scale, bias):
                k = norms[0]
                norms[0] += 1
                act.wait_ge(sem("sq_used"), root_at.pop(0))
                if k >= 2:
                    act.wait_ge(sem("norm_free"), k - 1)
                act.activation(nrm[:, k % 2, :], ps[:, 4 + k % 2, 0:T], ACT.Sqrt, scale=scale, bias=bias
                               ).then_inc(sem("norm_sqrt"), 1)

            root_at = []

            def squares(srcs):
                for x in srcs:
                    square(x)
                root_at.append(sq_n[0])

            act.sem_inc(sem("raw_ready"), 3 * SLOTS)
            act.sem_inc(sem("zg_ready"), SLOTS)
            act.sem_inc(sem("q_ready"), SLOTS)
            act.sem_inc(sem("gelu_done"), 2)
            act.sem_inc(sem("g_copied"), 2)
            act.sem_inc(sem("cv_ready"), 8)
            act.sem_inc(sem("gdn_free"), 1)
            act.wait_ge(sem("ld_cond"), 16)
            act.wait_ge(sem("s_zero"), 1)
            act.activation(sT[:, :, 0:NC], cT, ACT.Silu).then_inc(sem("cond_ready"), 1)
            with act.Fori(0, N_ADA1 // SLOTS) as i:
                act.wait_ge(gemm_done, i * SLOTS + SLOTS)
                act.copy(adasb, ps[:, 6, :]).then_inc(sem("ada_sb"), 1)
            act.wait_ge(sem("ld_const"), 16)
            act.wait_ge(sem("ld_x"), 16)
            squares([xT[:, k, :] for k in range(KT)])
            root(1.0 / D, epsc[:, 0:1])
            act.wait_ge(sem("small_done"), 1)
            act.wait_ge(sem("abs_ready"), 1)
            act.activation(sgr, ps[0:32, 6, 0:T], ACT.Sigmoid).then_inc(sem("sg_ready"), 1)
            act.wait_ge(sem("ld_par"), 16)
            act.activation(rbias2[:, 0:1], ralog, ACT.Exp).then_inc(sem("sg_ready"), 1)
            act.wait_ge(sem("abs_ready"), 1)
            act.activation(abr, abr, ACT.Exp, scale=-1.0).then_inc(sem("exp_ready"), 1)
            act.wait_ge(sem("ld_csi"), 16)
            act.wait_ge(sem("raw_zero"), 1)
            with act.Fori(0, N_CONV // SLOTS) as i:
                for s in range(SLOTS):
                    samp = raw[:, s, 3 + TP:RAW].rearrange("p (b w) -> p b w", w=4)
                    act.wait_ge(gemm_done, i * SLOTS + (T_CONV + s + 1))
                    act.copy(raw[:, s, 3:3 + TP], ps[:, s, 0:TP]).then_inc(sem("raw_ready"), 1)
                    act.copy(samp[:, :, 3], ps[:, s, TP:T]).then_inc(sem("raw_ready"), 1)
                    act.copy(samp[:, :, 0:3], csi[:, i * SLOTS + s, :, :]).then_inc(sem("raw_ready"), 1)
                    act.wait_ge(sem("raw_ready"), i * (3 * SLOTS) + 3 * (SLOTS + s + 1))
                    act.copy(cso[:, i * SLOTS + s, 0, :], raw[:, s, TP:TP + 3]).then_inc(sem("cso_ready"), 1)
                    act.copy(cso[:, i * SLOTS + s, 1:9, :], samp[:, :, 1:4]).then_inc(sem("cso_ready"), 1)
                    act.wait_ge(sem("conv_done"), i * SLOTS + s + 1)
                    act.activation(cv[:, i * SLOTS + s, 0:TP], cac[:, s, 0:TP], ACT.Silu,
                                   bias=convb[:, bass.ds(i * SLOTS + s, 1)]).then_inc(sem("cv_ready"), 1)
                    act.activation(cv[:, i * SLOTS + s, TP:T],
                                   cac[:, s, 3 + TP:3 + TP + 29:4],
                                   ACT.Silu, bias=convb[:, bass.ds(i * SLOTS + s, 1)]).then_inc(sem("cv_ready"), 1)
            with act.Fori(0, N_GATE // SLOTS) as i:
                for s in range(SLOTS):
                    act.wait_ge(gemm_done, i * SLOTS + (T_GATE + s + 1))
                    act.activation(zg[:, i * SLOTS + s, :], ps[:, s, 0:T], ACT.Silu).then_inc(sem("zg_ready"), 1)
            act.wait_ge(sem("dA_ready"), 1)
            act.activation(smp[:, 0:8], dAr[:, TP:T], ACT.Exp).then_inc(sem("smp_exp"), 1)
            act.wait_ge(sem("cv_ready"), 2 * CT + 8)
            for h in range(16):
                squares([cv[:, h, :]])
                if h:
                    root(float(P) if h - 1 < 8 else 1.0, epsc[:, 1:2] if h - 1 < 8 else epsc[:, 0:1])
            root(1.0, epsc[:, 0:1])

            act.wait_ge(sem("w_sub"), 1)
            act.wait_ge(sem("cso_stored"), 16)
            act.activation(Wt, Wt, ACT.Exp).then_inc(sem("w_exp"), 1)
            act.activation(LE1, BR[:, 0:24, TP - 1], ACT.Exp).then_inc(sem("w_exp"), 1)
            act.activation(nbe, cst2[:, 1, 16:24], ACT.Exp).then_inc(sem("w_exp"), 1)
            act.wait_ge(sem("bt_ps"), 1)
            act.copy(Bt.rearrange("p c n -> p (c n)"), ps[:, 7, :]).then_inc(sem("bt_ready"), 1)
            act.wait_ge(sem("m_sub"), 1)
            act.activation(Mb, Mb, ACT.Exp).then_inc(sem("m_exp"), 1)
            act.wait_ge(sem("h1_ps"), 1)
            act.copy(h1T.rearrange("p (g n) -> p g n", g=2), ps[:, 0:2, :]).then_inc(sem("h1_ready"), 1)
            act.wait_ge(sem("hf_ps"), 1)
            for j in range(2):
                act.copy(hso[:, 4 * j:4 * j + 4, :], ps[:, 2 + j, :].rearrange("p (a n) -> p a n", a=4)
                         ).then_inc(sem("hso_ready"), 1)
            act.wait_ge(sem("m_sub"), 2)
            act.activation(Mb, Mb, ACT.Exp).then_inc(sem("m_exp"), 1)
            act.wait_ge(sem("m_used"), 1)
            act.activation(Mb, BR[:, 0:HS, CH:TP], ACT.Exp).then_inc(sem("m_exp"), 1)

            act.wait_ge(sem("y_ps"), 16)
            act.wait_ge(sem("hf_ps"), 1)
            act.wait_ge(sem("norm_free"), 17)
            with act.Fori(0, 4) as i:
                act.wait_ge(sem("gdn_free"), i + 1)
                kt = cv[:, bass.ds(i * 2 + TK, 2), 0:TP]
                vt = cv[:, bass.ds(i * 2 + TV, 2), 0:TP]
                act.copy(kf.rearrange("p (h c) t -> p h (c t)", h=2), kt).then_inc(sem("kf_ready"), 1)
                act.copy(vf.rearrange("p (h c) t -> p h (c t)", h=2), vt).then_inc(sem("kf_ready"), 1)
                act.wait_ge(sem("dm_sub"), i + 1)
                act.activation(Dm, Dm, ACT.Exp).then_inc(sem("dm_exp"), 1)
                act.activation(qg, BR[:, bass.ds(i * 2 + 16, 2), CH:TP], ACT.Exp).then_inc(sem("qg_exp"), 1)
                def ada_copy(n):
                    act.wait_ge(gemm_done, i * 16 + (T_ADA2 + 4 * n))
                    if n > 1:
                        act.wait_ge(sem("ada_ps"), i * 4 + (N_ADA1 // SLOTS + n - 1))
                    act.copy(adasb, ps[:, 6, :]).then_inc(sem("ada_sb"), 1)

                for l in range(1, LV):
                    act.wait_ge(sem("x_ps"), i * LV + (l + 1))
                    if l > 1:
                        act.wait_ge(sem("tt_ps"), i * (LV - 1) + (l - 1))
                    act.copy(Xb.rearrange("p a t -> p (a t)"), ps[:, 0, :]).then_inc(sem("x_ready"), 1)
                    if l in (1, 3, 5):
                        ada_copy((l + 1) // 2)
                vn4 = VN.rearrange("p (h c) t -> p h c t", h=2)
                act.wait_ge(sem("vn_ps"), i * 2 + 1)
                act.copy(vn4[:, :, 0, :], ps[:, 0, 0:256].rearrange("p (h t) -> p h t", h=2)
                         ).then_inc(sem("vn_ready"), 1)
                ada_copy(4)
                act.wait_ge(sem("s_ps"), i * 2 + 1)
                act.copy(S1.rearrange("p h t -> p (h t)"), ps[:, 1, 0:256]).then_inc(sem("s_ready"), 1)
                act.wait_ge(sem("vn_ps"), i * 2 + 2)
                act.copy(vn4[:, :, 1, :], ps[:, 0, 0:256].rearrange("p (h t) -> p h t", h=2)
                         ).then_inc(sem("vn_ready"), 1)

            act.wait_ge(sem("bc_ps"), 4)
            act.copy(bcs[0:8], ps[0:8, 0, :]).then_inc(sem("bcs_ready"), 1)
            act.wait_ge(sem("vrow_ps"), 1)
            act.copy(vrow, ps[0:64, 3, 0:128]).then_inc(sem("vrow_ready"), 1)
            act.wait_ge(sem("ygate_ready"), 1)
            for g in range(2):
                squares([cv[:, TX + 4 * g + j, :] for j in range(4)])
                root(1.0 / 512, epsc[:, 0:1])
            act.wait_ge(sem("o_ready"), 1)
            for h in range(HG):
                squares([cv[:, TQ + h, :]])
                if h:
                    root(1.0 / P, epsc[:, 0:1])
            root(1.0 / P, epsc[:, 0:1])
            act.wait_ge(sem("x1_done"), N_OUT + SLOTS)
            squares([xT[:, k, :] for k in range(KT)])
            root(1.0 / D, epsc[:, 0:1])
            act.wait_ge(sem("gst_stored"), 128)
            act.wait_ge(sem("h_ready"), 2)
            act.copy(hTh, hT).then_inc(sem("hth_ready"), 1)
            with act.Fori(0, N_Q // SLOTS) as i:
                for s in range(SLOTS):
                    act.wait_ge(gemm_done, i * SLOTS + (T_Q + s + 1))
                    act.copy(qT[:, i * SLOTS + s, :], ps[:, s, 0:T]).then_inc(sem("q_ready"), 1)
            for t, (t0, n) in enumerate(TILES):
                act.wait_ge(sem("cv_sub"), t + 1)
                act.activation(cvv[0:n], cvv[0:n], ACT.Exp).then_inc(sem("cv_exp"), 1)
                act.wait_ge(sem("tk_ps"), t + 1)
                for j, v in enumerate((i1T, i2T, gT)):
                    act.copy(v[:, t0:t0 + n], ps[:, TKB[t], j * 128:j * 128 + n]).then_inc(sem("tk_ready"), 1)

            def gate_copy(n, b, quarter, t0):
                act.wait_ge(sem("g_ps"), n + 3)
                act.copy(G[:, bass.ds(quarter, QE), bass.ds(t0, GT)].rearrange("p a t -> p t a"),
                         ps[:, 6 + b, 0:GT * QE].rearrange("p (t a) -> p t a", t=GT)).then_inc(sem("g_copied"), 1)

            def split(i, j):
                if j == 1:
                    act.wait_ge(sem("v_done"), i * KT + 1)
                elif j and j <= SLOTS + 1:
                    act.wait_ge(gemm_done, i * SLOTS + (T_U + j - 1))
                elif j:
                    act.wait_ge(sem("v_done"), i * KT + (4 * (j - SLOTS - 1) + 1))
                act.wait_ge(sem(f"w_landed{j % SLOTS}"), i * 32 + (T_U // SLOTS * 16 + 16 * (j // SLOTS) + 16))
                act.copy(whi[:, j % 2], wring[:, j % SLOTS]).then_inc(sem("hi_ready"), 1)

            split(0, 0)
            act.wait_ge(sem("tk_ready"), 9)
            act.wait_ge(sem("x1_stored"), 16)
            with act.Fori(0, NG // 2) as i:
                for b in range(2):
                    gate_copy(i * 2 + b, b, 0, i * (2 * GT) + b * GT)

            def expert_step(i, groups, g0, quarter, t0, end=False):
                for s in range(SLOTS):
                    split(i, s + 1)
                    act.wait_ge(gemm_done, i * SLOTS + (T_U + s + 1))
                    act.wait_ge(sem("coef_ready"), i * SLOTS + (s + 1))
                    act.activation(craw[:, s % 2, :], ps[:, s % 2, 0:T], ACT.Gelu).then_inc(sem("gelu_done"), 1)
                    if groups and s:
                        g = groups[s - 1]
                        gate_copy(g0 + g, g % 2, quarter, t0 + g * GT)
                for q in range(3 if end else 4):
                    split(i, SLOTS + q + 1)

            for q in range(3):
                if q:
                    act.wait_ge(sem("coef_ready"), q * QE + 2)
                with act.Fori(0, 4) as i2:
                    at = (i2 * 6 + (NG * (q + 1)), (1 - q % 2) * QE, i2 * (6 * GT))
                    expert_step(i2 * 2 + 8 * q, (0, 1, 2), *at)
                    expert_step(i2 * 2 + (8 * q + 1), (3, 4, 5), *at)
            with act.Fori(24, 31) as i:
                expert_step(i, None, None, None, None)
            expert_step(31, None, None, None, None, end=True)
            act.wait_ge(sem("x2_ready"), 1)
            squares([xT[:, k, :] for k in range(KT)])
            root(1.0 / D, epsc[:, 0:1])

        @block.vector
        def _(dve):
            gemm_done = sem("gemm_done")
            st = Steps(dve, sem("dve_steps"))
            norms = [0]
            link = st.link

            def tt(out, x, y, op):
                return dve.tensor_tensor(out, x, y, op)

            def ts(out, x, s1, s2, op0, op1=ALU.bypass):
                return dve.tensor_scalar(out, x, s1, s2, op0, op1)

            def stt(out, x, s, y, op0, op1):
                return dve.scalar_tensor_tensor(out=out, in0=x, scalar=s, in1=y, op0=op0, op1=op1)

            def inv_root():
                k = norms[0]
                norms[0] += 1
                dve.wait_ge(sem("norm_sqrt"), k + 1)
                link(dve.reciprocal(nrm[:, k % 2, :], nrm[:, k % 2, :]))
                return nrm[:, k % 2, :]

            def over(v, n, at=1):
                return v.unsqueeze(at).broadcast_to(list(v.shape[:at]) + [n] + list(v.shape[at:]))

            dve.memset(sT[:, :, NC:32], 0.0).then_inc(sem("s_zero"), 1)
            dve.sem_inc(sem("x1_done"), SLOTS)
            dve.sem_inc(sem("v_added"), 4)
            dve.memset(raw[:, :, 0:3], 0.0).then_inc(sem("raw_zero"), 1)
            dve.wait_ge(sem("ld_par"), 16)
            dve.wait_ge(sem("ld_const"), 16)

            def modulated(w, sh, sc, k):
                link(stt(mod[:, sc:sc + KT, :], mod[:, sc:sc + KT, :], 1.0, over(w, NC, 2), ALU.add, ALU.mult))
                r = inv_root()
                link(tt(hT, xT, over(r, KT), ALU.mult))
                for j in range(KT):
                    st.mark(ts(hT[:, j, 0:TP], hT[:, j, 0:TP], mod[:, sc + j, 0:1], mod[:, sh + j, 0:1],
                               ALU.mult, ALU.add))
                link(tt(hT[:, :, TP:T], hT[:, :, TP:T], mod[:, sc:sc + KT, 1:NC], ALU.mult))
                tt(hT[:, :, TP:T], hT[:, :, TP:T], mod[:, sh:sh + KT, 1:NC], ALU.add).then_inc(sem("h_ready"), 1)
                dve.wait_ge(sem("h_ready"), k)
                dve.engine_nop().then_inc(sem("norm_free"), 1)

            dve.wait_ge(sem("ada_ps"), N_ADA1 // SLOTS)
            link(tt(mod[:, 0:32, :], ps[:, 7, 0:32 * NC].rearrange("p (n c) -> p n c", c=NC),
                    over(bada[:, 0:32], NC, 2), ALU.add))
            modulated(n1w, 0, 16, 1)

            dve.wait_ge(sem("small_done"), 1)
            link(ts(xbr, ps[0:32, 6, 0:T], rbias, None, ALU.add))
            stt(abr, xbr, -1.0, xbr, ALU.mult, ALU.max).then_inc(sem("abs_ready"), 1)
            dve.wait_ge(sem("exp_ready"), 1)
            link(ts(z1r, abr, 2.0, None, ALU.add))
            link(dve.reciprocal(z1r, z1r))
            link(tt(z1r, z1r, abr, ALU.mult))
            link(tt(z2r, z1r, z1r, ALU.mult))
            link(ts(polyr, z2r, 1.0 / 17, None, ALU.mult))
            for c in (15, 13, 11, 9, 7, 5, 3):
                link(stt(polyr, polyr, 1.0 / c, z2r, ALU.add, ALU.mult))
            link(stt(polyr, polyr, 1.0, z1r, ALU.add, ALU.mult))
            link(ts(polyr, polyr, 2.0, None, ALU.mult))
            link(stt(spr, xbr, 0.0, polyr, ALU.max, ALU.add))
            dve.wait_ge(sem("sg_ready"), 2)
            link(ts(dAr, spr, rbias2[:, 0:1], -1.0, ALU.mult, ALU.mult))
            link(dve.tensor_copy(smp[:, 8:16], spr[:, TP:T]))
            dve.tensor_copy(smp[:, 16:24], sgr[:, TP:T]).then_inc(sem("small_rows"), 1)
            dve.wait_ge(sem("small_rows"), 1)
            dve.sem_inc(sem("dA_ready"), 1)

            with dve.Fori(0, N_CONV // SLOTS) as i:
                st.enter(i, 3 * SLOTS)
                for s in range(SLOTS):
                    w = lambda j: convw[:, bass.ds(i * (4 * SLOTS) + (4 * s + j), 1)]
                    dve.wait_ge(sem("raw_ready"), i * (3 * SLOTS) + 3 * (SLOTS + s + 1))
                    dve.wait_ge(sem("cv_ready"), i * (2 * SLOTS) + 2 * (s + 1))
                    link(ts(cac[:, s, :], raw[:, s, 0:CV], w(0), None, ALU.mult))
                    for j in (1, 2):
                        link(stt(cac[:, s, :], raw[:, s, j:j + CV], w(j), cac[:, s, :], ALU.mult, ALU.add))
                    stt(cac[:, s, :], raw[:, s, 3:3 + CV], w(3), cac[:, s, :], ALU.mult, ALU.add
                        ).then_inc(sem("conv_done"), 1)
            st.leave(N_CONV // SLOTS)

            dve.wait_ge(sem("tok_ps"), 1)
            dve.tensor_copy(tok.rearrange("p a b -> p (a b)"), ps[:, 6, 0:192]).then_inc(sem("tok_ready"), 1)
            dve.wait_ge(sem("cs_ps"), 1)
            link(dve.tensor_copy(cst2.rearrange("p a b -> p (a b)"), ps[:, 7, 256:320]))
            dve.tensor_copy(csr, ps[0:32, 7, 0:TP]).then_inc(sem("cs_ready"), 1)
            dve.wait_ge(sem("cs_ready"), 1)
            for h in range(16):
                r = inv_root()
                tt(cv[:, h, :], cv[:, h, :], r, ALU.mult).then_inc(sem("norm_free"), 1)

            dve.wait_ge(sem("cso_stored"), 16)
            for c in range(2):
                for j in range(2):
                    dve.wait_ge(sem("xt_ps"), 8 * c + 4 * j + 4)
                    st.mark(tt(xdt[:, c, j * 512:(j + 1) * 512].rearrange("p (h d) -> p h d", d=64),
                               ps[:, 2 * c + j, :].rearrange("p (h d) -> p h d", d=64),
                               over(tok[:, 2 + c, 8 * j:8 * j + 8], 64, 2), ALU.mult))
            st.settle()
            dve.sem_inc(sem("xdt_ready"), 1)
            dve.wait_ge(sem("ld_br"), 16)
            for c in range(2):
                last = tt(Wt[:, c, :], BR[:, 0:24, c * CH + CH - 1], cst2[:, c, 0:24], ALU.subtract)
                if c == 0:
                    link(last)
            last.then_inc(sem("w_sub"), 1)
            dve.wait_ge(sem("w_exp"), 3)
            link(tt(wf0, Wt[:, 0, :], LE1, ALU.mult))
            stt(nbe, nbe, -1.0, tok[:, 5, 24:32], ALU.mult, ALU.mult).then_inc(sem("wf_ready"), 1)

            def decay(c):
                link(tt(Mb, BR[:, 0:HS, c * CH:(c + 1) * CH], over(cst2[:, c, 0:HS], CH, 2), ALU.subtract))
                ts(Mb, Mb, 0.0, None, ALU.min).then_inc(sem("m_sub"), 1)

            decay(0)
            dve.wait_ge(sem("cb_ps"), 1)
            link(tt(cbm, ps[:, 6, :].rearrange("p (a t) -> p a t", a=4), over(tri, 4), ALU.mult))
            for c in range(2):
                dve.wait_ge(sem("m_exp"), c + 1)
                link(tt(Mb[:, 0:8, :], Mb[:, 0:8, :], over(cbm[:, 2 * c, :], 8), ALU.mult))
                tt(Mb[:, 8:16, :], Mb[:, 8:16, :], over(cbm[:, 2 * c + 1, :], 8), ALU.mult
                   ).then_inc(sem("m_ready"), 1)
                if c == 0:
                    for hp in range(8):
                        dve.wait_ge(sem("y_ps"), hp // 4 * 4 + 4)
                        yt = cv[:, TX + hp, 0:CH]
                        stt(yt, yt, dcol[:, hp:hp + 1], ps[:, 4 + hp // 4, (hp % 4) * 128:(hp % 4 + 1) * 128],
                            ALU.mult, ALU.add).then_inc(sem("y_evac"), 1)
                    decay(1)
            dve.wait_ge(sem("m_used"), 1)
            for hp in range(8):
                yt = cv[:, TX + hp, CH:TP]
                stt(yt, yt, dcol[:, hp:hp + 1], ps[:, 4 + hp // 4, (hp % 4) * 128:(hp % 4 + 1) * 128],
                    ALU.mult, ALU.add).then_inc(sem("y_evac"), 1)
            dve.wait_ge(sem("m_exp"), 3)
            for g in range(2):
                m = Mb[:, 8 * g:8 * g + 8, :]
                last = tt(m, m, over(cv[:, TC + g, CH:TP], 8), ALU.mult)
                if g == 0:
                    link(last)
            last.then_inc(sem("ce_ready"), 1)
            dve.wait_ge(sem("y_evac"), 16)
            for hp in range(8):
                dve.wait_ge(sem("y_ps"), hp // 4 * 4 + 12)
                yt = cv[:, TX + hp, CH:TP]
                tt(yt, yt, ps[:, 6 + hp // 4, (hp % 4) * 128:(hp % 4 + 1) * 128], ALU.add
                   ).then_inc(sem("y_evac"), 1)

            dve.wait_ge(sem("norm_free"), 17)
            with dve.Fori(0, 4) as i:
                st.enter(i, GDN_STEPS)
                dve.wait_ge(sem("gdn_free"), i + 1)
                d4 = Dm.rearrange("p (h c) t -> p h c t", h=2)
                for h in range(2):
                    st.mark(tt(Dm[:, 2 * h:2 * h + 2, :],
                               BR[:, i * 2 + (16 + h), :].rearrange("p (c t) -> p c t", c=2),
                               over(cst2[:, :, bass.ds(i * 2 + (16 + h), 1)].rearrange("p c o -> p (c o)"), CH, 2),
                               ALU.subtract))
                tt(kb.rearrange("p (h c) t -> p h (c t)", h=2), cv[:, bass.ds(i * 2 + TK, 2), 0:TP],
                   BR[:, bass.ds(i * 2 + 24, 2), :], ALU.mult).then_inc(sem("kb_ready"), 1)
                st.settle()
                ts(Dm, Dm, 0.0, None, ALU.min).then_inc(sem("dm_sub"), 1)
                dve.wait_ge(sem("dm_exp"), i + 1)
                link(tt(Dm, Dm, over(tri, 4), ALU.mult))
                dve.wait_ge(sem("kk_ps"), i + 1)
                link(tt(LT, Dm, ps[:, 0, :].rearrange("p (a t) -> p a t", a=4), ALU.mult))
                link(tt(Bm0, LT, over(lvl[:, 0, :], 4), ALU.mult))
                dve.sem_inc(sem("lt_ready"), 1)
                tt(Tt, over(ident, 4), Bm0, ALU.subtract).then_inc(sem("t_ready"), 1)
                tt(QK, Dm, ps[:, 1, :].rearrange("p (a t) -> p a t", a=4), ALU.mult).then_inc(sem("qk_ready"), 1)
                dve.wait_ge(sem("x_ps"), i * LV + 1)
                tt(Tm, over(ident, 4), ps[:, 0, :].rearrange("p (a t) -> p a t", a=4), ALU.subtract
                   ).then_inc(sem("t_ready"), 1)
                dve.wait_ge(sem("qg_exp"), i + 1)
                st.mark(tt(qg, qg, cv[:, bass.ds(i * 2 + TQ, 2), CH:TP], ALU.mult))
                dve.wait_ge(sem("vt_ps"), i + 1)
                r4 = Rv.rearrange("p (h c) t -> p h c t", h=2)
                k4 = kd.rearrange("p (h c) t -> p h c t", h=2)
                v4 = ps[:, 2, :].rearrange("p (h c t) -> p h c t", h=2, c=2)
                kt4 = ps[:, 3, :].rearrange("p (h c t) -> p h c t", h=2, c=2)
                dve.wait_ge(sem("kt_ps"), i + 1)
                for c in range(2):
                    last = tt(k4[:, :, c, :], kt4[:, :, c, :], over(Wt[:, c, bass.ds(i * 2 + 16, 2)], P, 2), ALU.mult)
                    st.mark(last)
                    last = tt(r4[:, :, c, :], v4[:, :, c, :], over(tok[:, 4 + c, bass.ds(i * 2 + 24, 2)], P, 2),
                              ALU.mult)
                    if c == 0:
                        last.then_inc(sem("rv0_ready"), 1)
                    else:
                        last.then_inc(sem("rv_ready"), 1)
                for l in range(1, LV):
                    dve.wait_ge(sem("tt_ps"), i * (LV - 1) + l)
                    tt(Tt, Tt, ps[:, 1, :].rearrange("p (a t) -> p a t", a=4), ALU.subtract
                       ).then_inc(sem("t_ready"), 1)
                    if l < LV - 1:
                        tt(Tm, Tm, ps[:, 4, :].rearrange("p (a t) -> p a t", a=4), ALU.subtract
                           ).then_inc(sem("t_ready"), 1)
                    else:
                        dve.engine_nop().then_inc(sem("t_ready"), 1)
                dve.wait_ge(sem("ks_ps"), i + 1)
                for h in range(2):
                    last = stt(Rv[:, 2 * h + 1, :], ps[:, 0, 256 + h * 128:256 + (h + 1) * 128],
                               nbe[:, bass.ds(i * 2 + h, 1)], Rv[:, 2 * h + 1, :], ALU.mult, ALU.add)
                    if h == 0:
                        st.mark(last)
                last.then_inc(sem("rv_ready"), 1)
                dve.wait_ge(sem("o_ps"), i + 1)
                link(dve.tensor_copy(cv[:, bass.ds(i * 2 + TQ, 2), 0:TP],
                                     ps[:, 5, :].rearrange("p (h t) -> p h t", h=2)))
                dve.wait_ge(sem("ada_ps"), i * 4 + (N_ADA1 // SLOTS + 4))
                st.mark(tt(mod[:, bass.ds(i * 16 + 32, 16), :],
                           ps[:, 7, 0:16 * NC].rearrange("p (n c) -> p n c", c=NC),
                           over(bada[:, bass.ds(i * 16 + 32, 16)], NC, 2), ALU.add))
                dve.wait_ge(sem("s_ps"), i * 2 + 2)
                dve.wait_ge(sem("s2_free"), i + 1)
                for h in range(2):
                    last = stt(S2[:, h, :], S1[:, h, :], LE1[:, bass.ds(i * 2 + (16 + h), 1)],
                               ps[:, 1, h * 128:(h + 1) * 128], ALU.mult, ALU.add)
                    if h == 0:
                        st.mark(last)
                last.then_inc(sem("gdn_free"), 1)
            st.leave(4)

            dve.wait_ge(sem("ld_sr"), 16)
            for q in range(2):
                rows = slice(64 * q, 64 * q + 64)
                for dst, src in ((Esel, SR[:, 0:HS, 0]), (dtsel, SR[:, 0:HS, 1])):
                    link(dve.tensor_copy(dst[rows], src[rows, q:HS:2, :]))
            link(tt(XD, cv[:, TX:TX + 8, TP:T], dtsel, ALU.mult))
            dve.wait_ge(sem("ld_bc"), 16)
            for j in range(4):
                b = j % 2
                dve.wait_ge(sem(f"ld_sst{b}"), 16 * (j // 2 + 1))
                s4 = sst[:, b].rearrange("p (b t) n -> p b t n", b=2)
                t4 = stm.rearrange("p (b t) n -> p b t n", b=2)
                link(tt(s4, s4, over(Esel[:, :, 2 * j:2 * j + 2].rearrange("p t b -> p b t"), 128, 3), ALU.mult))
                for bb in range(2):
                    link(tt(t4[:, bb].rearrange("p (g t) n -> p g t n", g=2),
                            over(BC[:, 0:2, 2 * j + bb, :], 4, 2),
                            over(XD[:, :, 2 * j + bb].rearrange("p (g t) -> p g t", g=2), 128, 3), ALU.mult))
                link(tt(sst[:, b], sst[:, b], stm, ALU.add))
                dve.sem_inc(sem("sst_ready"), 1)
                for bb in range(2):
                    link(tt(t4[:, bb].rearrange("p (g t) n -> p g t n", g=2),
                            s4[:, bb].rearrange("p (g t) n -> p g t n", g=2),
                            over(BC[:, 2:4, 2 * j + bb, :], 4, 2), ALU.mult))
                dve.sem_inc(sem("sst_used"), 1)
                link(dve.tensor_reduce(ysm[:, 2 * j:2 * j + 2, :].rearrange("p b t -> p (b t)"), stm, AX, ALU.add))
            dve.sem_inc(sem("sst_done"), 1)
            xs = cv[:, TX:TX + 8, TP:T]
            link(tt(xs, xs, over(dcol, TS, 2), ALU.mult))
            link(tt(xs, xs, ysm.rearrange("p b t -> p t b"), ALU.add))
            link(tt(cv[:, TX:TX + 8, :], cv[:, TX:TX + 8, :], zg[:, 0:8, :], ALU.mult))
            dve.sem_inc(sem("ygate_ready"), 1)

            qs, ks, vs = (cv[:, t:t + 8, TP:T] for t in (TQ, TK, TV))
            eight = lambda v: v.rearrange("p (h b) -> p h b", b=TS)
            link(tt(eight(qkp), qs, ks, ALU.mult))
            dve.sem_inc(sem("qkp_ready"), 1)
            kq4 = kq.rearrange("p (h b) w -> p h b w", b=TS)
            link(dve.tensor_copy(kq4[:, :, :, 0], ks))
            link(dve.tensor_copy(kq4[:, :, :, 1], qs))
            dve.sem_inc(sem("kq_ready"), 1)
            dve.wait_ge(sem("skq_ps"), 1)
            dve.wait_ge(sem("qk_ps"), 1)
            skq = ps[:, 2, 0:128].rearrange("p (h b w) -> p h b w", b=TS, w=2)
            eg = SR[:, 16:24, 0, :]
            be = SR[:, 24:32, 2, :]
            link(tt(eight(vn), skq[:, :, :, 0], eg, ALU.mult))
            link(tt(eight(vn), vs, eight(vn), ALU.subtract))
            link(tt(eight(vn), eight(vn), be, ALU.mult))
            dve.sem_inc(sem("vns_ready"), 1)
            link(tt(eight(ksm), skq[:, :, :, 1], eg, ALU.mult))
            link(tt(vsm, vn, ps[:, 1, 0:64], ALU.mult))
            link(tt(qs, eight(ksm), eight(vsm), ALU.add))
            dve.sem_inc(sem("o_ready"), 1)
            for j in range(2):
                s3 = gst[:, 32 * j:32 * j + 32, :]
                s4 = s3.rearrange("p (h b) v -> p h b v", b=TS)
                link(tt(s4, s4, over(SR[:, 16 + 4 * j:20 + 4 * j, 0, :], 128, 3), ALU.mult))
                dve.wait_ge(sem("ld_gvb"), 16 * (j + 1))
                g4 = gvb.rearrange("p (h b) v -> p h b v", b=TS)
                link(tt(g4, g4, over(cv[:, TK + 4 * j:TK + 4 * j + 4, TP:T], 128, 3), ALU.mult))
                link(tt(s3, s3, gvb, ALU.add))
                dve.sem_inc(sem("gst_ready"), 1)
            for g in range(2):
                r = inv_root()
                for j in range(4):
                    t = 4 * g + j
                    v = cv[:, TX + t, :]
                    last = stt(v, v, ynw[:, t:t + 1], r, ALU.mult, ALU.mult)
                    if j < 3:
                        st.mark(last)
                last.then_inc(sem("norm_free"), 1)
            for h in range(HG):
                r = inv_root()
                v = cv[:, TQ + h, :]
                stt(v, v, onw[:, 0:1], r, ALU.mult, ALU.mult).then_inc(sem("norm_free"), 1)
            dve.wait_ge(sem("norm_free"), norms[0])
            tt(cv[:, TQ:TQ + 8, :], cv[:, TQ:TQ + 8, :], zg[:, 8:16, :], ALU.mult).then_inc(sem("mix_ready"), 1)

            G1 = 32
            with dve.Fori(0, N_OUT // SLOTS) as i:
                st.enter(i, 2 * SLOTS)
                for s in range(SLOTS):
                    n = i * SLOTS + s
                    dve.wait_ge(gemm_done, i * SLOTS + (T_OUT + s + 1))
                    st.mark(stt(xT[:, n, 0:TP], ps[:, s, 0:TP], mod[:, n + G1, 0:1], xT[:, n, 0:TP],
                                ALU.mult, ALU.add))
                    link(tt(gtmp[:, s, :], ps[:, s, TP:T], mod[:, n + G1, 1:NC], ALU.mult))
                    tt(xT[:, n, TP:T], xT[:, n, TP:T], gtmp[:, s, :], ALU.add).then_inc(sem("x1_done"), 1)
            st.leave(N_OUT // SLOTS)
            dve.wait_ge(sem("x1_done"), N_OUT + SLOTS)
            modulated(n2w, 48, 64, 2)

            for t, (t0, n) in enumerate(TILES):
                dve.wait_ge(sem("score_ps"), t + 1)
                if t:
                    dve.wait_ge(sem("tk_ps"), t)
                for j in range(16):
                    sc = ps[0:n, 4 * (t % 2) + j // 4, (j % 4) * 128:(j % 4 + 1) * 128]
                    link(dve.max(sv[0:n, j, 0:8], sc))
                    link(dve.max_index(siu[0:n, j, 0:8], sv[0:n, j, 0:8], sc))
                    link(dve.match_replace(s2b[0:n], sv[0:n, j, 0:8], sc, -3.0e38))
                    link(dve.max(sv[0:n, j, 8:16], s2b[0:n]))
                    link(dve.max_index(siu[0:n, j, 8:16], sv[0:n, j, 8:16], s2b[0:n]))
                link(dve.tensor_copy(sif[0:n], siu[0:n]))
                sv4 = sv[0:n].rearrange("p (h s) k -> p h s k", s=2)
                si4 = sif[0:n].rearrange("p (h s) k -> p h s k", s=2)
                link(tt(cand[0:n].rearrange("p h (a b) -> p h a b", b=16), over(sv4[:, :, 0, :], 16, 3),
                        over(sv4[:, :, 1, :], 16, 2), ALU.add))
                for h in range(8):
                    link(dve.max(cvv[0:n, h, 0:8], cand[0:n, h, :]))
                    link(dve.max_index(ciu[0:n, h, 0:8], cvv[0:n, h, 0:8], cand[0:n, h, :]))
                    link(dve.match_replace(c2b[0:n], cvv[0:n, h, 0:8], cand[0:n, h, :], -3.0e38))
                    link(dve.max(cvv[0:n, h, 8:16], c2b[0:n]))
                    link(dve.max_index(ciu[0:n, h, 8:16], cvv[0:n, h, 8:16], c2b[0:n]))
                link(dve.tensor_copy(gsum[0:n], cvv[0:n, :, 0]))
                link(tt(cvv[0:n], cvv[0:n], over(gsum[0:n], 16, 2), ALU.subtract))
                dve.sem_inc(sem("cv_sub"), 1)
                for side, (op, by), dst in ((0, (ALU.logical_shift_right, 4), tkI1),
                                            (1, (ALU.bitwise_and, 15), tkI2)):
                    link(ts(rcu[0:n], ciu[0:n], by, None, op))
                    link(dve.tensor_copy(rcf[0:n], rcu[0:n]))
                    rflat = rcf[0:n].rearrange("p h k -> p (h k)")
                    link(tt(oh[0:n], over(rflat, 16, 2), over(iota[0:n, 0:16], 128), ALU.is_equal))
                    o4 = oh[0:n].rearrange("p (h k) r -> p h k r", k=16)
                    link(tt(o4, o4, over(si4[:, :, side, :], 16, 2), ALU.mult))
                    link(dve.tensor_reduce(dst[0:n], oh[0:n], AX, ALU.add))
                dve.wait_ge(sem("cv_exp"), t + 1)
                link(dve.tensor_reduce(gsum[0:n], cvv[0:n], AX, ALU.add))
                link(dve.reciprocal(gsum[0:n], gsum[0:n]))
                link(tt(tkG[0:n].rearrange("p (h k) -> p h k", k=16), cvv[0:n], over(gsum[0:n], 16, 2), ALU.mult))
                dve.sem_inc(sem("top_done"), 1)

            dve.memset(acc, 0.0).then_inc(sem("acc_zero"), 1)
            dve.wait_ge(sem("acc_zero"), 1)
            dve.wait_ge(sem("tk_ready"), 9)
            dve.sem_inc(sem("coef_ready"), 2)
            dve.sem_inc(sem("oh_ready"), 1)
            dve.wait_ge(gemm_done, T_U)
            dve.wait_ge(sem("hth_ready"), 1)
            link(tt(hTl, hT, hTh_f, ALU.subtract))
            for part in range(3):
                link(dve.tensor_copy(gp[:, :, part], gT))
                if part < 2:
                    link(tt(gT, gT, gp[:, :, part], ALU.subtract))

            def split(i, j):
                dve.wait_ge(sem("hi_ready"), i * (2 * SLOTS) + (j + 1))
                tt(wlo[:, j % 2], wring[:, j % SLOTS], whi_f[:, j % 2], ALU.subtract).then_inc(sem("lo_ready"), 1)

            split(0, 0)

            def one_hots(n, b, quarter, t0):
                toks = bass.ds(t0, GT)
                dve.wait_ge(sem("g_ps"), n + 1)
                st.mark(tt(Aoh[:, b], over(iota, GT), over(i1T[:, toks], P, 2), ALU.is_equal))
                dve.wait_ge(sem("oh_ready"), n + 1)
                link(tt(Soh, over(iota[:, quarter * QE:(quarter + 1) * QE], GT), over(i2T[:, toks], QE, 2),
                        ALU.is_equal))
                tt(Boh[:, b], over(Soh, 3, 2), over(gp[:, toks, :], QE, 3), ALU.mult).then_inc(sem("oh_ready"), 1)

            with dve.Fori(0, NG // 2) as i:
                st.enter(i, 4)
                for b in range(2):
                    one_hots(i * 2 + b, b, 0, i * (2 * GT) + b * GT)
            st.leave(NG // 2)

            def expert_step(i, groups, g0, quarter, t0, col, end=False):
                def oh(j):
                    if groups:
                        g = groups[j]
                        one_hots(g0 + g, g % 2, quarter + 1, t0 + g * GT)

                for s in range(SLOTS):
                    split(i, s + 1)
                    if s < 3:
                        oh(s)
                    c, g = craw[:, s % 2, :], G[:, col + s, :]
                    dve.wait_ge(sem("gelu_done"), i * SLOTS + (s + 3))
                    st.mark(tt(chi[:, s, :], c, g, ALU.mult))
                    link(tt(c, c, g, ALU.mult))
                    tt(clo[:, s, :], c, chi_f[:, s, :], ALU.subtract).then_inc(sem("coef_ready"), 1)
                for q in range(4):
                    if not (end and q == 3):
                        split(i, SLOTS + q + 1)
                    dve.wait_ge(sem("v_added"), i * KT + (4 * q + 4))
                    for d in range(4):
                        dve.wait_ge(sem("v_done"), i * KT + (4 * q + d + 2))
                        tt(acc[:, 4 * q + d, :], acc[:, 4 * q + d, :], ps[:, 2 + d, 0:T], ALU.add
                           ).then_inc(sem("v_added"), 1)

            for q in range(4):
                dve.wait_ge(sem("g_copied"), NG * (q + 1) + 2)
                half = (q % 2) * QE
                if q < 3:
                    with dve.Fori(0, 4) as i2:
                        st.enter(i2, 28)
                        g0 = i2 * 6 + NG * (q + 1)
                        expert_step(i2 * 2 + 8 * q, (0, 1, 2), g0, q, i2 * (6 * GT), i2 * 8 + half)
                        expert_step(i2 * 2 + (8 * q + 1), (3, 4, 5), g0, q, i2 * (6 * GT), i2 * 8 + (half + 4))
                    st.leave(4)
                else:
                    with dve.Fori(0, 7) as i:
                        st.enter(i, 8)
                        expert_step(i + 24, None, None, None, None, i * 4 + half)
                    st.leave(7)
                    expert_step(31, None, None, None, None, 28 + half, end=True)

            dve.wait_ge(sem("x1_back"), 16)
            dve.wait_ge(sem("v_added"), N_U // SLOTS * KT + 4)
            G2 = 80
            for j in range(KT):
                st.mark(stt(xT[:, j, 0:TP], acc[:, j, 0:TP], mod[:, G2 + j, 0:1], xT[:, j, 0:TP], ALU.mult, ALU.add))
            link(tt(acc[:, :, TP:T], acc[:, :, TP:T], mod[:, G2:G2 + KT, 1:NC], ALU.mult))
            link(tt(xT[:, :, TP:T], xT[:, :, TP:T], acc[:, :, TP:T], ALU.add))
            dve.sem_inc(sem("x2_ready"), 1)
            r = inv_root()
            for j in range(KT):
                st.mark(stt(hT[:, j, :], xT[:, j, :], fnw[:, j:j + 1], r, ALU.mult, ALU.mult))
            st.settle()
            dve.sem_inc(sem("y_ready"), 1)

        @block.gpsimd
        def _(pool):
            def tt(out, x, y, op):
                return pool.tensor_tensor(out, x, y, op)

            def over(v, n, at=1):
                return v.unsqueeze(at).broadcast_to(list(v.shape[:at]) + [n] + list(v.shape[at:]))

            pool.sem_inc(sem("s2_free"), 1)
            pool.wait_ge(sem("smp_exp"), 1)
            pool.wait_ge(sem("cs_ready"), 1)
            pool.dma_start(a["rows_dram"][0:24, :], csr[0:24, :]).then_inc(sem("rows_out"), 16)
            pool.dma_start(a["rows_dram"][24:32, :], sgr[24:32, 0:TP]).then_inc(sem("rows_out"), 16)
            pool.dma_start(a["smp_dram"], smp[0:32]).then_inc(sem("rows_out"), 16)
            pool.wait_ge(sem("cso_ready"), 2 * CT)
            pool.dma_start(o["conv_out"], cso).then_inc(sem("cso_stored"), 16)
            pool.wait_ge(sem("rows_out"), 48)
            pool.wait_ge(sem("cv_ready"), 2 * CT + 8)
            pool.dma_start(BR, a["rows_dram"].partition_broadcast(P)).then_inc(sem("ld_br"), 16)
            pool.dma_start(SR.rearrange("p r k b -> p r (k b)"), a["smp_dram"].partition_broadcast(P)
                           ).then_inc(sem("ld_sr"), 16)
            pool.wait_ge(sem("xdt_ready"), 1)
            pool.wait_ge(sem("w_exp"), 3)
            pool.wait_ge(sem("cso_stored"), 16)
            x0, x1 = (xdt[:, c, :].rearrange("p (h d) -> p h d", d=64) for c in range(2))
            f0, f1 = (xwf[:, c, :].rearrange("p (h d) -> p h d", d=64) for c in range(2))
            tt(xw0, x0, over(Wt[:, 0, 0:HS], 64, 2), ALU.mult).then_inc(sem("xw_ready"), 1)
            tt(f1, x1, over(Wt[:, 1, 0:HS], 64, 2), ALU.mult).then_inc(sem("xw_ready"), 1)
            pool.wait_ge(sem("wf_ready"), 1)
            tt(f0, x0, over(wf0[:, 0:HS], 64, 2), ALU.mult).then_inc(sem("xw_ready"), 1)
            pool.wait_ge(sem("hso_ready"), 2)
            pool.dma_start(ssd_p, hso).then_inc(sem("hso_stored"), 16)
            with pool.Fori(0, 4) as i:
                pool.wait_ge(sem("lt_ready"), i + 1)
                for l in range(1, LV):
                    if l >= 2:
                        pool.wait_ge(sem("x_ps"), i * LV + (l - 1))
                        pool.wait_ge(sem("t_ready"), i * (2 * LV) + 1)
                    tt((Bm0, Bm1)[l % 2], LT, over(lvl[:, l, :], 4), ALU.mult).then_inc(sem("b_ready"), 1)
                pool.wait_ge(sem("gdn_free"), i + 2)
                pool.dma_start(gdn_p[:, bass.ds(i * 2, 2), :], S2).then_inc(sem("s2_stored"), 16)
                pool.wait_ge(sem("s2_stored"), i * 16 + 16)
                pool.sem_inc(sem("s2_free"), 1)
            def load_sst(j):
                pool.dma_start(sst[:, j % 2].rearrange("p (b t) n -> p b t n", b=2),
                               ssd_s_in[:, 2 * j:2 * j + 2]).then_inc(sem(f"ld_sst{j % 2}"), 16)

            load_sst(0)
            load_sst(1)
            pool.wait_ge(sem("bcs_ready"), 1)
            pool.dma_start(a["bc_dram"].rearrange("j b n -> b j n"),
                           bcs[0:8].rearrange("p (j n) -> p j n", j=4)).then_inc(sem("bc_out"), 16)
            pool.wait_ge(sem("bc_out"), 16)
            pool.dma_start(BC.rearrange("p j b n -> p (j b) n"),
                           a["bc_dram"].rearrange("j b n -> (j b) n").partition_broadcast(P)
                           ).then_inc(sem("ld_bc"), 16)
            for j in range(4):
                pool.wait_ge(sem("sst_ready"), j + 1)
                pool.dma_start(ssd_s_out[:, 2 * j:2 * j + 2], sst[:, j % 2].rearrange("p (b t) n -> p b t n", b=2)
                               ).then_inc(sem(f"sst_stored{j % 2}"), 16)
                if j < 2:
                    pool.wait_ge(sem(f"sst_stored{j}"), 16)
                    pool.wait_ge(sem("sst_used"), j + 1)
                    load_sst(j + 2)
            for j in range(2):
                pool.wait_ge(sem(f"sst_stored{j}"), 32)
            pool.wait_ge(sem("sst_done"), 1)
            for h in range(8):
                pool.dma_start(gst[:, 8 * h:8 * h + 8, :], gdn_s_in[:, h]).then_inc(sem("ld_gst"), 16)
            pool.wait_ge(sem("vrow_ready"), 1)
            pool.dma_start(a["v_dram"], vrow[0:64]).then_inc(sem("v_out"), 16)
            pool.wait_ge(sem("v_out"), 16)
            for j in range(2):
                if j:
                    pool.wait_ge(sem("gst_ready"), 1)
                pool.dma_start(gvb, a["v_dram"][32 * j:32 * j + 32, :].partition_broadcast(P)
                               ).then_inc(sem("ld_gvb"), 16)
            pool.wait_ge(sem("gst_ready"), 2)
            for h in range(8):
                pool.dma_start(gdn_s_out[:, h], gst[:, 8 * h:8 * h + 8, :]).then_inc(sem("gst_stored"), 16)
            pool.wait_ge(sem("x1_done"), N_OUT + SLOTS)
            pool.dma_start(a["x1_dram"], xT).then_inc(sem("x1_stored"), 16)
            pool.wait_ge(sem("gst_stored"), 128)
            pool.dma_start(sk, a["sub_keys"]).then_inc(sem("ld_sk"), 16)
            pool.wait_ge(sem("hso_stored"), 16)
            pool.wait_ge(sem("x1_stored"), 16)


def kernel(**inputs):
    import numpy as np
    import concourse.bacc as bacc
    from concourse.bass_utils import run_bass_kernel_spmd

    x = {k: np.asarray(v) for k, v in inputs.items()}
    f32 = np.float32

    def feat(v):
        return np.ascontiguousarray(v.reshape(v.shape[0], -1, P).transpose(2, 1, 0))

    def wtiles(w):
        return np.ascontiguousarray(w.reshape(KT, P, -1, P).transpose(2, 1, 0, 3))

    w_in = x["w_in"][0]
    z, xbc, dt, qkv, ar, br, gate = np.split(w_in, [1024, 2560, 2576, 5648, 5656, 5664], axis=1)
    conv_w = np.concatenate([x["gdn_conv_w"][0], x["ssd_conv_w"][0]], axis=1)
    cols = np.zeros((P, 2), f32)
    cols[0:24, 0] = np.concatenate([x["ssd_dt_bias"][0], x["gdn_dt_bias"][0]])
    cols[0:24, 1] = np.concatenate([x["ssd_A_log"][0], x["gdn_A_log"][0]])
    col = lambda v: v.reshape(-1, P).T
    params = np.concatenate([
        col(x["norm1_w"][0]), col(x["norm2_w"][0]), col(x["final_norm_w"]), col(x["b_ada"][0]),
        conv_w.reshape(4, CT, P).transpose(2, 1, 0).reshape(P, CT * 4),
        np.concatenate([np.zeros((P, 24), f32), col(x["ssd_conv_b"][0])], axis=1),
        col(np.repeat(x["ssd_D"][0], 64)), col(x["ssd_norm_w"][0]), col(x["gdn_norm_w"][0]), cols], axis=1)
    j, i = np.meshgrid(np.arange(P), np.arange(P), indexing="ij")
    levels = [((i // (2 * m) == j // (2 * m)) & (i // m % 2 == 1) & (j // m % 2 == 0)) for m in (1, 2, 4, 8, 16, 32, 64)]
    eps = np.zeros((P, 2), f32)
    eps[:, 0], eps[:, 1] = EPS, P * EPS
    consts = np.concatenate([np.eye(P), np.ones((P, P)), i >= j, i + 0.0] + levels + [eps, np.arange(P)[:, None] % 32 == np.arange(NC)], axis=1).astype(f32)
    state = np.concatenate([x["state_gdn_conv"][0], x["state_ssd_conv"][0]], axis=2)
    u = x["peer_u"][0].reshape(P, P, KT, P)
    arrays = {
        "condT": feat(np.concatenate([x["c_prompt"], x["c_sample"]])),
        "xT": feat(np.concatenate([x["x_prompt"][0], x["x_sample"][:, 0]])),
        "consts": consts, "params": params,
        "w_ada": x["w_ada"][0].reshape(4, 4, P, 24, 512).transpose(3, 0, 2, 1, 4).reshape(96, P, KT, P),
        "w_small": np.concatenate([dt, ar, br], axis=1).reshape(KT, P, 32).transpose(1, 0, 2),
        "w_in": wtiles(np.concatenate([qkv, xbc, z, gate], axis=1)),
        "w_out": wtiles(x["w_out"][0]), "w_q": wtiles(x["peer_w_q"][0]),
        "conv_state": state.reshape(8, 3, CT, P).transpose(3, 2, 0, 1),
        "sub_keys": x["peer_sub_keys"][0].reshape(16, P, P).transpose(2, 0, 1),
        "peer_u": u.transpose(1, 3, 2, 0),
        "peer_v": x["peer_v"][0].reshape(P, 32, 4, 4, 512).transpose(1, 3, 0, 2, 4).reshape(P, P, KT, P),
        "state_ssd": x["state_ssd"][0], "state_gdn": x["state_gdn"][0],
    }
    outs = {"yT": (P, KT, T), "conv_out": (P, CT, 9, 3), "ssd_state_p": (HS, 64, 128), "gdn_state_p": (HG, P, P),
            "ssd_state_s": (TS, HS, 64, 128), "gdn_state_s": (TS, HG, P, P)}
    scratch = {"rows_dram": (32, TP), "smp_dram": (32, 24), "bc_dram": (4, TS, 128), "v_dram": (64, 128),
               "x1_dram": (P, KT, T)}
    nc = bacc.Bacc("TRN2", target_bir_lowering=False, num_devices=1, dynamic_dma_scratch_size=4096)
    arrays = {f"in_{k}": np.ascontiguousarray(v) for k, v in arrays.items()}
    a = {k[3:]: nc.dram_tensor(k, v.shape, F32, kind="ExternalInput").ap() for k, v in arrays.items()}
    for k, shape in scratch.items():
        a[k] = nc.dram_tensor(k, shape, F32, kind="Internal").ap()
    o = {k: nc.dram_tensor(f"out_{k}", shape, F32, kind="ExternalOutput").ap() for k, shape in outs.items()}
    build(nc, a, o)
    r = run_bass_kernel_spmd(nc, [arrays], core_ids=[0]).results[0]
    y = r["out_yT"].transpose(2, 1, 0).reshape(T, D)
    conv = r["out_conv_out"].transpose(2, 3, 1, 0).reshape(9, 3, CT * P)
    gdn_c, ssd_c = conv[:, :, 0:3072], conv[:, :, 3072:]
    c = np.ascontiguousarray
    return (c(y[None, 0:TP]), c(y[TP:, None]), r["out_ssd_state_p"][None, None], c(ssd_c[None, 0:1]),
            r["out_gdn_state_p"][None, None], c(gdn_c[None, 0:1]), r["out_ssd_state_s"][None], c(ssd_c[None, 1:]),
            r["out_gdn_state_s"][None], c(gdn_c[None, 1:]))
```

```python
from contextlib import ExitStack

import concourse.bass as bass
from concourse import mybir

ALU = mybir.AluOpType
ACT = mybir.ActivationFunctionType
F32 = mybir.dt.float32
F32R = mybir.dt.float32r
BF16 = mybir.dt.bfloat16
U32 = mybir.dt.uint32
SB = 56280
AX = mybir.AxisListType.X

P = 128
D = 2048
KT = D // P
TP, TS = 256, 8
T = TP + TS
NC = 9
CH = 128
HS, HG = 16, 8
CT = 36
TQ, TK, TV, TX, TB, TC = 0, 8, 16, 24, 32, 34
RAW = 3 + TP + 4 * TS
CV = RAW - 3
EPS = 1e-6
LV = 7
TOPK = 16
TILES = ((TP, TS), (0, P), (P, P))
GT = 11
NG = T // GT
EARLY = 10
QE = 32
GDN_STEPS = 12
SLOTS = 4
N_ADA1, N_CONV, N_GATE, N_ADA2, N_OUT, N_Q, N_U = 32, CT, 16, 64, 16, 16, 128
T_CONV = N_ADA1
T_GATE = T_CONV + N_CONV
T_ADA2 = T_GATE + N_GATE
T_OUT = T_ADA2 + N_ADA2
T_Q = T_OUT + N_OUT
T_U = T_Q + N_Q
L_OUT = N_CONV + N_GATE
L_Q = L_OUT + N_OUT
L_E = L_Q + N_Q


class Steps:

    def __init__(self, eng, sem):
        self.eng, self.sem, self.base, self.k = eng, sem, 0, 0

    def mark(self, ins):
        ins.then_inc(self.sem, 1)
        self.k += 1

    def settle(self):
        self.eng.wait_ge(self.sem, self.base + self.k)

    def link(self, ins):
        self.mark(ins)
        self.settle()

    def enter(self, i, per):
        self.out, self.per, self.k = self.base + self.k, per, 0
        self.base = i * per + self.out

    def leave(self, count):
        assert self.k == self.per, (self.k, self.per)
        self.base, self.k = self.out + count * self.per, 0


def build(nc, a, o):
    with ExitStack() as ctx:
        sem_of = {}

        def sem(name):
            if name not in sem_of:
                sem_of[name] = ctx.enter_context(nc.semaphore(name))
            return sem_of[name]

        ps = ctx.enter_context(nc.psum_tensor("ps", [P, 8, 512], F32))
        left = [0]
        at = (nc.sbuf_base + 31) // 32 * 32
        placed = [0]

        def view(off, *dims, parts=P, of=F32):
            n = 1
            for d in dims:
                n *= d
            assert off + (n if of is not BF16 else n // 2) <= SB, (off, n)
            placed[0] += 1
            v = nc.alloc_sbuf_tensor_at(f"sb{placed[0]}", [parts, n], of, offset=at + 4 * off, align_bytes=8)[:, :]
            if len(dims) == 2:
                v = v.rearrange("p (a b) -> p a b", b=dims[1])
            elif len(dims) == 3:
                v = v.rearrange("p (a b c) -> p a b c", b=dims[1], c=dims[2])
            elif len(dims) == 4:
                v = v.rearrange("p (a b c d) -> p a b c d", b=dims[1], c=dims[2], d=dims[3])
            return v

        def take(*dims, parts=P):
            n = 1
            for d in dims:
                n *= d
            off = left[0]
            left[0] += n + (n % 2)
            return view(off, *dims, parts=parts)

        def take_r(*dims):
            off = left[0]
            n = 1
            for d in dims:
                n *= d
            left[0] += n
            v = view(off, *dims, of=F32R)
            return v, v.bitcast(F32)

        def take_b(*dims):
            n = 1
            for d in dims:
                n *= d
            off = left[0]
            left[0] += (n + 3) // 4 * 2
            return view(off, *dims, of=BF16)

        wring = take(SLOTS, KT, P)
        hT = take(KT, T)
        mod = take(96, NC)
        n_const = a["consts"].shape[1]
        cst = take(n_const)
        sel = cst[:, 512 + LV * 128 + 2:512 + LV * 128 + 2 + NC]
        ident, ones, tri = cst[:, 0:128], cst[:, 128:256], cst[:, 256:384]
        iota = cst[:, 384:512]
        lvl = cst[:, 512:512 + LV * 128].rearrange("p (l i) -> p l i", l=LV)
        epsc = cst[:, 512 + LV * 128:512 + LV * 128 + 2]
        of_head, of_token = cst[:, n_const - 16:n_const - 8], cst[:, n_const - 8:n_const]
        n_par = a["params"].shape[1]
        par = take(n_par)
        po = [0]

        def pview(n):
            v = par[:, po[0]:po[0] + n]
            po[0] += n
            return v

        n1w, n2w, fnw, bada = pview(16), pview(16), pview(16), pview(96)
        convw = pview(CT * 4)
        convb, dcol, ynw, onw = pview(CT), pview(8), pview(8), pview(1)
        rbias, ralog = pview(1)[0:32], pview(1)[0:32]
        sqb_off = left[0]
        sqb = take(4, T)
        nrm = take(2, T)
        xT_off = left[0]
        xT = take(KT, T)
        base = left[0]
        TKB = (6, 0, 4)

        cv = take(CT, T)
        zg_off = left[0]
        zg = take(16, T)
        br_off = left[0]
        BR = take(32, TP)
        tmp_off = left[0]
        hT_off = SLOTS * KT * P
        assert tmp_off + 8300 <= SB, tmp_off
        left[0] = tmp_off
        raw, cac = take(4, RAW), take(4, CV)
        cso, csi = take(CT, 9, 3), take(CT, 8, 3)
        left[0] = zg_off
        wsm = take(KT, 32)
        cT = take(KT, NC)
        xbr, abr, polyr, z1r, z2r = (take(T, parts=32) for _ in range(5))
        rbias2 = take(2, parts=32)
        left[0] = br_off
        whi, whi_f = take_r(2, KT, P)
        wlo, _ = take_r(2, KT, P)
        left[0] = tmp_off + 6700
        sgr = take(T, parts=32)
        smp = take(24, parts=32)
        tok = take(6, 32)
        cst2 = take(2, 32)
        Wt = take(2, 24)
        LE1 = take(24)
        wf0 = take(24)
        nbe = take(8)
        sT = take(KT, 32)
        gtmp = take(SLOTS, TS)
        spr, dAr = take(T, parts=32), take(T, parts=32)
        csr = take(TP, parts=32)
        hTl = view(hT_off, KT, T, of=F32R)
        mixl = view(left[0], KT, T, of=F32R)
        SR = view(left[0], 32, 3, TS)
        adasb = view(left[0] + 768, 512)
        h1h, h1h_f = take_r(KT, T)
        mixh = view(zg_off, KT, T, of=F32R)
        mixh_f = mixh.bitcast(F32)
        assert left[0] <= SB, left[0]

        left[0] = hT_off
        xdt, xwf = take(2, 1024), take(2, 1024)
        left[0] = tmp_off
        xw0, Bt = take(16, 64), take(2, 256)
        h1T, cbm = take(1024), take(4, 128)
        Mb = take(16, 128)
        assert left[0] <= tmp_off + 6700
        hso = take(8, 128)
        assert left[0] <= tmp_off + 6700, left[0] - tmp_off

        left[0] = hT_off
        kf, vf, kb, Dm, LT, QK, Tm, Tt = (take(4, 128) for _ in range(8))
        left[0] = tmp_off
        Xb, Bm0, Bm1, Rv, kd, VN = (take(4, 128) for _ in range(6))
        S1, S2, qg = take(2, 128), take(2, 128), take(2, 128)
        assert left[0] <= tmp_off + 6700

        left[0] = hT_off
        Esel, XD, dtsel, ysm = take(8, TS), take(8, TS), take(8, TS), take(TS, 8)
        kq, qkp = take(64, 2), take(64)
        vn, egs, bts, ksm, vsm = take(64), take(64), take(64), take(64), take(64)
        qkb = take(64)
        bcs = take(4 * 128, parts=8)
        vrow = take(128, parts=64)
        left[0] = br_off
        BC = take(4, TS, 128)
        sst = take(2, 2 * 8, 128)
        left[0] = tmp_off
        stm = take(16, 128)
        left[0] = br_off
        gst = take(64, 128)
        left[0] = tmp_off
        gvb = take(32, 128)
        assert left[0] <= tmp_off + 6700

        left[0] = xT_off
        G = take(2 * QE, T)
        g_end = left[0]
        Boh = take_b(2, GT, 3, QE)
        assert left[0] == br_off
        left[0] = br_off + 4 * KT * P
        Aoh, Soh = take_b(2, GT, 128), take_b(2, GT, QE)
        acc = take(KT, T)
        hTh, hTh_f = take_r(KT, T)
        small_off = left[0]
        chi, chi_f = take_r(SLOTS, T)
        clo, _ = take_r(SLOTS, T)
        craw = view(sqb_off, 2, T)
        i1T, i2T = take(T), take(T)
        gp = take_b(T, 3)
        assert left[0] <= SB, left[0]
        Qs = view(xT_off, 16, 128)
        left[0] = xT_off + QE * T
        sk = take(16, 128)
        work = take(2048)
        cand = take(8, 256)
        oh = take(128, 16)
        assert left[0] <= g_end
        left[0] = small_off
        sv, sif = take(16, 16), take(16, 16)
        siu = take(16, 16).bitcast(U32)
        cvv = take(8, 16)
        ciu, rcu = take(8, 16).bitcast(U32), take(8, 16).bitcast(U32)
        rcf = take(8, 16)
        gsum = take(8)
        tkI1, tkI2, tkG = take(128), take(128), take(128)
        gT = take(T)
        assert left[0] <= small_off + 2 * SLOTS * T
        qT = acc

        block = ctx.enter_context(nc.Block())

        ssd_p = o["ssd_state_p"].rearrange("(t q) d n -> (q d) t n", q=2)
        ssd_s_in = a["state_ssd"].rearrange("b (t q) d n -> (q d) b t n", q=2)
        ssd_s_out = o["ssd_state_s"].rearrange("b (t q) d n -> (q d) b t n", q=2)
        gdn_s_in = a["state_gdn"].rearrange("b h k v -> k h b v")
        gdn_s_out = o["gdn_state_s"].rearrange("b h k v -> k h b v")
        gdn_p = o["gdn_state_p"].rearrange("h k v -> k h v")

        @block.sync
        def _(sp):
            landed = [sem(f"w_landed{s}") for s in range(SLOTS)]
            gemm_done = sem("gemm_done")

            sp.dma_start(cT, a["condT"]).then_inc(sem("ld_cond"), 16)

            lo_ready = sem("lo_ready")

            def tiles(src, free, n0, count, t0=0, first=0):
                with sp.Fori(first, count // SLOTS) as i:
                    for s in range(SLOTS):
                        sp.wait_ge(free, i * SLOTS + (n0 + s - SLOTS + 1))
                        sp.dma_start(wring[:, s, :, :], src[i * SLOTS + (t0 + s)]).then_inc(landed[s], 16)

            def four(src, free, n0, t0=0):
                for s in range(SLOTS):
                    sp.wait_ge(free, n0 + s - SLOTS + 1)
                    sp.dma_start(wring[:, s, :, :], src[t0 + s]).then_inc(landed[s], 16)

            for s in range(SLOTS):
                sp.dma_start(wring[:, s, :, :], a["w_ada"][s]).then_inc(landed[s], 16)
                if s == 0:
                    sp.dma_start(cst, a["consts"]).then_inc(sem("ld_const"), 16)
                    sp.dma_start(par, a["params"]).then_inc(sem("ld_par"), 16)
                if s == 1:
                    sp.dma_start(xT, a["xT"]).then_inc(sem("ld_x"), 16)
                if s == 2:
                    sp.dma_start(wsm, a["w_small"]).then_inc(sem("ld_wsm"), 16)
                    sp.dma_start(csi, a["conv_state"]).then_inc(sem("ld_csi"), 16)
            tiles(a["w_ada"], gemm_done, 0, N_ADA1, first=1)
            four(a["w_in"], gemm_done, T_CONV)
            tiles(a["w_in"], lo_ready, 0, N_CONV + N_GATE, first=1)
            four(a["w_ada"], lo_ready, L_OUT, t0=N_ADA1)
            tiles(a["w_ada"], gemm_done, T_ADA2, N_ADA2, t0=N_ADA1, first=1)
            four(a["w_out"], gemm_done, T_OUT)
            tiles(a["w_out"], lo_ready, L_OUT, N_OUT, first=1)
            tiles(a["w_q"], lo_ready, L_Q, N_Q)

            with sp.Fori(0, N_U // SLOTS) as i:
                for half, src in enumerate((a["peer_u"], a["peer_v"])):
                    for s in range(SLOTS):
                        sp.wait_ge(lo_ready, i * (2 * SLOTS) + (L_E + SLOTS * half + s - SLOTS + 1))
                        sp.dma_start(wring[:, s, :, :], src[i * SLOTS + s]).then_inc(landed[s], 16)
            sp.wait_ge(sem("coef_ready"), N_U + 2)
            sp.wait_ge(sem("x1_stored"), 16)
            sp.dma_start(xT, a["x1_dram"]).then_inc(sem("x1_back"), 16)
            sp.wait_ge(sem("y_ready"), 1)
            sp.dma_start(o["yT"], hT).then_inc(sem("y_stored"), 16)
            sp.wait_ge(sem("y_stored"), 16)

        @block.tensor
        def _(pe):
            landed = [sem(f"w_landed{s}") for s in range(SLOTS)]
            gemm_done = sem("gemm_done")
            sq_n = [0]
            norms = [0]

            def mm(out, l, r, start=True, stop=True):
                return pe.matmul(out, l, r, start=start, stop=stop)

            def tr(out, in_):
                return pe.transpose(out, in_, ident[0:in_.shape[0], 0:in_.shape[0]])

            def tile(out, b, n, high, low):
                pe.wait_ge(sem("hi_ready"), n + 1)
                for k in range(KT):
                    mm(out, whi[:, b, k, :], high[:, k, :], k == 0, False)
                    mm(out, whi[:, b, k, :], low[:, k, :], False, False)
                pe.wait_ge(sem("lo_ready"), n + 1)
                for k in range(KT):
                    last = mm(out, wlo[:, b, k, :], high[:, k, :], False, k == KT - 1)
                last.then_inc(gemm_done, 1)

            def norm(count):
                k = norms[0]
                norms[0] += 1
                if k >= 2:
                    pe.wait_ge(sem("norm_sqrt"), k - 1)
                for j in range(count):
                    n = sq_n[0]
                    sq_n[0] += 1
                    pe.wait_ge(sem("sq_ready"), n + 1)
                    mm(ps[:, 4 + k % 2, 0:T], ones, sqb[:, n % 4, :], j == 0, j == count - 1
                       ).then_inc(sem("sq_used"), 1)

            pe.sem_inc(sem("v_done"), 1)
            pe.sem_inc(sem("g_ps"), 2)
            pe.wait_ge(sem("cond_ready"), 1)
            pe.wait_ge(sem("ld_const"), 16)

            def ada_part(s):
                for j in range(4):
                    last = pe.matmul(ps[32 * j:32 * j + 32, 6, :], sT[:, 4 * s + j, :],
                                     wring[:, s, :, :].rearrange("p (k c) n -> p k (c n)", k=4)[:, j, :],
                                     start=s == 0, stop=s == SLOTS - 1, tile_position=(0, 32 * j))
                last.then_inc(gemm_done, 1)

            def ada_turn(n, col):
                pe.wait_ge(sem("ada_sb"), n)
                for j in range(4):
                    last = mm(ps[:, 7, bass.ds(col + j * NC, NC)], adasb[:, j * P:(j + 1) * P], sel)
                last.then_inc(sem("ada_ps"), 1)

            with pe.Fori(0, N_ADA1 // SLOTS) as i:
                for s in range(SLOTS):
                    pe.wait_ge(landed[s], i * 16 + 16)
                    ada_part(s)
                ada_turn(i + 1, i * (SLOTS * NC))
            norm(KT)
            pe.wait_ge(sem("h_ready"), 1)
            pe.wait_ge(sem("ld_wsm"), 16)
            for k in range(KT):
                last = mm(ps[0:32, 6, 0:T], wsm[:, k, :], hT[:, k, :], k == 0, k == KT - 1)
            last.then_inc(sem("small_done"), 1)
            pe.wait_ge(sem("hl_ready"), 4)
            with pe.Fori(0, N_CONV // SLOTS) as i:
                for s in range(SLOTS):
                    pe.wait_ge(sem("raw_ready"), i * (3 * SLOTS) + 3 * (s + 1))
                    tile(ps[:, s, 0:T], s % 2, i * SLOTS + s, h1h, hTl)
            pe.wait_ge(sem("raw_ready"), 3 * (N_CONV + SLOTS))
            with pe.Fori(0, N_GATE // SLOTS) as i:
                for s in range(SLOTS):
                    pe.wait_ge(sem("zg_ready"), i * SLOTS + s + 1)
                    tile(ps[:, s, 0:T], s % 2, i * SLOTS + (N_CONV + s), h1h, hTl)
            pe.wait_ge(sem("small_rows"), 1)
            for j, row in enumerate((dAr, spr, sgr)):
                for c in range(2):
                    last = tr(ps[:, 6, (2 * j + c) * 32:(2 * j + c + 1) * 32], row[:, c * CH:(c + 1) * CH])
            last.then_inc(sem("tok_ps"), 1)
            pe.wait_ge(sem("tok_ready"), 1)
            for c in range(2):
                mm(ps[0:32, 7, c * CH:(c + 1) * CH], tok[:, c, :], tri)
                last = mm(ps[:, 7, 256 + 32 * c:288 + 32 * c], tri, tok[:, c, :])
            last.then_inc(sem("cs_ps"), 1)
            for h in range(16):
                norm(1)

            pe.wait_ge(sem("zg_ready"), N_GATE + SLOTS)
            pe.wait_ge(sem("cv_ready"), 2 * CT + 8)
            for c in range(2):
                for j in range(8):
                    tr(ps[:, 2 * c + j // 4, (j % 4) * 128:(j % 4 + 1) * 128], cv[:, TX + j, c * CH:(c + 1) * CH]
                       ).then_inc(sem("xt_ps"), 1)
            pe.wait_ge(sem("cs_ready"), 1)
            for c in range(2):
                for g in range(2):
                    last = tr(ps[:, 7, (2 * c + g) * 128:(2 * c + g + 1) * 128], cv[:, TB + g, c * CH:(c + 1) * CH])
            last.then_inc(sem("bt_ps"), 1)
            for c in range(2):
                for g in range(2):
                    s = slice(c * CH, (c + 1) * CH)
                    last = mm(ps[:, 6, (2 * c + g) * 128:(2 * c + g + 1) * 128], cv[:, TB + g, s], cv[:, TC + g, s])
            last.then_inc(sem("cb_ps"), 1)
            pe.wait_ge(sem("bt_ready"), 1)
            pe.wait_ge(sem("xw_ready"), 1)
            for g in range(2):
                last = mm(ps[:, g, :], Bt[:, 0, g * 128:(g + 1) * 128],
                          xw0[:, g * 8:(g + 1) * 8, :])
            last.then_inc(sem("h1_ps"), 1)
            pe.wait_ge(sem("xw_ready"), 3)
            for hp in range(8):
                for c in range(2):
                    last = mm(ps[:, 2 + hp // 4, (hp % 4) * 128:(hp % 4 + 1) * 128],
                              xwf[:, c, hp * 128:(hp + 1) * 128], Bt[:, c, (hp // 4) * 128:(hp // 4 + 1) * 128],
                              c == 0, c == 1)
            last.then_inc(sem("hf_ps"), 1)
            pe.wait_ge(sem("norm_sqrt"), 17)
            pe.wait_ge(sem("h1_ready"), 1)
            for c in range(2):
                pe.wait_ge(sem("m_ready"), c + 1)
                if c == 1:
                    pe.wait_ge(sem("y_evac"), 8)
                for h in range(HS):
                    hp, q = h // 2, h % 2
                    out = ps[64 * q:64 * q + 64, 4 + hp // 4, (hp % 4) * 128:(hp % 4 + 1) * 128]
                    last = pe.matmul(out, xdt[:, c, h * 64:(h + 1) * 64], Mb[:, h, :], start=True, stop=c == 0,
                                     skip_group_check=True)
                    if c == 0:
                        if h % 2:
                            last.then_inc(sem("y_ps"), 1)
                if c == 1:
                    last.then_inc(sem("m_used"), 1)
            pe.wait_ge(sem("ce_ready"), 1)
            for h in range(HS):
                hp, q = h // 2, h % 2
                out = ps[64 * q:64 * q + 64, 6 + hp // 4, (hp % 4) * 128:(hp % 4 + 1) * 128]
                last = pe.matmul(out, h1T[:, h * 64:(h + 1) * 64], Mb[:, h, :], start=True, stop=True,
                                 skip_group_check=True)
                if h % 2:
                    last.then_inc(sem("y_ps"), 1)

            def ada(i, j):
                s, n = j % SLOTS, j // SLOTS
                pe.wait_ge(landed[s], i * 64 + (T_ADA2 // SLOTS * 16 + 16 * n + 16))
                if s == 0 and n:
                    ada_turn(i * 4 + (N_ADA1 // SLOTS + n), (n - 1) * (SLOTS * NC))
                ada_part(s)

            pe.wait_ge(sem("y_evac"), 24)
            pe.wait_ge(sem("hso_ready"), 2)
            with pe.Fori(0, 4) as i:
                pe.wait_ge(sem("kf_ready"), i * 2 + 2)
                pe.wait_ge(sem("kb_ready"), i + 1)
                pe.wait_ge(sem("gdn_free"), i + 1)
                for p in range(4):
                    h, c = p // 2, p % 2
                    mm(ps[:, 0, p * 128:(p + 1) * 128], kf[:, p, :], kb[:, p, :])
                for p in range(4):
                    last = mm(ps[:, 1, p * 128:(p + 1) * 128], kf[:, p, :], cv[:, i * 2 + (TQ + p // 2), (p % 2) * CH:(p % 2 + 1) * CH])
                last.then_inc(sem("kk_ps"), 1)
                for p in range(4):
                    last = tr(ps[:, 2, p * 128:(p + 1) * 128], vf[:, p, :])
                last.then_inc(sem("vt_ps"), 1)
                for p in range(4):
                    last = tr(ps[:, 3, p * 128:(p + 1) * 128], kf[:, p, :])
                last.then_inc(sem("kt_ps"), 1)
                ada(i, 0)
                ada(i, 1)
                pe.wait_ge(sem("lt_ready"), i + 1)
                for p in range(4):
                    last = tr(ps[:, 0, p * 128:(p + 1) * 128], Bm0[:, p, :])
                last.then_inc(sem("x_ps"), 1)
                ada(i, 2)
                for l in range(1, LV):
                    Bm = (Bm0, Bm1)[l % 2]
                    pe.wait_ge(sem("b_ready"), i * (LV - 1) + l)
                    pe.wait_ge(sem("t_ready"), i * (2 * LV) + 2 * l)
                    for p in range(4):
                        last = mm(ps[:, 0, p * 128:(p + 1) * 128], Bm[:, p, :], Tm[:, p, :])
                    last.then_inc(sem("x_ps"), 1)
                    ada(i, 2 * l + 1)
                    pe.wait_ge(sem("x_ready"), i * (LV - 1) + l)
                    if l < LV - 1:
                        for p in range(4):
                            mm(ps[:, 4, p * 128:(p + 1) * 128], Tt[:, p, :], Xb[:, p, :])
                    for p in range(4):
                        last = mm(ps[:, 1, p * 128:(p + 1) * 128], Xb[:, p, :], Tt[:, p, :])
                    last.then_inc(sem("tt_ps"), 1)
                    ada(i, 2 * l + 2)
                pe.wait_ge(sem("t_ready"), i * (2 * LV) + 2 * LV)
                pe.wait_ge(sem("rv_ready"), i * 2 + 1)
                for h in range(2):
                    last = mm(ps[:, 0, h * 128:(h + 1) * 128], Tt[:, 2 * h, :], Rv[:, 2 * h, :])
                last.then_inc(sem("vn_ps"), 1)
                ada(i, 15)
                ada_turn(i * 4 + (N_ADA1 // SLOTS + 4), 3 * SLOTS * NC)
                pe.wait_ge(sem("vn_ready"), i * 2 + 1)
                for h in range(2):
                    last = mm(ps[:, 1, h * 128:(h + 1) * 128], kd[:, 2 * h, :], VN[:, 2 * h, :])
                last.then_inc(sem("s_ps"), 1)
                for h in range(2):
                    mm(ps[:, 5, (2 * h) * 128:(2 * h + 1) * 128], VN[:, 2 * h, :], QK[:, 2 * h, :])
                pe.wait_ge(sem("s_ready"), i + 1)
                for h in range(2):
                    last = mm(ps[:, 0, 256 + h * 128:256 + (h + 1) * 128], kf[:, 2 * h + 1, :], S1[:, h, :])
                last.then_inc(sem("ks_ps"), 1)
                pe.wait_ge(sem("rv_ready"), i * 2 + 2)
                for h in range(2):
                    last = mm(ps[:, 0, h * 128:(h + 1) * 128], Tt[:, 2 * h + 1, :], Rv[:, 2 * h + 1, :])
                last.then_inc(sem("vn_ps"), 1)
                pe.wait_ge(sem("vn_ready"), i * 2 + 2)
                for h in range(2):
                    out = ps[:, 5, (2 * h + 1) * 128:(2 * h + 2) * 128]
                    mm(out, S1[:, h, :], qg[:, h, :], True, False)
                    last = mm(out, VN[:, 2 * h + 1, :], QK[:, 2 * h + 1, :], False, True)
                last.then_inc(sem("o_ps"), 1)
                for h in range(2):
                    last = mm(ps[:, 1, h * 128:(h + 1) * 128], kd[:, 2 * h + 1, :], VN[:, 2 * h + 1, :])
                last.then_inc(sem("s_ps"), 1)

            pe.wait_ge(sem("gdn_free"), 5)
            for j in range(4):
                tr(ps[0:8, 0, j * 128:(j + 1) * 128], cv[:, TB + j, TP:T]).then_inc(sem("bc_ps"), 1)
            pe.wait_ge(sem("qkp_ready"), 1)
            mm(ps[:, 1, 0:64], ones, qkp).then_inc(sem("qk_ps"), 1)
            pe.wait_ge(sem("kq_ready"), 1)
            pe.wait_ge(sem("ld_gst"), 128)
            for j in range(64):
                last = mm(ps[:, 2, 2 * j:2 * j + 2], gst[:, j, :], kq[:, j, :])
            last.then_inc(sem("skq_ps"), 1)
            pe.wait_ge(sem("vns_ready"), 1)
            tr(ps[0:64, 3, 0:128], vn).then_inc(sem("vrow_ps"), 1)

            norm(4)
            norm(4)
            for h in range(HG):
                norm(1)

            pe.wait_ge(sem("mixl_ready"), 2)
            with pe.Fori(0, N_OUT // SLOTS) as i:
                for s in range(SLOTS):
                    pe.wait_ge(sem("x1_done"), i * SLOTS + s + 1)
                    tile(ps[:, s, 0:T], s % 2, i * SLOTS + (L_OUT + s), mixh, mixl)
            norm(KT)
            pe.wait_ge(sem("hl_ready"), 8)
            with pe.Fori(0, N_Q // SLOTS) as i:
                for s in range(SLOTS):
                    pe.wait_ge(sem("q_ready"), i * SLOTS + s + 1)
                    tile(ps[:, s, 0:T], s % 2, i * SLOTS + (L_Q + s), hTh, hTl)
            pe.wait_ge(sem("q_ready"), N_Q + SLOTS)
            pe.wait_ge(sem("ld_sk"), 16)
            pe.wait_ge(sem("norm_sqrt"), norms[0])
            pe.wait_ge(sem("qs_ready"), 1)
            for j in range(16):
                last = mm(ps[:, 4, 0:128], Qs[:, j, :], sk[:, j, :], j == 0, j == 15)
            last.then_inc(sem("score_ps"), 1)

            def scores(t):
                t0, n = TILES[t]
                for j in range(16):
                    last = mm(ps[0:n, 4 * (t - 1) + j // 4, (j % 4) * 128:(j % 4 + 1) * 128],
                              qT[:, j, t0:t0 + n], sk[:, j, :])
                last.then_inc(sem("score_ps"), 1)

            scores(1)
            pe.wait_ge(sem("pair_ready"), 1)
            for side in range(2):
                last = mm(ps[0:64, 5, side * 32:side * 32 + 32], ident[:, side * 64:side * 64 + 64],
                          sv[:, 0:2, :].rearrange("p a k -> p (a k)"))
            last.then_inc(sem("pair_ps"), 1)
            pe.wait_ge(sem("top_done"), 1)
            for j in range(3):
                last = mm(ps[:, TKB[0], j * 128:j * 128 + TS],
                          oh[0:64, 8 * j:8 * j + 8, :].rearrange("p h k -> p (h k)"), of_token[0:64])
            last.then_inc(sem("tk_ps"), 1)
            pe.wait_ge(sem("tk_ready"), 3)
            scores(2)

            def turn(t):
                n = TILES[t][1]
                pe.wait_ge(sem("top_done"), t + 1)
                for j, v in enumerate((tkI1, tkI2, tkG)):
                    last = tr(ps[:, TKB[t], j * 128:j * 128 + n], v[0:n, :])
                last.then_inc(sem("tk_ps"), 1)

            def gate_group(n, b, bank):
                pe.wait_ge(sem("aoh_ready"), n + 1)
                pe.wait_ge(sem("boh_ready"), n + 1)
                pe.wait_ge(sem("g_copied"), n + 1)
                for j in range(GT):
                    for part in range(3):
                        last = mm(ps[:, bank + b, j * QE:(j + 1) * QE], Aoh[:, b, j, :], Boh[:, b, j, part, :],
                                  part == 0, part == 2)
                last.then_inc(sem("g_ps"), 1)

            turn(1)
            with pe.Fori(0, EARLY // 2) as i:
                for b in range(2):
                    gate_group(i * 2 + b, b, 2)
            turn(2)
            with pe.Fori(EARLY // 2, NG // 2) as i:
                for b in range(2):
                    gate_group(i * 2 + b, b, 2)
            pe.wait_ge(sem("g_copied"), NG + 2)

            def expert_step(i, gates, g0):
                for s in range(SLOTS):
                    pe.wait_ge(sem("gelu_done"), i * SLOTS + s + 1)
                    tile(ps[:, s % 2, 0:T], s % 2, i * (2 * SLOTS) + (L_E + s), hTh, hTl)
                    if gates and s:
                        gate_group(g0 + gates[s - 1], gates[s - 1] % 2, 6)
                for q in range(4):
                    b, m = q % 2, i * (2 * SLOTS) + (L_E + SLOTS + q)
                    pe.wait_ge(sem("hi_ready"), m + 1)
                    for e in range(SLOTS):
                        if q == 0:
                            pe.wait_ge(sem("coef_ready"), i * SLOTS + (e + 3))
                        for d in range(4):
                            if e == 0:
                                pe.wait_ge(sem("v_added"), i * KT + (4 * q + d + 1))
                            mm(ps[:, 2 + d, 0:T], whi[:, b, 4 * e + d, :], chi[:, e, :], e == 0, False)
                            mm(ps[:, 2 + d, 0:T], whi[:, b, 4 * e + d, :], clo[:, e, :], False, False)
                    pe.wait_ge(sem("lo_ready"), m + 1)
                    for d in range(4):
                        for e in range(SLOTS):
                            last = mm(ps[:, 2 + d, 0:T], wlo[:, b, 4 * e + d, :], chi[:, e, :], False, e == SLOTS - 1)
                        last.then_inc(sem("v_done"), 1)

            with pe.Fori(0, 12) as i2:
                expert_step(i2 * 2, (0, 1, 2), i2 * 6 + NG)
                expert_step(i2 * 2 + 1, (3, 4, 5), i2 * 6 + NG)
            with pe.Fori(24, 32) as i:
                expert_step(i, None, None)
            norm(KT)

        @block.scalar
        def _(act):
            gemm_done = sem("gemm_done")
            sq_n = [0]
            norms = [0]
            s_act = Steps(act, sem("act_steps"))

            def square(src):
                n = sq_n[0]
                sq_n[0] += 1
                if n >= 4:
                    act.wait_ge(sem("sq_used"), n - 3)
                act.activation(sqb[:, n % 4, :], src, ACT.Square).then_inc(sem("sq_ready"), 1)

            def root(scale, bias):
                k = norms[0]
                norms[0] += 1
                act.wait_ge(sem("sq_used"), root_at.pop(0))
                if k >= 2:
                    act.wait_ge(sem("norm_free"), k - 1)
                act.activation(nrm[:, k % 2, :], ps[:, 4 + k % 2, 0:T], ACT.Sqrt, scale=scale, bias=bias
                               ).then_inc(sem("norm_sqrt"), 1)

            root_at = []

            def squares(srcs):
                for x in srcs:
                    square(x)
                root_at.append(sq_n[0])

            act.sem_inc(sem("raw_ready"), 3 * SLOTS)
            act.sem_inc(sem("zg_ready"), SLOTS)
            act.sem_inc(sem("q_ready"), SLOTS)
            act.sem_inc(sem("gelu_done"), 2)
            act.sem_inc(sem("g_copied"), 2)
            act.sem_inc(sem("cv_ready"), 8)
            act.sem_inc(sem("gdn_free"), 1)
            act.wait_ge(sem("ld_cond"), 16)
            act.wait_ge(sem("s_zero"), 1)
            act.activation(sT[:, :, 0:NC], cT, ACT.Silu).then_inc(sem("cond_ready"), 1)
            with act.Fori(0, N_ADA1 // SLOTS) as i:
                act.wait_ge(gemm_done, i * SLOTS + SLOTS)
                act.copy(adasb, ps[:, 6, :]).then_inc(sem("ada_sb"), 1)
            act.wait_ge(sem("ld_const"), 16)
            act.wait_ge(sem("ld_x"), 16)
            squares([xT[:, k, :] for k in range(KT)])
            root(1.0 / D, epsc[:, 0:1])
            act.wait_ge(sem("small_done"), 1)
            act.wait_ge(sem("abs_ready"), 1)
            act.activation(sgr, ps[0:32, 6, 0:T], ACT.Sigmoid).then_inc(sem("sg_ready"), 1)
            act.wait_ge(sem("ld_par"), 16)
            act.activation(rbias2[:, 0:1], ralog, ACT.Exp).then_inc(sem("sg_ready"), 1)
            act.wait_ge(sem("abs_ready"), 1)
            act.activation(abr, abr, ACT.Exp, scale=-1.0).then_inc(sem("exp_ready"), 1)
            act.wait_ge(sem("ld_csi"), 16)
            act.wait_ge(sem("raw_zero"), 1)

            def high(slot, lands, done, b=None):
                if done is not None:
                    act.wait_ge(gemm_done, done)
                act.wait_ge(sem(f"w_landed{slot}"), lands)
                act.copy(whi[:, slot % 2], wring[:, slot]).then_inc(sem("hi_ready"), 1)

            def high_h(k, dst):
                act.wait_ge(sem("h_ready"), k)
                for j in range(0, KT, 4):
                    act.copy(dst[:, j:j + 4], hT[:, j:j + 4]).then_inc(sem("hth_ready"), 1)

            def high_after(i, s, t0):
                high((s + 2) % SLOTS, i * 16 + (t0 // SLOTS * 16 + 16 + 16 * ((s + 2) // SLOTS)), None)

            high_h(1, h1h)
            for s in range(2):
                high(s, T_CONV // SLOTS * 16 + 16, None)
            with act.Fori(0, N_CONV // SLOTS) as i:
                for s in range(SLOTS):
                    samp = raw[:, s, 3 + TP:RAW].rearrange("p (b w) -> p b w", w=4)
                    act.wait_ge(gemm_done, i * SLOTS + (T_CONV + s + 1))
                    act.copy(raw[:, s, 3:3 + TP], ps[:, s, 0:TP]).then_inc(sem("raw_ready"), 1)
                    act.copy(samp[:, :, 3], ps[:, s, TP:T]).then_inc(sem("raw_ready"), 1)
                    act.copy(samp[:, :, 0:3], csi[:, i * SLOTS + s, :, :]).then_inc(sem("raw_ready"), 1)
                    act.wait_ge(sem("raw_ready"), i * (3 * SLOTS) + 3 * (SLOTS + s + 1))
                    act.copy(cso[:, i * SLOTS + s, 0, :], raw[:, s, TP:TP + 3]).then_inc(sem("cso_ready"), 1)
                    act.copy(cso[:, i * SLOTS + s, 1:9, :], samp[:, :, 1:4]).then_inc(sem("cso_ready"), 1)
                    high_after(i, s, T_CONV)
                    act.wait_ge(sem("conv_done"), i * SLOTS + s + 1)
                    act.activation(cv[:, i * SLOTS + s, 0:TP], cac[:, s, 0:TP], ACT.Silu,
                                   bias=convb[:, bass.ds(i * SLOTS + s, 1)]).then_inc(sem("cv_ready"), 1)
                    act.activation(cv[:, i * SLOTS + s, TP:T],
                                   cac[:, s, 3 + TP:3 + TP + 29:4],
                                   ACT.Silu, bias=convb[:, bass.ds(i * SLOTS + s, 1)]).then_inc(sem("cv_ready"), 1)
            def gates(i, more):
                for s in range(SLOTS):
                    act.wait_ge(gemm_done, i * SLOTS + (T_GATE + s + 1))
                    act.activation(zg[:, bass.ds(i * SLOTS + s, 1), :], ps[:, s:s + 1, 0:T], ACT.Silu
                                   ).then_inc(sem("zg_ready"), 1)
                    if s < 2 or more:
                        high_after(i, s, T_GATE)

            with act.Fori(0, N_GATE // SLOTS - 1) as i:
                gates(i, True)
            gates(N_GATE // SLOTS - 1, False)
            act.wait_ge(sem("dA_ready"), 1)
            act.activation(smp[:, 0:8], dAr[:, TP:T], ACT.Exp).then_inc(sem("smp_exp"), 1)
            act.wait_ge(sem("cv_ready"), 2 * CT + 8)
            for h in range(16):
                squares([cv[:, h, :]])
                if h:
                    root(float(P) if h - 1 < 8 else 1.0, epsc[:, 1:2] if h - 1 < 8 else epsc[:, 0:1])
            root(1.0, epsc[:, 0:1])

            act.wait_ge(sem("w_sub"), 1)
            act.wait_ge(sem("cso_stored"), 16)
            act.activation(Wt, Wt, ACT.Exp).then_inc(sem("w_exp"), 1)
            act.activation(LE1, BR[:, 0:24, TP - 1], ACT.Exp).then_inc(sem("w_exp"), 1)
            act.activation(nbe, cst2[:, 1, 16:24], ACT.Exp).then_inc(sem("w_exp"), 1)
            act.wait_ge(sem("bt_ps"), 1)
            act.copy(Bt.rearrange("p c n -> p (c n)"), ps[:, 7, :]).then_inc(sem("bt_ready"), 1)
            act.wait_ge(sem("m_sub"), 1)
            act.activation(Mb, Mb, ACT.Exp).then_inc(sem("m_exp"), 1)
            act.wait_ge(sem("h1_ps"), 1)
            act.copy(h1T.rearrange("p (g n) -> p g n", g=2), ps[:, 0:2, :]).then_inc(sem("h1_ready"), 1)
            act.wait_ge(sem("hf_ps"), 1)
            for j in range(2):
                act.copy(hso[:, 4 * j:4 * j + 4, :], ps[:, 2 + j, :].rearrange("p (a n) -> p a n", a=4)
                         ).then_inc(sem("hso_ready"), 1)
            act.wait_ge(sem("m_sub"), 2)
            act.activation(Mb, Mb, ACT.Exp).then_inc(sem("m_exp"), 1)
            act.wait_ge(sem("m_used"), 1)
            act.activation(Mb, BR[:, 0:HS, CH:TP], ACT.Exp).then_inc(sem("m_exp"), 1)

            act.wait_ge(sem("y_ps"), 16)
            act.wait_ge(sem("hf_ps"), 1)
            act.wait_ge(sem("norm_free"), 17)
            with act.Fori(0, 4) as i:
                act.wait_ge(sem("gdn_free"), i + 1)
                kt = cv[:, bass.ds(i * 2 + TK, 2), 0:TP]
                vt = cv[:, bass.ds(i * 2 + TV, 2), 0:TP]
                act.copy(kf.rearrange("p (h c) t -> p h (c t)", h=2), kt).then_inc(sem("kf_ready"), 1)
                act.copy(vf.rearrange("p (h c) t -> p h (c t)", h=2), vt).then_inc(sem("kf_ready"), 1)
                act.wait_ge(sem("dm_sub"), i + 1)
                act.activation(Dm, Dm, ACT.Exp).then_inc(sem("dm_exp"), 1)
                act.activation(qg, BR[:, bass.ds(i * 2 + 16, 2), CH:TP], ACT.Exp).then_inc(sem("qg_exp"), 1)
                def ada_copy(n):
                    act.wait_ge(gemm_done, i * 16 + (T_ADA2 + 4 * n))
                    if n > 1:
                        act.wait_ge(sem("ada_ps"), i * 4 + (N_ADA1 // SLOTS + n - 1))
                    act.copy(adasb, ps[:, 6, :]).then_inc(sem("ada_sb"), 1)

                for l in range(1, LV):
                    act.wait_ge(sem("x_ps"), i * LV + (l + 1))
                    if l > 1:
                        act.wait_ge(sem("tt_ps"), i * (LV - 1) + (l - 1))
                    act.copy(Xb.rearrange("p a t -> p (a t)"), ps[:, 0, :]).then_inc(sem("x_ready"), 1)
                    if l in (1, 3, 5):
                        ada_copy((l + 1) // 2)
                vn4 = VN.rearrange("p (h c) t -> p h c t", h=2)
                act.wait_ge(sem("vn_ps"), i * 2 + 1)
                act.copy(vn4[:, :, 0, :], ps[:, 0, 0:256].rearrange("p (h t) -> p h t", h=2)
                         ).then_inc(sem("vn_ready"), 1)
                ada_copy(4)
                act.wait_ge(sem("s_ps"), i * 2 + 1)
                act.copy(S1.rearrange("p h t -> p (h t)"), ps[:, 1, 0:256]).then_inc(sem("s_ready"), 1)
                act.wait_ge(sem("vn_ps"), i * 2 + 2)
                act.copy(vn4[:, :, 1, :], ps[:, 0, 0:256].rearrange("p (h t) -> p h t", h=2)
                         ).then_inc(sem("vn_ready"), 1)

            act.wait_ge(sem("bc_ps"), 4)
            act.copy(bcs[0:8], ps[0:8, 0, :]).then_inc(sem("bcs_ready"), 1)
            act.wait_ge(sem("vrow_ps"), 1)
            act.copy(vrow, ps[0:64, 3, 0:128]).then_inc(sem("vrow_ready"), 1)
            act.wait_ge(sem("ygate_ready"), 1)
            for g in range(2):
                squares([cv[:, TX + 4 * g + j, :] for j in range(4)])
                root(1.0 / 512, epsc[:, 0:1])
            act.wait_ge(sem("o_ready"), 1)
            for h in range(HG):
                squares([cv[:, TQ + h, :]])
                if h:
                    root(1.0 / P, epsc[:, 0:1])
            root(1.0 / P, epsc[:, 0:1])
            act.wait_ge(sem("mix_ready"), 1)
            act.copy(mixh[:, 0:8], cv[:, TX:TX + 8, :]).then_inc(sem("mixh_ready"), 1)
            act.wait_ge(sem("mix_ready"), 2)
            act.copy(mixh[:, 8:16], cv[:, TQ:TQ + 8, :]).then_inc(sem("mixh_ready"), 1)

            def high_next(i, s, t0):
                high((s + 1) % SLOTS, i * 16 + (t0 // SLOTS * 16 + 16 + 16 * ((s + 1) // SLOTS)),
                     i * SLOTS + (t0 + s))

            act.wait_ge(sem("gst_stored"), 128)
            high(0, T_OUT // SLOTS * 16 + 16, None)
            with act.Fori(0, N_OUT // SLOTS) as i:
                for s in range(SLOTS):
                    high_next(i, s, T_OUT)
            act.wait_ge(sem("x1_done"), N_OUT + SLOTS)
            squares([xT[:, k, :] for k in range(KT)])
            root(1.0 / D, epsc[:, 0:1])
            high_h(2, hTh)
            with act.Fori(0, N_Q // SLOTS) as i:
                for s in range(SLOTS):
                    high_next(i, s, T_Q)
                    act.wait_ge(gemm_done, i * SLOTS + (T_Q + s + 1))
                    act.copy(qT[:, i * SLOTS + s, :], ps[:, s, 0:T]).then_inc(sem("q_ready"), 1)
            def finish(t):
                t0, n = TILES[t]
                c = cvv[0:64, 0:1] if t == 0 else cvv
                act.wait_ge(sem("cv_sub"), t + 1)
                act.activation(c, c, ACT.Exp).then_inc(sem("cv_exp"), 1)
                act.wait_ge(sem("tk_ps"), t + 1)
                for j, v in enumerate((i1T, i2T, gT)):
                    act.copy(v[:, t0:t0 + n], ps[:, TKB[t], j * 128:j * 128 + n]).then_inc(sem("tk_ready"), 1)

            def gate_copy(n, b, quarter, t0, bank=6):
                act.wait_ge(sem("g_ps"), n + 3)
                act.copy(G[:, bass.ds(quarter, QE), bass.ds(t0, GT)].rearrange("p a t -> p t a"),
                         ps[:, bank + b, 0:GT * QE].rearrange("p (t a) -> p t a", t=GT)).then_inc(sem("g_copied"), 1)

            def split(i, j):
                if j == 1:
                    act.wait_ge(sem("v_done"), i * KT + 1)
                elif j and j <= SLOTS + 1:
                    act.wait_ge(gemm_done, i * SLOTS + (T_U + j - 1))
                elif j:
                    act.wait_ge(sem("v_done"), i * KT + (4 * (j - SLOTS - 1) + 1))
                high(j % SLOTS, i * 32 + (T_U // SLOTS * 16 + 16 * (j // SLOTS) + 16), None)

            act.wait_ge(sem("x1_stored"), 16)
            finish(0)
            finish(1)
            with act.Fori(0, EARLY // 2) as i:
                for b in range(2):
                    gate_copy(i * 2 + b, b, 0, i * (2 * GT) + b * GT, 2)
            finish(2)
            with act.Fori(EARLY // 2, NG // 2) as i:
                for b in range(2):
                    gate_copy(i * 2 + b, b, 0, i * (2 * GT) + b * GT, 2)

            def expert_step(i, groups, g0, quarter, t0, end=False):
                for s in range(SLOTS):
                    split(i, s + 1)
                    act.wait_ge(gemm_done, i * SLOTS + (T_U + s + 1))
                    act.wait_ge(sem("coef_ready"), i * SLOTS + (s + 1))
                    act.activation(craw[:, s % 2, :], ps[:, s % 2, 0:T], ACT.Gelu).then_inc(sem("gelu_done"), 1)
                    if groups and s:
                        g = groups[s - 1]
                        gate_copy(g0 + g, g % 2, quarter, t0 + g * GT)
                for q in range(3 if end else 4):
                    split(i, SLOTS + q + 1)

            for q in range(3):
                if q:
                    act.wait_ge(sem("coef_ready"), q * QE + 2)
                with act.Fori(0, 4) as i2:
                    at = (i2 * 6 + (NG * (q + 1)), (1 - q % 2) * QE, i2 * (6 * GT))
                    expert_step(i2 * 2 + 8 * q, (0, 1, 2), *at)
                    expert_step(i2 * 2 + (8 * q + 1), (3, 4, 5), *at)
            with act.Fori(24, 31) as i:
                expert_step(i, None, None, None, None)
            expert_step(31, None, None, None, None, end=True)
            act.wait_ge(sem("x2_ready"), 1)
            squares([xT[:, k, :] for k in range(KT)])
            root(1.0 / D, epsc[:, 0:1])

        @block.vector
        def _(dve):
            gemm_done = sem("gemm_done")
            st = Steps(dve, sem("dve_steps"))
            norms = [0]
            link = st.link

            def tt(out, x, y, op):
                return dve.tensor_tensor(out, x, y, op)

            def ts(out, x, s1, s2, op0, op1=ALU.bypass):
                return dve.tensor_scalar(out, x, s1, s2, op0, op1)

            def stt(out, x, s, y, op0, op1):
                return dve.scalar_tensor_tensor(out=out, in0=x, scalar=s, in1=y, op0=op0, op1=op1)

            def inv_root():
                k = norms[0]
                norms[0] += 1
                dve.wait_ge(sem("norm_sqrt"), k + 1)
                link(dve.reciprocal(nrm[:, k % 2, :], nrm[:, k % 2, :]))
                return nrm[:, k % 2, :]

            def over(v, n, at=1):
                return v.unsqueeze(at).broadcast_to(list(v.shape[:at]) + [n] + list(v.shape[at:]))

            dve.memset(sT[:, :, NC:32], 0.0).then_inc(sem("s_zero"), 1)
            dve.sem_inc(sem("x1_done"), SLOTS)
            dve.sem_inc(sem("v_added"), 4)
            dve.memset(raw[:, :, 0:3], 0.0).then_inc(sem("raw_zero"), 1)
            dve.wait_ge(sem("ld_par"), 16)
            dve.wait_ge(sem("ld_const"), 16)

            def modulated(w, sh, sc, k):
                link(stt(mod[:, sc:sc + KT, :], mod[:, sc:sc + KT, :], 1.0, over(w, NC, 2), ALU.add, ALU.mult))
                r = inv_root()
                link(tt(hT, xT, over(r, KT), ALU.mult))
                for j in range(KT):
                    st.mark(ts(hT[:, j, 0:TP], hT[:, j, 0:TP], mod[:, sc + j, 0:1], mod[:, sh + j, 0:1],
                               ALU.mult, ALU.add))
                link(tt(hT[:, :, TP:T], hT[:, :, TP:T], mod[:, sc:sc + KT, 1:NC], ALU.mult))
                tt(hT[:, :, TP:T], hT[:, :, TP:T], mod[:, sh:sh + KT, 1:NC], ALU.add).then_inc(sem("h_ready"), 1)
                dve.wait_ge(sem("h_ready"), k)
                dve.engine_nop().then_inc(sem("norm_free"), 1)

            dve.wait_ge(sem("ada_ps"), N_ADA1 // SLOTS)
            link(tt(mod[:, 0:32, :], ps[:, 7, 0:32 * NC].rearrange("p (n c) -> p n c", c=NC),
                    over(bada[:, 0:32], NC, 2), ALU.add))
            modulated(n1w, 0, 16, 1)

            dve.wait_ge(sem("small_done"), 1)
            link(ts(xbr, ps[0:32, 6, 0:T], rbias, None, ALU.add))
            stt(abr, xbr, -1.0, xbr, ALU.mult, ALU.max).then_inc(sem("abs_ready"), 1)
            dve.wait_ge(sem("exp_ready"), 1)
            link(ts(z1r, abr, 2.0, None, ALU.add))
            link(dve.reciprocal(z1r, z1r))
            link(tt(z1r, z1r, abr, ALU.mult))
            link(tt(z2r, z1r, z1r, ALU.mult))
            link(ts(polyr, z2r, 1.0 / 17, None, ALU.mult))
            for c in (15, 13, 11, 9, 7, 5, 3):
                link(stt(polyr, polyr, 1.0 / c, z2r, ALU.add, ALU.mult))
            link(stt(polyr, polyr, 1.0, z1r, ALU.add, ALU.mult))
            link(ts(polyr, polyr, 2.0, None, ALU.mult))
            link(stt(spr, xbr, 0.0, polyr, ALU.max, ALU.add))
            dve.wait_ge(sem("sg_ready"), 2)
            link(ts(dAr, spr, rbias2[:, 0:1], -1.0, ALU.mult, ALU.mult))
            link(dve.tensor_copy(smp[:, 8:16], spr[:, TP:T]))
            dve.tensor_copy(smp[:, 16:24], sgr[:, TP:T]).then_inc(sem("small_rows"), 1)
            dve.wait_ge(sem("small_rows"), 1)
            dve.sem_inc(sem("dA_ready"), 1)

            def low(n, slot):
                dve.wait_ge(sem("hi_ready"), n + 1)
                tt(wlo[:, slot % 2], wring[:, slot], whi_f[:, slot % 2], ALU.subtract).then_inc(sem("lo_ready"), 1)

            def low_h(k, high):
                for j in range(0, KT, 4):
                    dve.wait_ge(sem("hth_ready"), 4 * k + j // 4 + 1)
                    tt(hTl[:, j:j + 4], hT[:, j:j + 4], high[:, j:j + 4], ALU.subtract).then_inc(sem("hl_ready"), 1)

            low_h(0, h1h_f)
            low(0, 0)
            low(1, 1)
            with dve.Fori(0, N_CONV // SLOTS) as i:
                st.enter(i, 3 * SLOTS)
                for s in range(SLOTS):
                    w = lambda j: convw[:, bass.ds(i * (4 * SLOTS) + (4 * s + j), 1)]
                    dve.wait_ge(sem("raw_ready"), i * (3 * SLOTS) + 3 * (SLOTS + s + 1))
                    dve.wait_ge(sem("cv_ready"), i * (2 * SLOTS) + 2 * (s + 1))
                    link(ts(cac[:, s, :], raw[:, s, 0:CV], w(0), None, ALU.mult))
                    for j in (1, 2):
                        link(stt(cac[:, s, :], raw[:, s, j:j + CV], w(j), cac[:, s, :], ALU.mult, ALU.add))
                    stt(cac[:, s, :], raw[:, s, 3:3 + CV], w(3), cac[:, s, :], ALU.mult, ALU.add
                        ).then_inc(sem("conv_done"), 1)
                    low(i * SLOTS + (s + 2), (s + 2) % SLOTS)
            st.leave(N_CONV // SLOTS)
            with dve.Fori(0, N_GATE // SLOTS - 1) as i:
                for s in range(SLOTS):
                    low(i * SLOTS + (N_CONV + s + 2), (s + 2) % SLOTS)
            for s in (2, 3):
                low(N_CONV + N_GATE - SLOTS + s, s)

            dve.wait_ge(sem("tok_ps"), 1)
            dve.tensor_copy(tok.rearrange("p a b -> p (a b)"), ps[:, 6, 0:192]).then_inc(sem("tok_ready"), 1)
            dve.wait_ge(sem("cs_ps"), 1)
            link(dve.tensor_copy(cst2.rearrange("p a b -> p (a b)"), ps[:, 7, 256:320]))
            dve.tensor_copy(csr, ps[0:32, 7, 0:TP]).then_inc(sem("cs_ready"), 1)
            dve.wait_ge(sem("cs_ready"), 1)
            for h in range(16):
                r = inv_root()
                tt(cv[:, h, :], cv[:, h, :], r, ALU.mult).then_inc(sem("norm_free"), 1)

            dve.wait_ge(sem("cso_stored"), 16)
            for c in range(2):
                for j in range(2):
                    dve.wait_ge(sem("xt_ps"), 8 * c + 4 * j + 4)
                    st.mark(tt(xdt[:, c, j * 512:(j + 1) * 512].rearrange("p (h d) -> p h d", d=64),
                               ps[:, 2 * c + j, :].rearrange("p (h d) -> p h d", d=64),
                               over(tok[:, 2 + c, 8 * j:8 * j + 8], 64, 2), ALU.mult))
            st.settle()
            dve.sem_inc(sem("xdt_ready"), 1)
            dve.wait_ge(sem("ld_br"), 16)
            for c in range(2):
                last = tt(Wt[:, c, :], BR[:, 0:24, c * CH + CH - 1], cst2[:, c, 0:24], ALU.subtract)
                if c == 0:
                    link(last)
            last.then_inc(sem("w_sub"), 1)
            dve.wait_ge(sem("w_exp"), 3)
            link(tt(wf0, Wt[:, 0, :], LE1, ALU.mult))
            stt(nbe, nbe, -1.0, tok[:, 5, 24:32], ALU.mult, ALU.mult).then_inc(sem("wf_ready"), 1)

            def decay(c):
                link(tt(Mb, BR[:, 0:HS, c * CH:(c + 1) * CH], over(cst2[:, c, 0:HS], CH, 2), ALU.subtract))
                ts(Mb, Mb, 0.0, None, ALU.min).then_inc(sem("m_sub"), 1)

            decay(0)
            dve.wait_ge(sem("cb_ps"), 1)
            link(tt(cbm, ps[:, 6, :].rearrange("p (a t) -> p a t", a=4), over(tri, 4), ALU.mult))
            for c in range(2):
                dve.wait_ge(sem("m_exp"), c + 1)
                link(tt(Mb[:, 0:8, :], Mb[:, 0:8, :], over(cbm[:, 2 * c, :], 8), ALU.mult))
                tt(Mb[:, 8:16, :], Mb[:, 8:16, :], over(cbm[:, 2 * c + 1, :], 8), ALU.mult
                   ).then_inc(sem("m_ready"), 1)
                if c == 0:
                    for hp in range(8):
                        dve.wait_ge(sem("y_ps"), hp // 4 * 4 + 4)
                        yt = cv[:, TX + hp, 0:CH]
                        stt(yt, yt, dcol[:, hp:hp + 1], ps[:, 4 + hp // 4, (hp % 4) * 128:(hp % 4 + 1) * 128],
                            ALU.mult, ALU.add).then_inc(sem("y_evac"), 1)
                    decay(1)
            dve.wait_ge(sem("m_used"), 1)
            for hp in range(8):
                yt = cv[:, TX + hp, CH:TP]
                stt(yt, yt, dcol[:, hp:hp + 1], ps[:, 4 + hp // 4, (hp % 4) * 128:(hp % 4 + 1) * 128],
                    ALU.mult, ALU.add).then_inc(sem("y_evac"), 1)
            dve.wait_ge(sem("m_exp"), 3)
            for g in range(2):
                m = Mb[:, 8 * g:8 * g + 8, :]
                last = tt(m, m, over(cv[:, TC + g, CH:TP], 8), ALU.mult)
                if g == 0:
                    link(last)
            last.then_inc(sem("ce_ready"), 1)
            dve.wait_ge(sem("y_evac"), 16)
            for hp in range(8):
                dve.wait_ge(sem("y_ps"), hp // 4 * 4 + 12)
                yt = cv[:, TX + hp, CH:TP]
                tt(yt, yt, ps[:, 6 + hp // 4, (hp % 4) * 128:(hp % 4 + 1) * 128], ALU.add
                   ).then_inc(sem("y_evac"), 1)

            dve.wait_ge(sem("norm_free"), 17)
            with dve.Fori(0, 4) as i:
                st.enter(i, GDN_STEPS)
                dve.wait_ge(sem("gdn_free"), i + 1)
                d4 = Dm.rearrange("p (h c) t -> p h c t", h=2)
                for h in range(2):
                    st.mark(tt(Dm[:, 2 * h:2 * h + 2, :],
                               BR[:, i * 2 + (16 + h), :].rearrange("p (c t) -> p c t", c=2),
                               over(cst2[:, :, bass.ds(i * 2 + (16 + h), 1)].rearrange("p c o -> p (c o)"), CH, 2),
                               ALU.subtract))
                tt(kb.rearrange("p (h c) t -> p h (c t)", h=2), cv[:, bass.ds(i * 2 + TK, 2), 0:TP],
                   BR[:, bass.ds(i * 2 + 24, 2), :], ALU.mult).then_inc(sem("kb_ready"), 1)
                st.settle()
                ts(Dm, Dm, 0.0, None, ALU.min).then_inc(sem("dm_sub"), 1)
                dve.wait_ge(sem("dm_exp"), i + 1)
                link(tt(Dm, Dm, over(tri, 4), ALU.mult))
                dve.wait_ge(sem("kk_ps"), i + 1)
                link(tt(LT, Dm, ps[:, 0, :].rearrange("p (a t) -> p a t", a=4), ALU.mult))
                link(tt(Bm0, LT, over(lvl[:, 0, :], 4), ALU.mult))
                dve.sem_inc(sem("lt_ready"), 1)
                tt(Tt, over(ident, 4), Bm0, ALU.subtract).then_inc(sem("t_ready"), 1)
                tt(QK, Dm, ps[:, 1, :].rearrange("p (a t) -> p a t", a=4), ALU.mult).then_inc(sem("qk_ready"), 1)
                dve.wait_ge(sem("x_ps"), i * LV + 1)
                tt(Tm, over(ident, 4), ps[:, 0, :].rearrange("p (a t) -> p a t", a=4), ALU.subtract
                   ).then_inc(sem("t_ready"), 1)
                dve.wait_ge(sem("qg_exp"), i + 1)
                st.mark(tt(qg, qg, cv[:, bass.ds(i * 2 + TQ, 2), CH:TP], ALU.mult))
                dve.wait_ge(sem("vt_ps"), i + 1)
                r4 = Rv.rearrange("p (h c) t -> p h c t", h=2)
                k4 = kd.rearrange("p (h c) t -> p h c t", h=2)
                v4 = ps[:, 2, :].rearrange("p (h c t) -> p h c t", h=2, c=2)
                kt4 = ps[:, 3, :].rearrange("p (h c t) -> p h c t", h=2, c=2)
                dve.wait_ge(sem("kt_ps"), i + 1)
                for c in range(2):
                    last = tt(k4[:, :, c, :], kt4[:, :, c, :], over(Wt[:, c, bass.ds(i * 2 + 16, 2)], P, 2), ALU.mult)
                    st.mark(last)
                    last = tt(r4[:, :, c, :], v4[:, :, c, :], over(tok[:, 4 + c, bass.ds(i * 2 + 24, 2)], P, 2),
                              ALU.mult)
                    if c == 0:
                        last.then_inc(sem("rv0_ready"), 1)
                    else:
                        last.then_inc(sem("rv_ready"), 1)
                for l in range(1, LV):
                    dve.wait_ge(sem("tt_ps"), i * (LV - 1) + l)
                    tt(Tt, Tt, ps[:, 1, :].rearrange("p (a t) -> p a t", a=4), ALU.subtract
                       ).then_inc(sem("t_ready"), 1)
                    if l < LV - 1:
                        tt(Tm, Tm, ps[:, 4, :].rearrange("p (a t) -> p a t", a=4), ALU.subtract
                           ).then_inc(sem("t_ready"), 1)
                    else:
                        dve.engine_nop().then_inc(sem("t_ready"), 1)
                dve.wait_ge(sem("ks_ps"), i + 1)
                for h in range(2):
                    last = stt(Rv[:, 2 * h + 1, :], ps[:, 0, 256 + h * 128:256 + (h + 1) * 128],
                               nbe[:, bass.ds(i * 2 + h, 1)], Rv[:, 2 * h + 1, :], ALU.mult, ALU.add)
                    if h == 0:
                        st.mark(last)
                last.then_inc(sem("rv_ready"), 1)
                dve.wait_ge(sem("o_ps"), i + 1)
                link(dve.tensor_copy(cv[:, bass.ds(i * 2 + TQ, 2), 0:TP],
                                     ps[:, 5, :].rearrange("p (h t) -> p h t", h=2)))
                dve.wait_ge(sem("ada_ps"), i * 4 + (N_ADA1 // SLOTS + 4))
                st.mark(tt(mod[:, bass.ds(i * 16 + 32, 16), :],
                           ps[:, 7, 0:16 * NC].rearrange("p (n c) -> p n c", c=NC),
                           over(bada[:, bass.ds(i * 16 + 32, 16)], NC, 2), ALU.add))
                dve.wait_ge(sem("s_ps"), i * 2 + 2)
                dve.wait_ge(sem("s2_free"), i + 1)
                for h in range(2):
                    last = stt(S2[:, h, :], S1[:, h, :], LE1[:, bass.ds(i * 2 + (16 + h), 1)],
                               ps[:, 1, h * 128:(h + 1) * 128], ALU.mult, ALU.add)
                    if h == 0:
                        st.mark(last)
                last.then_inc(sem("gdn_free"), 1)
            st.leave(4)

            dve.wait_ge(sem("ld_sr"), 16)
            for q in range(2):
                rows = slice(64 * q, 64 * q + 64)
                for dst, src in ((Esel, SR[:, 0:HS, 0]), (dtsel, SR[:, 0:HS, 1])):
                    link(dve.tensor_copy(dst[rows], src[rows, q:HS:2, :]))
            link(tt(XD, cv[:, TX:TX + 8, TP:T], dtsel, ALU.mult))
            dve.wait_ge(sem("ld_bc"), 16)
            for j in range(4):
                b = j % 2
                dve.wait_ge(sem(f"ld_sst{b}"), 16 * (j // 2 + 1))
                s4 = sst[:, b].rearrange("p (b t) n -> p b t n", b=2)
                t4 = stm.rearrange("p (b t) n -> p b t n", b=2)
                link(tt(s4, s4, over(Esel[:, :, 2 * j:2 * j + 2].rearrange("p t b -> p b t"), 128, 3), ALU.mult))
                for bb in range(2):
                    link(tt(t4[:, bb].rearrange("p (g t) n -> p g t n", g=2),
                            over(BC[:, 0:2, 2 * j + bb, :], 4, 2),
                            over(XD[:, :, 2 * j + bb].rearrange("p (g t) -> p g t", g=2), 128, 3), ALU.mult))
                link(tt(sst[:, b], sst[:, b], stm, ALU.add))
                dve.sem_inc(sem("sst_ready"), 1)
                for bb in range(2):
                    link(tt(t4[:, bb].rearrange("p (g t) n -> p g t n", g=2),
                            s4[:, bb].rearrange("p (g t) n -> p g t n", g=2),
                            over(BC[:, 2:4, 2 * j + bb, :], 4, 2), ALU.mult))
                dve.sem_inc(sem("sst_used"), 1)
                link(dve.tensor_reduce(ysm[:, 2 * j:2 * j + 2, :].rearrange("p b t -> p (b t)"), stm, AX, ALU.add))
            dve.sem_inc(sem("sst_done"), 1)
            xs = cv[:, TX:TX + 8, TP:T]
            link(tt(xs, xs, over(dcol, TS, 2), ALU.mult))
            link(tt(xs, xs, ysm.rearrange("p b t -> p t b"), ALU.add))
            link(tt(cv[:, TX:TX + 8, :], cv[:, TX:TX + 8, :], zg[:, 0:8, :], ALU.mult))
            dve.sem_inc(sem("ygate_ready"), 1)

            qs, ks, vs = (cv[:, t:t + 8, TP:T] for t in (TQ, TK, TV))
            eight = lambda v: v.rearrange("p (h b) -> p h b", b=TS)
            link(tt(eight(qkp), qs, ks, ALU.mult))
            dve.sem_inc(sem("qkp_ready"), 1)
            kq4 = kq.rearrange("p (h b) w -> p h b w", b=TS)
            link(dve.tensor_copy(kq4[:, :, :, 0], ks))
            link(dve.tensor_copy(kq4[:, :, :, 1], qs))
            dve.sem_inc(sem("kq_ready"), 1)
            dve.wait_ge(sem("skq_ps"), 1)
            dve.wait_ge(sem("qk_ps"), 1)
            skq = ps[:, 2, 0:128].rearrange("p (h b w) -> p h b w", b=TS, w=2)
            eg = SR[:, 16:24, 0, :]
            be = SR[:, 24:32, 2, :]
            link(tt(eight(vn), skq[:, :, :, 0], eg, ALU.mult))
            link(tt(eight(vn), vs, eight(vn), ALU.subtract))
            link(tt(eight(vn), eight(vn), be, ALU.mult))
            dve.sem_inc(sem("vns_ready"), 1)
            link(tt(eight(ksm), skq[:, :, :, 1], eg, ALU.mult))
            link(tt(vsm, vn, ps[:, 1, 0:64], ALU.mult))
            link(tt(qs, eight(ksm), eight(vsm), ALU.add))
            dve.sem_inc(sem("o_ready"), 1)
            for j in range(2):
                s3 = gst[:, 32 * j:32 * j + 32, :]
                s4 = s3.rearrange("p (h b) v -> p h b v", b=TS)
                link(tt(s4, s4, over(SR[:, 16 + 4 * j:20 + 4 * j, 0, :], 128, 3), ALU.mult))
                dve.wait_ge(sem("ld_gvb"), 16 * (j + 1))
                g4 = gvb.rearrange("p (h b) v -> p h b v", b=TS)
                link(tt(g4, g4, over(cv[:, TK + 4 * j:TK + 4 * j + 4, TP:T], 128, 3), ALU.mult))
                link(tt(s3, s3, gvb, ALU.add))
                dve.sem_inc(sem("gst_ready"), 1)
            for g in range(2):
                r = inv_root()
                for j in range(4):
                    t = 4 * g + j
                    v = cv[:, TX + t, :]
                    last = stt(v, v, ynw[:, t:t + 1], r, ALU.mult, ALU.mult)
                    if j < 3:
                        st.mark(last)
                last.then_inc(sem("norm_free"), 1)
            dve.wait_ge(sem("norm_free"), norms[0])
            dve.sem_inc(sem("mix_ready"), 1)
            for h in range(HG):
                r = inv_root()
                v = cv[:, TQ + h, :]
                stt(v, v, onw[:, 0:1], r, ALU.mult, ALU.mult).then_inc(sem("norm_free"), 1)
            dve.wait_ge(sem("norm_free"), norms[0])
            tt(cv[:, TQ:TQ + 8, :], cv[:, TQ:TQ + 8, :], zg[:, 8:16, :], ALU.mult).then_inc(sem("mix_ready"), 1)
            for j, t in enumerate((TX, TQ)):
                dve.wait_ge(sem("mixh_ready"), j + 1)
                tt(mixl[:, 8 * j:8 * j + 8], cv[:, t:t + 8, :], mixh_f[:, 8 * j:8 * j + 8], ALU.subtract
                   ).then_inc(sem("mixl_ready"), 1)
            low(L_OUT, 0)

            G1 = 32
            with dve.Fori(0, N_OUT // SLOTS) as i:
                st.enter(i, 2 * SLOTS)
                for s in range(SLOTS):
                    n = i * SLOTS + s
                    low(i * SLOTS + (L_OUT + s + 1), (s + 1) % SLOTS)
                    dve.wait_ge(gemm_done, i * SLOTS + (T_OUT + s + 1))
                    st.mark(stt(xT[:, n, 0:TP], ps[:, s, 0:TP], mod[:, n + G1, 0:1], xT[:, n, 0:TP],
                                ALU.mult, ALU.add))
                    link(tt(gtmp[:, s, :], ps[:, s, TP:T], mod[:, n + G1, 1:NC], ALU.mult))
                    tt(xT[:, n, TP:T], xT[:, n, TP:T], gtmp[:, s, :], ALU.add).then_inc(sem("x1_done"), 1)
            st.leave(N_OUT // SLOTS)
            dve.wait_ge(sem("x1_done"), N_OUT + SLOTS)
            modulated(n2w, 48, 64, 2)
            low_h(1, hTh_f)
            with dve.Fori(0, N_Q // SLOTS) as i:
                for s in range(SLOTS):
                    low(i * SLOTS + (L_Q + s + 1), (s + 1) % SLOTS)

            dve.wait_ge(sem("x1_stored"), 16)
            link(dve.memset(Qs, 0.0))
            dve.wait_ge(sem("q_ready"), N_Q + SLOTS)
            for j in range(16):
                at = (j % 2) * 64 + (j // 2) * TS
                st.mark(dve.tensor_copy(Qs[:, j, at:at + TS], qT[:, j, TP:T]))
            st.settle()
            dve.sem_inc(sem("qs_ready"), 1)

            def top16(items, between=()):
                between = list(between)

                def stage(ops):
                    for it in items:
                        for op in ops:
                            st.mark(op(*it))
                    if between:
                        between.pop(0)()
                    st.settle()

                stage([lambda x, v, i, w: dve.max(v[:, 0:8], x)])
                stage([lambda x, v, i, w: dve.max_index(i[:, 0:8], v[:, 0:8], x),
                       lambda x, v, i, w: dve.match_replace(w, v[:, 0:8], x, -3.0e38)])
                stage([lambda x, v, i, w: dve.max(v[:, 8:16], w)])
                stage([lambda x, v, i, w: dve.max_index(i[:, 8:16], v[:, 8:16], w)])

            def candidates(t, n, heads, values, indices, between=()):
                link(tt(cand[0:n, 0:heads].rearrange("p h (a b) -> p h a b", b=16), over(values(0), 16, 3),
                        over(values(1), 16, 2), ALU.add))
                top16([(cand[0:n, h, :], cvv[0:n, h, :], ciu[0:n, h, :], work[0:n, h * 256:(h + 1) * 256])
                       for h in range(heads)], between)
                c, gs = cvv[0:n, 0:heads], gsum[0:n, 0:heads]
                link(dve.tensor_copy(gs, c[:, :, 0]))
                link(tt(c, c, over(gs, 16, 2), ALU.subtract))
                dve.sem_inc(sem("cv_sub"), 1)
                m = heads * 16
                for side, (op, by), dst in ((0, (ALU.logical_shift_right, 4), tkI1),
                                            (1, (ALU.bitwise_and, 15), tkI2)):
                    link(ts(rcu[0:n, 0:heads], ciu[0:n, 0:heads], by, None, op))
                    link(dve.tensor_copy(rcf[0:n, 0:heads], rcu[0:n, 0:heads]))
                    rflat = rcf[0:n, 0:heads].rearrange("p h k -> p (h k)")
                    link(tt(oh[0:n, 0:m], over(rflat, 16, 2), over(iota[0:n, 0:16], m), ALU.is_equal))
                    o4 = oh[0:n, 0:m].rearrange("p (h k) r -> p h k r", k=16)
                    link(tt(o4, o4, over(indices(side), 16, 2), ALU.mult))
                    link(dve.tensor_reduce(dst[0:n, 0:m], oh[0:n, 0:m], AX, ALU.add))
                dve.wait_ge(sem("cv_exp"), t + 1)
                link(dve.tensor_reduce(gs, c, AX, ALU.add))
                link(dve.reciprocal(gs, gs))
                link(tt(tkG[0:n, 0:m].rearrange("p (h k) -> p h k", k=16), c, over(gs, 16, 2), ALU.mult))

            dve.wait_ge(sem("score_ps"), 1)
            top16([(ps[:, 4, 0:128], sv[:, 0, :], siu[:, 0, :], work[:, 0:128])])
            link(dve.tensor_copy(sv[:, 1, :], siu[:, 0, :]))
            dve.sem_inc(sem("pair_ready"), 1)
            dve.wait_ge(sem("pair_ps"), 1)
            link(dve.tensor_copy(sv[0:64, 2:6, :].rearrange("p a k -> p (a k)"), ps[0:64, 5, 0:64]))
            candidates(0, 64, 1, lambda side: sv[0:64, 2 + 2 * side:3 + 2 * side, :],
                       lambda side: sv[0:64, 3 + 2 * side:4 + 2 * side, :])
            for j, v in enumerate((tkI1, tkI2, tkG)):
                st.mark(tt(oh[0:64, 8 * j:8 * j + 8, :], over(v[0:64, 0:16], 8), over(of_head[0:64], 16, 2), ALU.mult))
            st.settle()
            dve.sem_inc(sem("top_done"), 1)

            def prompt(t, between=((), ())):
                n = TILES[t][1]
                dve.wait_ge(sem("score_ps"), t + 1)
                dve.wait_ge(sem("tk_ps"), t)
                top16([(ps[0:n, 4 * (t - 1) + j // 4, (j % 4) * 128:(j % 4 + 1) * 128], sv[0:n, j, :], siu[0:n, j, :],
                        work[0:n, j * 128:(j + 1) * 128]) for j in range(16)], between[0])
                link(dve.tensor_copy(sif[0:n], siu[0:n]))
                sv4 = sv[0:n].rearrange("p (h s) k -> p h s k", s=2)
                si4 = sif[0:n].rearrange("p (h s) k -> p h s k", s=2)
                candidates(t, n, 8, lambda side: sv4[:, :, side, :], lambda side: si4[:, :, side, :], between[1])
                dve.sem_inc(sem("top_done"), 1)

            def gate_parts(t0, n, ready):
                dve.wait_ge(sem("tk_ready"), ready)
                for part in range(3):
                    link(dve.tensor_copy(gp[:, t0:t0 + n, part], gT[:, t0:t0 + n]))
                    if part < 2:
                        link(tt(gT[:, t0:t0 + n], gT[:, t0:t0 + n], gp[:, t0:t0 + n, part], ALU.subtract))
                dve.sem_inc(sem("gp_ready"), 1)

            def one_hots(n, b, quarter, t0):
                dve.wait_ge(sem("g_ps"), n + 1)
                tt(Soh[:, b], over(iota[:, quarter * QE:(quarter + 1) * QE], GT),
                   over(i2T[:, bass.ds(t0, GT)], QE, 2), ALU.is_equal).then_inc(sem("soh_ready"), 1)
                tt(Aoh[:, b], over(iota, GT), over(i1T[:, bass.ds(t0, GT)], P, 2), ALU.is_equal
                   ).then_inc(sem("aoh_ready"), 1)

            def early(*groups):
                def go():
                    for g in groups:
                        one_hots(g, g % 2, 0, g * GT)
                return go

            prompt(1)
            prompt(2, ((lambda: gate_parts(0, P, 6), early(0, 1), early(2, 3), early(4, 5)),
                       (early(6), early(7), early(8), early(9))))

            dve.memset(acc, 0.0).then_inc(sem("acc_zero"), 1)
            dve.wait_ge(sem("acc_zero"), 1)
            dve.sem_inc(sem("coef_ready"), 2)
            gate_parts(TP, TS, 3)
            gate_parts(P, P, 9)

            def split(i, j):
                low(i * (2 * SLOTS) + (L_E + j), j % SLOTS)

            with dve.Fori(EARLY // 2, NG // 2) as i:
                for b in range(2):
                    one_hots(i * 2 + b, b, 0, i * (2 * GT) + b * GT)

            def expert_step(i, groups, g0, quarter, t0, col, end=False):
                def oh(j):
                    if groups:
                        g = groups[j]
                        one_hots(g0 + g, g % 2, quarter + 1, t0 + g * GT)

                for s in range(SLOTS):
                    split(i, s + 1)
                    if s < 3:
                        oh(s)
                    c, g = craw[:, s % 2, :], G[:, col + s, :]
                    dve.wait_ge(sem("gelu_done"), i * SLOTS + (s + 3))
                    st.mark(tt(chi[:, s, :], c, g, ALU.mult))
                    link(tt(c, c, g, ALU.mult))
                    tt(clo[:, s, :], c, chi_f[:, s, :], ALU.subtract).then_inc(sem("coef_ready"), 1)
                for q in range(4):
                    if not (end and q == 3):
                        split(i, SLOTS + q + 1)
                    dve.wait_ge(sem("v_added"), i * KT + (4 * q + 4))
                    for d in range(4):
                        dve.wait_ge(sem("v_done"), i * KT + (4 * q + d + 2))
                        tt(acc[:, 4 * q + d, :], acc[:, 4 * q + d, :], ps[:, 2 + d, 0:T], ALU.add
                           ).then_inc(sem("v_added"), 1)

            for q in range(4):
                dve.wait_ge(sem("g_copied"), NG * (q + 1) + 2)
                half = (q % 2) * QE
                if q < 3:
                    with dve.Fori(0, 4) as i2:
                        st.enter(i2, 16)
                        g0 = i2 * 6 + NG * (q + 1)
                        expert_step(i2 * 2 + 8 * q, (0, 1, 2), g0, q, i2 * (6 * GT), i2 * 8 + half)
                        expert_step(i2 * 2 + (8 * q + 1), (3, 4, 5), g0, q, i2 * (6 * GT), i2 * 8 + (half + 4))
                    st.leave(4)
                else:
                    with dve.Fori(0, 7) as i:
                        st.enter(i, 8)
                        expert_step(i + 24, None, None, None, None, i * 4 + half)
                    st.leave(7)
                    expert_step(31, None, None, None, None, 28 + half, end=True)

            dve.wait_ge(sem("x1_back"), 16)
            dve.wait_ge(sem("v_added"), N_U // SLOTS * KT + 4)
            G2 = 80
            for j in range(KT):
                st.mark(stt(xT[:, j, 0:TP], acc[:, j, 0:TP], mod[:, G2 + j, 0:1], xT[:, j, 0:TP], ALU.mult, ALU.add))
            link(tt(acc[:, :, TP:T], acc[:, :, TP:T], mod[:, G2:G2 + KT, 1:NC], ALU.mult))
            link(tt(xT[:, :, TP:T], xT[:, :, TP:T], acc[:, :, TP:T], ALU.add))
            dve.sem_inc(sem("x2_ready"), 1)
            r = inv_root()
            for j in range(KT):
                st.mark(stt(hT[:, j, :], xT[:, j, :], fnw[:, j:j + 1], r, ALU.mult, ALU.mult))
            st.settle()
            dve.sem_inc(sem("y_ready"), 1)

        @block.gpsimd
        def _(pool):
            def tt(out, x, y, op):
                return pool.tensor_tensor(out, x, y, op)

            def over(v, n, at=1):
                return v.unsqueeze(at).broadcast_to(list(v.shape[:at]) + [n] + list(v.shape[at:]))

            pool.sem_inc(sem("s2_free"), 1)
            pool.wait_ge(sem("smp_exp"), 1)
            pool.wait_ge(sem("cs_ready"), 1)
            pool.dma_start(a["rows_dram"][0:24, :], csr[0:24, :]).then_inc(sem("rows_out"), 16)
            pool.dma_start(a["rows_dram"][24:32, :], sgr[24:32, 0:TP]).then_inc(sem("rows_out"), 16)
            pool.dma_start(a["smp_dram"], smp[0:32]).then_inc(sem("rows_out"), 16)
            pool.wait_ge(sem("cso_ready"), 2 * CT)
            pool.dma_start(o["conv_out"], cso).then_inc(sem("cso_stored"), 16)
            pool.wait_ge(sem("rows_out"), 48)
            pool.wait_ge(sem("cv_ready"), 2 * CT + 8)
            pool.dma_start(BR, a["rows_dram"].partition_broadcast(P)).then_inc(sem("ld_br"), 16)
            pool.dma_start(SR.rearrange("p r k b -> p r (k b)"), a["smp_dram"].partition_broadcast(P)
                           ).then_inc(sem("ld_sr"), 16)
            pool.wait_ge(sem("xdt_ready"), 1)
            pool.wait_ge(sem("w_exp"), 3)
            pool.wait_ge(sem("cso_stored"), 16)
            x0, x1 = (xdt[:, c, :].rearrange("p (h d) -> p h d", d=64) for c in range(2))
            f0, f1 = (xwf[:, c, :].rearrange("p (h d) -> p h d", d=64) for c in range(2))
            tt(xw0, x0, over(Wt[:, 0, 0:HS], 64, 2), ALU.mult).then_inc(sem("xw_ready"), 1)
            tt(f1, x1, over(Wt[:, 1, 0:HS], 64, 2), ALU.mult).then_inc(sem("xw_ready"), 1)
            pool.wait_ge(sem("wf_ready"), 1)
            tt(f0, x0, over(wf0[:, 0:HS], 64, 2), ALU.mult).then_inc(sem("xw_ready"), 1)
            pool.wait_ge(sem("hso_ready"), 2)
            pool.dma_start(ssd_p, hso).then_inc(sem("hso_stored"), 16)
            with pool.Fori(0, 4) as i:
                pool.wait_ge(sem("lt_ready"), i + 1)
                for l in range(1, LV):
                    if l >= 2:
                        pool.wait_ge(sem("x_ps"), i * LV + (l - 1))
                        pool.wait_ge(sem("t_ready"), i * (2 * LV) + 1)
                    tt((Bm0, Bm1)[l % 2], LT, over(lvl[:, l, :], 4), ALU.mult).then_inc(sem("b_ready"), 1)
                pool.wait_ge(sem("gdn_free"), i + 2)
                pool.dma_start(gdn_p[:, bass.ds(i * 2, 2), :], S2).then_inc(sem("s2_stored"), 16)
                pool.wait_ge(sem("s2_stored"), i * 16 + 16)
                pool.sem_inc(sem("s2_free"), 1)
            def load_sst(j):
                pool.dma_start(sst[:, j % 2].rearrange("p (b t) n -> p b t n", b=2),
                               ssd_s_in[:, 2 * j:2 * j + 2]).then_inc(sem(f"ld_sst{j % 2}"), 16)

            load_sst(0)
            load_sst(1)
            pool.wait_ge(sem("bcs_ready"), 1)
            pool.dma_start(a["bc_dram"].rearrange("j b n -> b j n"),
                           bcs[0:8].rearrange("p (j n) -> p j n", j=4)).then_inc(sem("bc_out"), 16)
            pool.wait_ge(sem("bc_out"), 16)
            pool.dma_start(BC.rearrange("p j b n -> p (j b) n"),
                           a["bc_dram"].rearrange("j b n -> (j b) n").partition_broadcast(P)
                           ).then_inc(sem("ld_bc"), 16)
            for j in range(4):
                pool.wait_ge(sem("sst_ready"), j + 1)
                pool.dma_start(ssd_s_out[:, 2 * j:2 * j + 2], sst[:, j % 2].rearrange("p (b t) n -> p b t n", b=2)
                               ).then_inc(sem(f"sst_stored{j % 2}"), 16)
                if j < 2:
                    pool.wait_ge(sem(f"sst_stored{j}"), 16)
                    pool.wait_ge(sem("sst_used"), j + 1)
                    load_sst(j + 2)
            for j in range(2):
                pool.wait_ge(sem(f"sst_stored{j}"), 32)
            pool.wait_ge(sem("sst_done"), 1)
            for h in range(8):
                pool.dma_start(gst[:, 8 * h:8 * h + 8, :], gdn_s_in[:, h]).then_inc(sem("ld_gst"), 16)
            pool.wait_ge(sem("vrow_ready"), 1)
            pool.dma_start(a["v_dram"], vrow[0:64]).then_inc(sem("v_out"), 16)
            pool.wait_ge(sem("v_out"), 16)
            for j in range(2):
                if j:
                    pool.wait_ge(sem("gst_ready"), 1)
                pool.dma_start(gvb, a["v_dram"][32 * j:32 * j + 32, :].partition_broadcast(P)
                               ).then_inc(sem("ld_gvb"), 16)
            pool.wait_ge(sem("gst_ready"), 2)
            for h in range(8):
                pool.dma_start(gdn_s_out[:, h], gst[:, 8 * h:8 * h + 8, :]).then_inc(sem("gst_stored"), 16)
            pool.wait_ge(sem("x1_done"), N_OUT + SLOTS)
            pool.dma_start(a["x1_dram"], xT).then_inc(sem("x1_stored"), 16)
            pool.wait_ge(sem("gst_stored"), 128)
            pool.dma_start(sk, a["sub_keys"]).then_inc(sem("ld_sk"), 16)
            pool.wait_ge(sem("hso_stored"), 16)
            pool.wait_ge(sem("x1_stored"), 16)

            def gate_rows(n, b, t0):
                pool.wait_ge(sem("soh_ready"), n + 1)
                tt(Boh[:, b], over(Soh[:, b], 3, 2), over(gp[:, bass.ds(t0, GT), :], QE, 3), ALU.mult
                   ).then_inc(sem("boh_ready"), 1)

            pool.wait_ge(sem("tk_ready"), 6)
            pool.wait_ge(sem("gp_ready"), 1)
            with pool.Fori(0, EARLY // 2) as i:
                for b in range(2):
                    gate_rows(i * 2 + b, b, i * (2 * GT) + b * GT)
            pool.wait_ge(sem("gp_ready"), 3)
            with pool.Fori(EARLY // 2, NG // 2) as i:
                for b in range(2):
                    gate_rows(i * 2 + b, b, i * (2 * GT) + b * GT)
            for q in range(1, 4):
                with pool.Fori(0, NG // 2) as i:
                    for b in range(2):
                        gate_rows(i * 2 + (NG * q + b), b, i * (2 * GT) + b * GT)


def kernel(**inputs):
    import numpy as np
    import concourse.bacc as bacc
    from concourse.bass_utils import run_bass_kernel_spmd

    x = {k: np.asarray(v) for k, v in inputs.items()}
    f32 = np.float32

    def feat(v):
        return np.ascontiguousarray(v.reshape(v.shape[0], -1, P).transpose(2, 1, 0))

    def wtiles(w):
        return np.ascontiguousarray(w.reshape(KT, P, -1, P).transpose(2, 1, 0, 3))

    w_in = x["w_in"][0]
    z, xbc, dt, qkv, ar, br, gate = np.split(w_in, [1024, 2560, 2576, 5648, 5656, 5664], axis=1)
    conv_w = np.concatenate([x["gdn_conv_w"][0], x["ssd_conv_w"][0]], axis=1)
    cols = np.zeros((P, 2), f32)
    cols[0:24, 0] = np.concatenate([x["ssd_dt_bias"][0], x["gdn_dt_bias"][0]])
    cols[0:24, 1] = np.concatenate([x["ssd_A_log"][0], x["gdn_A_log"][0]])
    col = lambda v: v.reshape(-1, P).T
    params = np.concatenate([
        col(x["norm1_w"][0]), col(x["norm2_w"][0]), col(x["final_norm_w"]), col(x["b_ada"][0]),
        conv_w.reshape(4, CT, P).transpose(2, 1, 0).reshape(P, CT * 4),
        np.concatenate([np.zeros((P, 24), f32), col(x["ssd_conv_b"][0])], axis=1),
        col(np.repeat(x["ssd_D"][0], 64)), col(x["ssd_norm_w"][0]), col(x["gdn_norm_w"][0]), cols], axis=1)
    j, i = np.meshgrid(np.arange(P), np.arange(P), indexing="ij")
    levels = [((i // (2 * m) == j // (2 * m)) & (i // m % 2 == 1) & (j // m % 2 == 0)) for m in (1, 2, 4, 8, 16, 32, 64)]
    eps = np.zeros((P, 2), f32)
    eps[:, 0], eps[:, 1] = EPS, P * EPS
    consts = np.concatenate([np.eye(P), np.ones((P, P)), i >= j, i + 0.0] + levels + [eps, np.arange(P)[:, None] % 32 == np.arange(NC),
                             np.arange(P)[:, None] // TS == np.arange(8), np.arange(P)[:, None] % TS == np.arange(TS)],
                            axis=1).astype(f32)
    state = np.concatenate([x["state_gdn_conv"][0], x["state_ssd_conv"][0]], axis=2)
    u = x["peer_u"][0].reshape(P, P, KT, P)
    arrays = {
        "condT": feat(np.concatenate([x["c_prompt"], x["c_sample"]])),
        "xT": feat(np.concatenate([x["x_prompt"][0], x["x_sample"][:, 0]])),
        "consts": consts, "params": params,
        "w_ada": x["w_ada"][0].reshape(4, 4, P, 24, 512).transpose(3, 0, 2, 1, 4).reshape(96, P, KT, P),
        "w_small": np.concatenate([dt, ar, br], axis=1).reshape(KT, P, 32).transpose(1, 0, 2),
        "w_in": wtiles(np.concatenate([qkv, xbc, z, gate], axis=1)),
        "w_out": wtiles(x["w_out"][0]), "w_q": wtiles(x["peer_w_q"][0]),
        "conv_state": state.reshape(8, 3, CT, P).transpose(3, 2, 0, 1),
        "sub_keys": x["peer_sub_keys"][0].reshape(16, P, P).transpose(2, 0, 1),
        "peer_u": u.transpose(1, 3, 2, 0),
        "peer_v": x["peer_v"][0].reshape(P, 32, 4, 4, 512).transpose(1, 3, 0, 2, 4).reshape(P, P, KT, P),
        "state_ssd": x["state_ssd"][0], "state_gdn": x["state_gdn"][0],
    }
    outs = {"yT": (P, KT, T), "conv_out": (P, CT, 9, 3), "ssd_state_p": (HS, 64, 128), "gdn_state_p": (HG, P, P),
            "ssd_state_s": (TS, HS, 64, 128), "gdn_state_s": (TS, HG, P, P)}
    scratch = {"rows_dram": (32, TP), "smp_dram": (32, 24), "bc_dram": (4, TS, 128), "v_dram": (64, 128),
               "x1_dram": (P, KT, T)}
    nc = bacc.Bacc("TRN2", target_bir_lowering=False, num_devices=1, dynamic_dma_scratch_size=4096)
    arrays = {f"in_{k}": np.ascontiguousarray(v) for k, v in arrays.items()}
    a = {k[3:]: nc.dram_tensor(k, v.shape, F32, kind="ExternalInput").ap() for k, v in arrays.items()}
    for k, shape in scratch.items():
        a[k] = nc.dram_tensor(k, shape, F32, kind="Internal").ap()
    o = {k: nc.dram_tensor(f"out_{k}", shape, F32, kind="ExternalOutput").ap() for k, shape in outs.items()}
    build(nc, a, o)
    r = run_bass_kernel_spmd(nc, [arrays], core_ids=[0]).results[0]
    y = r["out_yT"].transpose(2, 1, 0).reshape(T, D)
    conv = r["out_conv_out"].transpose(2, 3, 1, 0).reshape(9, 3, CT * P)
    gdn_c, ssd_c = conv[:, :, 0:3072], conv[:, :, 3072:]
    c = np.ascontiguousarray
    return (c(y[None, 0:TP]), c(y[TP:, None]), r["out_ssd_state_p"][None, None], c(ssd_c[None, 0:1]),
            r["out_gdn_state_p"][None, None], c(gdn_c[None, 0:1]), r["out_ssd_state_s"][None], c(ssd_c[None, 1:]),
            r["out_gdn_state_s"][None], c(gdn_c[None, 1:]))
```

```python
from contextlib import ExitStack

import concourse.bass as bass
from concourse import mybir

ALU = mybir.AluOpType
ACT = mybir.ActivationFunctionType
F32 = mybir.dt.float32
F32R = mybir.dt.float32r
BF16 = mybir.dt.bfloat16
U32 = mybir.dt.uint32
SB = 56280
AX = mybir.AxisListType.X

P = 128
D = 2048
KT = D // P
TP, TS = 256, 8
T = TP + TS
NC = 9
CH = 128
HS, HG = 16, 8
CT = 36
TQ, TK, TV, TX, TB, TC = 0, 8, 16, 24, 32, 34
RAW = 3 + TP + 4 * TS
CV = RAW - 3
EPS = 1e-6
LV = 7
TOPK = 16
TILES = ((TP, TS), (0, P), (P, P))
GT = 11
NG = T // GT
EARLY = 8
QE = 32
GDN_STEPS = 12
SLOTS = 4
N_ADA1, N_CONV, N_GATE, N_ADA2, N_OUT, N_Q, N_U = 32, CT, 16, 64, 16, 16, 128
T_CONV = N_ADA1
T_GATE = T_CONV + N_CONV
T_ADA2 = T_GATE + N_GATE
T_OUT = T_ADA2 + N_ADA2
T_REST = T_ADA2 + 48
T_Q = T_OUT + N_OUT
T_U = T_Q + N_Q
L_OUT = N_CONV + N_GATE
L_Q = L_OUT + N_OUT
L_E = L_Q + N_Q


class Steps:

    def __init__(self, eng, sem):
        self.eng, self.sem, self.base, self.k = eng, sem, 0, 0

    def mark(self, ins):
        ins.then_inc(self.sem, 1)
        self.k += 1

    def settle(self):
        self.eng.wait_ge(self.sem, self.base + self.k)

    def link(self, ins):
        self.mark(ins)
        self.settle()

    def enter(self, i, per):
        self.out, self.per, self.k = self.base + self.k, per, 0
        self.base = i * per + self.out

    def leave(self, count):
        assert self.k == self.per, (self.k, self.per)
        self.base, self.k = self.out + count * self.per, 0


def build(nc, a, o):
    with ExitStack() as ctx:
        sem_of = {}

        def sem(name):
            if name not in sem_of:
                sem_of[name] = ctx.enter_context(nc.semaphore(name))
            return sem_of[name]

        ps = ctx.enter_context(nc.psum_tensor("ps", [P, 8, 512], F32))
        left = [0]
        at = (nc.sbuf_base + 31) // 32 * 32
        placed = [0]

        def view(off, *dims, parts=P, of=F32):
            n = 1
            for d in dims:
                n *= d
            assert off + (n if of is not BF16 else n // 2) <= SB, (off, n)
            placed[0] += 1
            v = nc.alloc_sbuf_tensor_at(f"sb{placed[0]}", [parts, n], of, offset=at + 4 * off, align_bytes=8)[:, :]
            if len(dims) == 2:
                v = v.rearrange("p (a b) -> p a b", b=dims[1])
            elif len(dims) == 3:
                v = v.rearrange("p (a b c) -> p a b c", b=dims[1], c=dims[2])
            elif len(dims) == 4:
                v = v.rearrange("p (a b c d) -> p a b c d", b=dims[1], c=dims[2], d=dims[3])
            return v

        def take(*dims, parts=P):
            n = 1
            for d in dims:
                n *= d
            off = left[0]
            left[0] += n + (n % 2)
            return view(off, *dims, parts=parts)

        def take_r(*dims):
            off = left[0]
            n = 1
            for d in dims:
                n *= d
            left[0] += n
            v = view(off, *dims, of=F32R)
            return v, v.bitcast(F32)

        def take_b(*dims):
            n = 1
            for d in dims:
                n *= d
            off = left[0]
            left[0] += (n + 3) // 4 * 2
            return view(off, *dims, of=BF16)

        wring = take(SLOTS, KT, P)
        hT = take(KT, T)
        mod = take(96, NC)
        n_const = a["consts"].shape[1]
        cst = take(n_const)
        sel = cst[:, 512 + LV * 128 + 2:512 + LV * 128 + 2 + NC]
        ident, ones, tri = cst[:, 0:128], cst[:, 128:256], cst[:, 256:384]
        iota = cst[:, 384:512]
        lvl = cst[:, 512:512 + LV * 128].rearrange("p (l i) -> p l i", l=LV)
        epsc = cst[:, 512 + LV * 128:512 + LV * 128 + 2]
        of_head, of_token = cst[:, n_const - 16:n_const - 8], cst[:, n_const - 8:n_const]
        n_par = a["params"].shape[1]
        par = take(n_par)
        po = [0]

        def pview(n):
            v = par[:, po[0]:po[0] + n]
            po[0] += n
            return v

        n1w, n2w, fnw, bada = pview(16), pview(16), pview(16), pview(96)
        convw = pview(CT * 4)
        convb, dcol, ynw, onw = pview(CT), pview(8), pview(8), pview(1)
        rbias, ralog = pview(1)[0:32], pview(1)[0:32]
        sqb_off = left[0]
        sqb = take(4, T)
        nrm = take(2, T)
        xT_off = left[0]
        xT = take(KT, T)
        TKB = (6, 0, 4)

        cv_off = left[0]
        cv = take(CT, T)
        zg_off = left[0]
        zg = take(16, T)
        br_off = left[0]
        BR = take(32, TP)
        tmp_off = left[0]
        hT_off = SLOTS * KT * P
        left[0] = tmp_off
        raw, cac = take(4, RAW), take(4, CV)
        cso, csi = take(CT, 9, 3), take(CT, 8, 3)
        left[0] = zg_off
        wsm = take(KT, 32)
        cT = take(KT, NC)
        xbr, abr, polyr, z1r, z2r = (take(T, parts=32) for _ in range(5))
        rbias2 = take(2, parts=32)
        left[0] = br_off
        whi, whi_f = take_r(2, KT, P)
        wlo, _ = take_r(2, KT, P)
        left[0] = tmp_off + 6700
        sgr = take(T, parts=32)
        smp = take(24, parts=32)
        tok = take(6, 32)
        cst2 = take(2, 32)
        Wt = take(2, 24)
        LE1 = take(24)
        wf0 = take(24)
        nbe = take(8)
        sT = take(KT, 32)
        gtmp = take(SLOTS, TS)
        spr, dAr = take(T, parts=32), take(T, parts=32)
        csr = take(TP, parts=32)
        hTl = view(hT_off, KT, T, of=F32R)
        mixl = view(left[0], KT, T, of=F32R)
        tail_off = left[0]
        SR = view(left[0], 32, 3, TS)
        adasb = view(left[0] + 768, 512)
        h1h, h1h_f = take_r(KT, T)
        mixh = view(zg_off, KT, T, of=F32R)
        mixh_f = mixh.bitcast(F32)
        assert left[0] <= SB, left[0]

        left[0] = hT_off
        xdt, xwf = take(2, 1024), take(2, 1024)
        left[0] = tmp_off
        xw0, Bt = take(16, 64), take(2, 256)
        h1T, cbm = take(1024), take(4, 128)
        Mb = take(16, 128)
        assert left[0] <= tmp_off + 6700
        hso = take(8, 128)
        assert left[0] <= tmp_off + 6700, left[0] - tmp_off

        left[0] = hT_off
        kf, vf, kb, Dm, LT, QK, Tm, Tt = (take(4, 128) for _ in range(8))
        left[0] = tmp_off
        Xb, Bm0, Bm1, Rv, kd, VN = (take(4, 128) for _ in range(6))
        S1, S2, qg = take(2, 128), take(2, 128), take(2, 128)
        sst = take(2, 8 * 128)
        assert left[0] <= tmp_off + 6700
        left[0] = tail_off + 1280
        stm = take(8 * 128)
        BC = take(2, 4 * 128)
        Esel, XD, dtsel, ysm = take(8, TS), take(8, TS), take(8, TS), take(TS, 8)
        bcs = view(tail_off + 1280, 4 * 128, parts=8)
        assert left[0] <= SB

        left[0] = hT_off
        gst1 = take(32, 128)
        assert left[0] <= hT_off + KT * T
        left[0] = tmp_off
        gst0 = take(32, 128)
        gst = (gst0, gst1)
        kq, qkp = take(64, 2), take(64)
        vn, ksm, vsm = take(64), take(64), take(64)
        vrow = take(128, parts=64)
        assert left[0] <= tmp_off + 6700
        gvb = view(cv_off + TV * T, 16, 128)

        left[0] = xT_off
        G = take(2 * QE, T)
        g_end = left[0]
        Boh = take_b(2, GT, 3, QE)
        assert left[0] == br_off
        left[0] = br_off + 4 * KT * P
        Aoh, Soh = take_b(2, GT, 128), take_b(2, GT, QE)
        acc = take(KT, T)
        hTh, hTh_f = take_r(KT, T)
        small_off = left[0]
        chi, chi_f = take_r(SLOTS, T)
        clo, _ = take_r(SLOTS, T)
        craw = view(sqb_off, 2, T)
        i1T, i2T = take(T), take(T)
        gp = take_b(T, 3)
        assert left[0] <= SB, left[0]
        Qs = view(xT_off, 16, 128)
        left[0] = xT_off + QE * T
        sk = take(16, 128)
        work = take(2048)
        cand = take(8, 256)
        oh = take(128, 16)
        assert left[0] <= g_end
        left[0] = small_off
        sv, sif = take(16, 16), take(16, 16)
        siu = take(16, 16).bitcast(U32)
        cvv = take(8, 16)
        ciu, rcu = take(8, 16).bitcast(U32), take(8, 16).bitcast(U32)
        rcf = take(8, 16)
        gsum = take(8)
        tkI1, tkI2, tkG = take(128), take(128), take(128)
        gT = take(T)
        sv_s, siu_s = take(6, 16), take(1, 16).bitcast(U32)
        assert left[0] <= small_off + 2 * SLOTS * T
        left[0] = sqb_off
        sv_2, siu_2 = take(16, 16), take(16, 16).bitcast(U32)
        qst = take(SLOTS, TP)
        assert left[0] <= xT_off
        qT = acc

        block = ctx.enter_context(nc.Block())

        ssd_p = o["ssd_state_p"].rearrange("(t q) d n -> (q d) t n", q=2)
        ssd_s_in = a["state_ssd"].rearrange("b (t q) d n -> (q d) b t n", q=2)
        ssd_s_out = o["ssd_state_s"].rearrange("b (t q) d n -> (q d) b t n", q=2)
        gdn_s_in = a["state_gdn"].rearrange("b h k v -> k h b v")
        gdn_s_out = o["gdn_state_s"].rearrange("b h k v -> k h b v")
        gdn_p = o["gdn_state_p"].rearrange("h k v -> k h v")

        @block.sync
        def _(sp):
            landed = [sem(f"w_landed{s}") for s in range(SLOTS)]
            gemm_done = sem("gemm_done")

            lo_ready = sem("lo_ready")
            sp.dma_start(cT, a["condT"]).then_inc(sem("ld_cond"), 16)

            def tiles(src, free, n0, count, t0=0, first=0):
                with sp.Fori(first, count // SLOTS) as i:
                    for s in range(SLOTS):
                        sp.wait_ge(free, i * SLOTS + (n0 + s - SLOTS + 1))
                        sp.dma_start(wring[:, s, :, :], src[i * SLOTS + (t0 + s)]).then_inc(landed[s], 16)

            def four(src, free, n0, t0=0):
                for s in range(SLOTS):
                    sp.wait_ge(free, n0 + s - SLOTS + 1)
                    sp.dma_start(wring[:, s, :, :], src[t0 + s]).then_inc(landed[s], 16)

            for s in range(SLOTS):
                sp.dma_start(wring[:, s, :, :], a["w_ada"][s]).then_inc(landed[s], 16)
                if s == 0:
                    sp.dma_start(cst, a["consts"]).then_inc(sem("ld_const"), 16)
                    sp.dma_start(par, a["params"]).then_inc(sem("ld_par"), 16)
                if s == 1:
                    sp.dma_start(xT, a["xT"]).then_inc(sem("ld_x"), 16)
                if s == 2:
                    sp.dma_start(wsm, a["w_small"]).then_inc(sem("ld_wsm"), 16)
                    sp.dma_start(csi, a["conv_state"]).then_inc(sem("ld_csi"), 16)
            tiles(a["w_ada"], gemm_done, 0, N_ADA1, first=1)
            four(a["w_in"], gemm_done, T_CONV)
            tiles(a["w_in"], lo_ready, 0, N_CONV + N_GATE, first=1)
            four(a["w_ada"], lo_ready, L_OUT, t0=N_ADA1)
            tiles(a["w_ada"], gemm_done, T_ADA2, N_ADA2, t0=N_ADA1, first=1)
            four(a["w_out"], gemm_done, T_OUT)
            tiles(a["w_out"], lo_ready, L_OUT, N_OUT, first=1)
            tiles(a["w_q"], lo_ready, L_Q, N_Q)

            with sp.Fori(0, N_U // SLOTS) as i:
                for half, src in enumerate((a["peer_u"], a["peer_v"])):
                    for s in range(SLOTS):
                        sp.wait_ge(lo_ready, i * (2 * SLOTS) + (L_E + SLOTS * half + s - SLOTS + 1))
                        sp.dma_start(wring[:, s, :, :], src[i * SLOTS + s]).then_inc(landed[s], 16)
            sp.wait_ge(sem("coef_ready"), N_U + 2)
            sp.wait_ge(sem("x1_stored"), 16)
            sp.dma_start(xT, a["x1_dram"]).then_inc(sem("x1_back"), 16)
            for j in range(0, KT, 4):
                sp.wait_ge(sem("y_ready"), j // 4 + 1)
                sp.dma_start(o["yT"][:, j:j + 4], hT[:, j:j + 4]).then_inc(sem("y_stored"), 16)
            sp.wait_ge(sem("y_stored"), 64)

        @block.tensor
        def _(pe):
            landed = [sem(f"w_landed{s}") for s in range(SLOTS)]
            gemm_done = sem("gemm_done")
            sq_n = [0]
            norms = [0]

            def mm(out, l, r, start=True, stop=True):
                return pe.matmul(out, l, r, start=start, stop=stop)

            def tr(out, in_):
                return pe.transpose(out, in_, ident[0:in_.shape[0], 0:in_.shape[0]])

            def tile(out, b, n, high, low):
                pe.wait_ge(sem("hi_ready"), n + 1)
                for k in range(KT):
                    mm(out, whi[:, b, k, :], high[:, k, :], k == 0, False)
                    mm(out, whi[:, b, k, :], low[:, k, :], False, False)
                pe.wait_ge(sem("lo_ready"), n + 1)
                for k in range(KT):
                    last = mm(out, wlo[:, b, k, :], high[:, k, :], False, k == KT - 1)
                last.then_inc(gemm_done, 1)

            def norm(count, bank=4):
                k = norms[0]
                norms[0] += 1
                if k >= 2:
                    pe.wait_ge(sem("norm_sqrt"), k - 1)
                for j in range(count):
                    n = sq_n[0]
                    sq_n[0] += 1
                    pe.wait_ge(sem("sq_ready"), n + 1)
                    mm(ps[:, bank + k % 2, 0:T], ones, sqb[:, n % 4, :], j == 0, j == count - 1
                       ).then_inc(sem("sq_used"), 1)

            pe.sem_inc(sem("v_done"), 1)
            pe.sem_inc(sem("g_ps"), 2)
            pe.wait_ge(sem("cond_ready"), 1)
            pe.wait_ge(sem("ld_const"), 16)

            def ada_part(s):
                for j in range(4):
                    last = pe.matmul(ps[32 * j:32 * j + 32, 6, :], sT[:, 4 * s + j, :],
                                     wring[:, s, :, :].rearrange("p (k c) n -> p k (c n)", k=4)[:, j, :],
                                     start=s == 0, stop=s == SLOTS - 1, tile_position=(0, 32 * j))
                last.then_inc(gemm_done, 1)

            def ada_turn(n, col):
                pe.wait_ge(sem("ada_sb"), n)
                for j in range(4):
                    last = mm(ps[:, 7, bass.ds(col + j * NC, NC)], adasb[:, j * P:(j + 1) * P], sel)
                last.then_inc(sem("ada_ps"), 1)

            def ada_first(first, last):
                with pe.Fori(first, last) as i:
                    for s in range(SLOTS):
                        pe.wait_ge(landed[s], i * 16 + 16)
                        ada_part(s)
                    ada_turn(i + 1, i * (SLOTS * NC))

            ada_first(0, 4)
            norm(KT)
            ada_first(4, N_ADA1 // SLOTS)
            pe.wait_ge(sem("h_ready"), 4)
            pe.wait_ge(sem("ld_wsm"), 16)
            for k in range(KT):
                last = mm(ps[0:32, 6, 0:T], wsm[:, k, :], hT[:, k, :], k == 0, k == KT - 1)
            last.then_inc(sem("small_done"), 1)
            pe.wait_ge(sem("hl_ready"), 4)
            with pe.Fori(0, N_CONV // SLOTS) as i:
                for s in range(SLOTS):
                    pe.wait_ge(sem("raw_ready"), i * (3 * SLOTS) + 3 * (s + 1))
                    tile(ps[:, s, 0:T], s % 2, i * SLOTS + s, h1h, hTl)
            pe.wait_ge(sem("raw_ready"), 3 * (N_CONV + SLOTS))
            with pe.Fori(0, N_GATE // SLOTS) as i:
                for s in range(SLOTS):
                    pe.wait_ge(sem("zg_ready"), i * SLOTS + s + 1)
                    tile(ps[:, s, 0:T], s % 2, i * SLOTS + (N_CONV + s), h1h, hTl)
                    pe.wait_ge(sem("norm_sqrt"), i * SLOTS + (s + 1))
                    pe.wait_ge(sem("sq_ready"), i * SLOTS + (KT + s + 1))
                    mm(ps[:, 4 + (s + 1) % 2, 0:T], ones, sqb[:, s, :]).then_inc(sem("sq_used"), 1)
            norms[0] += N_GATE
            sq_n[0] += N_GATE
            pe.wait_ge(sem("small_rows"), 1)
            for j, row in enumerate((dAr, spr, sgr)):
                for c in range(2):
                    last = tr(ps[:, 6, (2 * j + c) * 32:(2 * j + c + 1) * 32], row[:, c * CH:(c + 1) * CH])
            last.then_inc(sem("tok_ps"), 1)
            pe.wait_ge(sem("tok_ready"), 1)
            for c in range(2):
                mm(ps[0:32, 7, c * CH:(c + 1) * CH], tok[:, c, :], tri)
                last = mm(ps[:, 7, 256 + 32 * c:288 + 32 * c], tri, tok[:, c, :])
            last.then_inc(sem("cs_ps"), 1)
            pe.wait_ge(sem("zg_ready"), N_GATE + SLOTS)
            pe.wait_ge(sem("cv_ready"), 2 * CT + 8)
            for c in range(2):
                for j in range(8):
                    tr(ps[:, 2 * c + j // 4, (j % 4) * 128:(j % 4 + 1) * 128], cv[:, TX + j, c * CH:(c + 1) * CH]
                       ).then_inc(sem("xt_ps"), 1)
            pe.wait_ge(sem("cs_ready"), 1)
            for c in range(2):
                for g in range(2):
                    last = tr(ps[:, 7, (2 * c + g) * 128:(2 * c + g + 1) * 128], cv[:, TB + g, c * CH:(c + 1) * CH])
            last.then_inc(sem("bt_ps"), 1)
            for c in range(2):
                for g in range(2):
                    s = slice(c * CH, (c + 1) * CH)
                    last = mm(ps[:, 6, (2 * c + g) * 128:(2 * c + g + 1) * 128], cv[:, TB + g, s], cv[:, TC + g, s])
            last.then_inc(sem("cb_ps"), 1)
            pe.wait_ge(sem("bt_ready"), 1)
            pe.wait_ge(sem("xw_ready"), 1)
            for g in range(2):
                last = mm(ps[:, g, :], Bt[:, 0, g * 128:(g + 1) * 128],
                          xw0[:, g * 8:(g + 1) * 8, :])
            last.then_inc(sem("h1_ps"), 1)
            pe.wait_ge(sem("xw_ready"), 3)
            for hp in range(8):
                for c in range(2):
                    last = mm(ps[:, 2 + hp // 4, (hp % 4) * 128:(hp % 4 + 1) * 128],
                              xwf[:, c, hp * 128:(hp + 1) * 128], Bt[:, c, (hp // 4) * 128:(hp // 4 + 1) * 128],
                              c == 0, c == 1)
            last.then_inc(sem("hf_ps"), 1)
            pe.wait_ge(sem("norm_sqrt"), 17)
            pe.wait_ge(sem("h1_ready"), 1)
            for c in range(2):
                pe.wait_ge(sem("m_ready"), c + 1)
                if c == 1:
                    pe.wait_ge(sem("y_evac"), 8)
                for h in range(HS):
                    hp, q = h // 2, h % 2
                    out = ps[64 * q:64 * q + 64, 4 + hp // 4, (hp % 4) * 128:(hp % 4 + 1) * 128]
                    last = pe.matmul(out, xdt[:, c, h * 64:(h + 1) * 64], Mb[:, h, :], start=True, stop=c == 0,
                                     skip_group_check=True)
                    if c == 0:
                        if h % 2:
                            last.then_inc(sem("y_ps"), 1)
                if c == 1:
                    last.then_inc(sem("m_used"), 1)
            pe.wait_ge(sem("ce_ready"), 1)
            for h in range(HS):
                hp, q = h // 2, h % 2
                out = ps[64 * q:64 * q + 64, 6 + hp // 4, (hp % 4) * 128:(hp % 4 + 1) * 128]
                last = pe.matmul(out, h1T[:, h * 64:(h + 1) * 64], Mb[:, h, :], start=True, stop=True,
                                 skip_group_check=True)
                if h % 2:
                    last.then_inc(sem("y_ps"), 1)

            pe.wait_ge(sem("y_evac"), 24)
            for j in range(4):
                tr(ps[0:8, 0, j * 128:(j + 1) * 128], cv[:, TB + j, TP:T]).then_inc(sem("bc_ps"), 1)

            def ada(i, j):
                s, n = j % SLOTS, j // SLOTS
                pe.wait_ge(landed[s], i * 48 + (T_ADA2 // SLOTS * 16 + 16 * n + 16))
                if s == 0 and n:
                    ada_turn(i * 3 + (N_ADA1 // SLOTS + n), (n - 1) * (SLOTS * NC))
                ada_part(s)

            pe.wait_ge(sem("bcs_ready"), 1)
            pe.wait_ge(sem("y_evac"), 24)
            pe.wait_ge(sem("hso_ready"), 2)
            with pe.Fori(0, 4) as i:
                pe.wait_ge(sem("kf_ready"), i * 2 + 2)
                pe.wait_ge(sem("kb_ready"), i + 1)
                pe.wait_ge(sem("gdn_free"), i + 1)
                for p in range(4):
                    h, c = p // 2, p % 2
                    mm(ps[:, 0, p * 128:(p + 1) * 128], kf[:, p, :], kb[:, p, :])
                for p in range(4):
                    last = mm(ps[:, 1, p * 128:(p + 1) * 128], kf[:, p, :],
                              cv[:, i * 2 + (TQ + p // 2), (p % 2) * CH:(p % 2 + 1) * CH])
                last.then_inc(sem("kk_ps"), 1)
                for p in range(4):
                    last = tr(ps[:, 2, p * 128:(p + 1) * 128], vf[:, p, :])
                last.then_inc(sem("vt_ps"), 1)
                for p in range(4):
                    last = tr(ps[:, 3, p * 128:(p + 1) * 128], kf[:, p, :])
                last.then_inc(sem("kt_ps"), 1)
                ada(i, 0)
                pe.wait_ge(sem("lt_ready"), i + 1)
                for p in range(4):
                    last = tr(ps[:, 0, p * 128:(p + 1) * 128], Bm0[:, p, :])
                last.then_inc(sem("x_ps"), 1)
                ada(i, 1)
                for l in range(1, LV):
                    Bm = (Bm0, Bm1)[l % 2]
                    pe.wait_ge(sem("b_ready"), i * (LV - 1) + l)
                    pe.wait_ge(sem("t_ready"), i * (2 * LV) + (2 if l == 1 else 2 * l - 1))
                    for p in range(4):
                        last = mm(ps[:, 0, p * 128:(p + 1) * 128], Bm[:, p, :], Tm[:, p, :])
                    last.then_inc(sem("x_ps"), 1)
                    ada(i, (0, 2, 4, 5, 7, 8, 10)[l])
                    pe.wait_ge(sem("x_ready"), i * (LV - 1) + l)
                    pe.wait_ge(sem("t_ready"), i * (2 * LV) + 2 * l)
                    if l < LV - 1:
                        for p in range(4):
                            last = mm(ps[:, 4, p * 128:(p + 1) * 128], Tt[:, p, :], Xb[:, p, :])
                        last.then_inc(sem("tm_ps"), 1)
                    for p in range(4):
                        last = mm(ps[:, 1, p * 128:(p + 1) * 128], Xb[:, p, :], Tt[:, p, :])
                    last.then_inc(sem("tt_ps"), 1)
                    if l % 2:
                        ada(i, (0, 3, 0, 6, 0, 9)[l])
                pe.wait_ge(sem("t_ready"), i * (2 * LV) + 2 * LV)
                pe.wait_ge(sem("rv_ready"), i * 2 + 1)
                for h in range(2):
                    last = mm(ps[:, 0, h * 128:(h + 1) * 128], Tt[:, 2 * h, :], Rv[:, 2 * h, :])
                last.then_inc(sem("vn_ps"), 1)
                ada(i, 11)
                ada_turn(i * 3 + (N_ADA1 // SLOTS + 3), 2 * SLOTS * NC)
                pe.wait_ge(sem("vn_ready"), i * 2 + 1)
                for h in range(2):
                    last = mm(ps[:, 1, h * 128:(h + 1) * 128], kd[:, 2 * h, :], VN[:, 2 * h, :])
                last.then_inc(sem("s_ps"), 1)
                for h in range(2):
                    mm(ps[:, 5, (2 * h) * 128:(2 * h + 1) * 128], VN[:, 2 * h, :], QK[:, 2 * h, :])
                pe.wait_ge(sem("s_ready"), i + 1)
                for h in range(2):
                    last = mm(ps[:, 0, 256 + h * 128:256 + (h + 1) * 128], kf[:, 2 * h + 1, :], S1[:, h, :])
                last.then_inc(sem("ks_ps"), 1)
                pe.wait_ge(sem("rv_ready"), i * 2 + 2)
                for h in range(2):
                    last = mm(ps[:, 0, h * 128:(h + 1) * 128], Tt[:, 2 * h + 1, :], Rv[:, 2 * h + 1, :])
                last.then_inc(sem("vn_ps"), 1)
                pe.wait_ge(sem("vn_ready"), i * 2 + 2)
                for h in range(2):
                    out = ps[:, 5, (2 * h + 1) * 128:(2 * h + 2) * 128]
                    mm(out, S1[:, h, :], qg[:, h, :], True, False)
                    last = mm(out, VN[:, 2 * h + 1, :], QK[:, 2 * h + 1, :], False, True)
                last.then_inc(sem("o_ps"), 1)
                for h in range(2):
                    last = mm(ps[:, 1, h * 128:(h + 1) * 128], kd[:, 2 * h + 1, :], VN[:, 2 * h + 1, :])
                last.then_inc(sem("s_ps"), 1)

            def ada_rest(g):
                for s in range(SLOTS):
                    pe.wait_ge(landed[s], 16 * (T_REST // SLOTS + g + 1))
                    ada_part(s)
                ada_turn((T_REST - T_ADA2 + N_ADA1) // SLOTS + g + 1, g * SLOTS * NC)

            pe.wait_ge(sem("gdn_free"), 5)
            ada_rest(0)
            norm(4)
            norm(4)
            pe.wait_ge(sem("qkp_ready"), 1)
            mm(ps[:, 1, 0:64], ones, qkp).then_inc(sem("qk_ps"), 1)
            pe.wait_ge(sem("kq_ready"), 1)
            pe.wait_ge(sem("ld_gst"), 128)
            for j in range(64):
                if j == 32:
                    ada_rest(1)
                last = mm(ps[:, 2, 2 * j:2 * j + 2], gst[j // 32][:, j % 32, :], kq[:, j, :])
            last.then_inc(sem("skq_ps"), 1)
            pe.wait_ge(sem("vns_ready"), 1)
            tr(ps[0:64, 3, 0:128], vn).then_inc(sem("vrow_ps"), 1)
            for half in range(2):
                for h in range(4):
                    norm(1)
                ada_rest(2 + half)

            pe.wait_ge(sem("mixl_ready"), 2)
            with pe.Fori(0, N_OUT // SLOTS) as i:
                for s in range(SLOTS):
                    pe.wait_ge(sem("x1_done"), i * SLOTS + s + 1)
                    tile(ps[:, s, 0:T], s % 2, i * SLOTS + (L_OUT + s), mixh, mixl)
            norm(KT)
            def scores(i, s):
                pe.wait_ge(sem("q_staged"), i * SLOTS + s + 1)
                pe.wait_ge(sem("score_used"), i * SLOTS + s + 1)
                for half in range(2):
                    last = mm(ps[:, 4 + s, half * P:(half + 1) * P],
                              qst[:, s, half * P:(half + 1) * P],
                              sk[:, bass.ds(i * SLOTS + s, 1), :].rearrange("p o t -> p (o t)"))
                last.then_inc(sem("score_ps"), 1)

            pe.sem_inc(sem("score_ps"), SLOTS)
            pe.wait_ge(sem("ld_sk"), 16)
            pe.wait_ge(sem("norm_sqrt"), norms[0])
            pe.wait_ge(sem("hl_ready"), 8)
            with pe.Fori(0, N_Q // SLOTS) as i:
                for s in range(SLOTS):
                    pe.wait_ge(sem("q_ready"), i * SLOTS + s + 1)
                    tile(ps[:, s, 0:T], s % 2, i * SLOTS + (L_Q + s), hTh, hTl)
                    if s:
                        scores(i, s - 1)
                scores(i, 3)
            pe.wait_ge(sem("qs_ready"), 1)
            pe.wait_ge(sem("score_used"), N_Q + SLOTS)
            for j in range(16):
                last = mm(ps[:, 4, 0:128], Qs[:, j, :], sk[:, j, :], j == 0, j == 15)
            last.then_inc(sem("score_ps"), 1)

            pe.wait_ge(sem("pair_ready"), 1)
            for side in range(2):
                last = mm(ps[0:64, 5, side * 32:side * 32 + 32], ident[:, side * 64:side * 64 + 64],
                          sv_s[:, 0:2, :].rearrange("p a k -> p (a k)"))
            last.then_inc(sem("pair_ps"), 1)
            pe.wait_ge(sem("top_done"), 1)
            for j in range(3):
                last = mm(ps[:, TKB[0], j * 128:j * 128 + TS],
                          oh[0:64, 8 * j:8 * j + 8, :].rearrange("p h k -> p (h k)"), of_token[0:64])
            last.then_inc(sem("tk_ps"), 1)

            def turn(t):
                n = TILES[t][1]
                pe.wait_ge(sem("top_done"), t + 1)
                for j, v in enumerate((tkI1, tkI2, tkG)):
                    last = tr(ps[:, TKB[t], j * 128:j * 128 + n], v[0:n, :])
                last.then_inc(sem("tk_ps"), 1)

            def gate_group(n, b, bank):
                pe.wait_ge(sem("aoh_ready"), n + 1)
                pe.wait_ge(sem("boh_ready"), n + 1)
                pe.wait_ge(sem("g_copied"), n + 1)
                for j in range(GT):
                    for part in range(3):
                        last = mm(ps[:, bank + b, j * QE:(j + 1) * QE], Aoh[:, b, j, :], Boh[:, b, j, part, :],
                                  part == 0, part == 2)
                last.then_inc(sem("g_ps"), 1)

            turn(1)
            with pe.Fori(0, EARLY // 2) as i:
                for b in range(2):
                    gate_group(i * 2 + b, b, 2)
            turn(2)
            with pe.Fori(EARLY // 2, NG // 2) as i:
                for b in range(2):
                    gate_group(i * 2 + b, b, 2)
            pe.wait_ge(sem("g_copied"), NG + 2)

            def expert_step(i, gates, g0):
                for s in range(SLOTS):
                    pe.wait_ge(sem("gelu_done"), i * SLOTS + s + 1)
                    tile(ps[:, s % 2, 0:T], s % 2, i * (2 * SLOTS) + (L_E + s), hTh, hTl)
                    if gates and s:
                        gate_group(g0 + gates[s - 1], gates[s - 1] % 2, 6)
                for q in range(4):
                    b, m = q % 2, i * (2 * SLOTS) + (L_E + SLOTS + q)
                    pe.wait_ge(sem("hi_ready"), m + 1)
                    for e in range(SLOTS):
                        if q == 0:
                            pe.wait_ge(sem("coef_ready"), i * SLOTS + (e + 3))
                        for d in range(4):
                            if e == 0:
                                pe.wait_ge(sem("v_added"), i * KT + (4 * q + d + 1))
                            mm(ps[:, 2 + d, 0:T], whi[:, b, 4 * e + d, :], chi[:, e, :], e == 0, False)
                            mm(ps[:, 2 + d, 0:T], whi[:, b, 4 * e + d, :], clo[:, e, :], False, False)
                    pe.wait_ge(sem("lo_ready"), m + 1)
                    for d in range(4):
                        for e in range(SLOTS):
                            last = mm(ps[:, 2 + d, 0:T], wlo[:, b, 4 * e + d, :], chi[:, e, :], False, e == SLOTS - 1)
                        last.then_inc(sem("v_done"), 1)

            with pe.Fori(0, 12) as i2:
                expert_step(i2 * 2, (0, 1, 2), i2 * 6 + NG)
                expert_step(i2 * 2 + 1, (3, 4, 5), i2 * 6 + NG)
            with pe.Fori(24, 32) as i:
                expert_step(i, None, None)
            pe.wait_ge(sem("gelu_done"), N_U + 2)
            norm(KT, bank=0)

        @block.scalar
        def _(act):
            gemm_done = sem("gemm_done")
            sq_n = [0]
            norms = [0]
            s_act = Steps(act, sem("act_steps"))

            def square(src):
                n = sq_n[0]
                sq_n[0] += 1
                if n >= 4:
                    act.wait_ge(sem("sq_used"), n - 3)
                act.activation(sqb[:, n % 4, :], src, ACT.Square).then_inc(sem("sq_ready"), 1)

            def root(scale, bias, bank=4):
                k = norms[0]
                norms[0] += 1
                act.wait_ge(sem("sq_used"), root_at.pop(0))
                if k >= 2:
                    act.wait_ge(sem("norm_free"), k - 1)
                act.activation(nrm[:, k % 2, :], ps[:, bank + k % 2, 0:T], ACT.Sqrt, scale=scale, bias=bias
                               ).then_inc(sem("norm_sqrt"), 1)

            root_at = []

            def squares(srcs):
                for x in srcs:
                    square(x)
                root_at.append(sq_n[0])

            act.sem_inc(sem("raw_ready"), 3 * SLOTS)
            act.sem_inc(sem("zg_ready"), SLOTS)
            act.sem_inc(sem("q_ready"), SLOTS)
            act.sem_inc(sem("gelu_done"), 2)
            act.sem_inc(sem("g_copied"), 2)
            act.sem_inc(sem("cv_ready"), 8)
            act.sem_inc(sem("gdn_free"), 1)
            act.wait_ge(sem("ld_cond"), 16)
            act.wait_ge(sem("s_zero"), 1)
            act.activation(sT[:, :, 0:NC], cT, ACT.Silu).then_inc(sem("cond_ready"), 1)

            def ada_first(first, last):
                with act.Fori(first, last) as i:
                    act.wait_ge(gemm_done, i * SLOTS + SLOTS)
                    act.copy(adasb, ps[:, 6, :]).then_inc(sem("ada_sb"), 1)

            ada_first(0, 4)
            act.wait_ge(sem("ld_const"), 16)
            act.wait_ge(sem("ld_x"), 16)
            squares([xT[:, k, :] for k in range(KT)])
            root(1.0 / D, epsc[:, 0:1])
            ada_first(4, N_ADA1 // SLOTS)
            act.wait_ge(sem("small_done"), 1)
            act.wait_ge(sem("abs_ready"), 1)
            act.activation(sgr, ps[0:32, 6, 0:T], ACT.Sigmoid).then_inc(sem("sg_ready"), 1)
            act.wait_ge(sem("ld_par"), 16)
            act.activation(rbias2[:, 0:1], ralog, ACT.Exp).then_inc(sem("sg_ready"), 1)
            act.wait_ge(sem("abs_ready"), 1)
            act.activation(abr, abr, ACT.Exp, scale=-1.0).then_inc(sem("exp_ready"), 1)
            act.wait_ge(sem("ld_csi"), 16)
            act.wait_ge(sem("raw_zero"), 1)

            def high(slot, lands, done):
                if done is not None:
                    act.wait_ge(gemm_done, done)
                act.wait_ge(sem(f"w_landed{slot}"), lands)
                act.copy(whi[:, slot % 2], wring[:, slot]).then_inc(sem("hi_ready"), 1)

            def high_h(k, dst):
                for j in range(0, KT, 4):
                    act.wait_ge(sem("h_ready"), 4 * k + j // 4 + 1)
                    act.copy(dst[:, j:j + 4], hT[:, j:j + 4]).then_inc(sem("hth_ready"), 1)

            def high_after(i, s, t0):
                high((s + 2) % SLOTS, i * 16 + (t0 // SLOTS * 16 + 16 + 16 * ((s + 2) // SLOTS)), None)

            high_h(0, h1h)
            for s in range(2):
                high(s, T_CONV // SLOTS * 16 + 16, None)
            with act.Fori(0, N_CONV // SLOTS) as i:
                for s in range(SLOTS):
                    samp = raw[:, s, 3 + TP:RAW].rearrange("p (b w) -> p b w", w=4)
                    act.wait_ge(gemm_done, i * SLOTS + (T_CONV + s + 1))
                    act.copy(raw[:, s, 3:3 + TP], ps[:, s, 0:TP]).then_inc(sem("raw_ready"), 1)
                    act.copy(samp[:, :, 3], ps[:, s, TP:T]).then_inc(sem("raw_ready"), 1)
                    act.copy(samp[:, :, 0:3], csi[:, i * SLOTS + s, :, :]).then_inc(sem("raw_ready"), 1)
                    act.wait_ge(sem("raw_ready"), i * (3 * SLOTS) + 3 * (SLOTS + s + 1))
                    act.copy(cso[:, i * SLOTS + s, 0, :], raw[:, s, TP:TP + 3]).then_inc(sem("cso_ready"), 1)
                    act.copy(cso[:, i * SLOTS + s, 1:9, :], samp[:, :, 1:4]).then_inc(sem("cso_ready"), 1)
                    high_after(i, s, T_CONV)
                    act.wait_ge(sem("conv_done"), i * SLOTS + s + 1)
                    act.activation(cv[:, i * SLOTS + s, 0:TP], cac[:, s, 0:TP], ACT.Silu,
                                   bias=convb[:, bass.ds(i * SLOTS + s, 1)]).then_inc(sem("cv_ready"), 1)
                    act.activation(cv[:, i * SLOTS + s, TP:T],
                                   cac[:, s, 3 + TP:3 + TP + 29:4],
                                   ACT.Silu, bias=convb[:, bass.ds(i * SLOTS + s, 1)]).then_inc(sem("cv_ready"), 1)
            def gates(i, scale, bias, more=True):
                for s in range(SLOTS):
                    act.wait_ge(sem("sq_used"), i * SLOTS + (KT + s - 3))
                    act.activation(sqb[:, s, :], cv[:, i * SLOTS + s, :], ACT.Square).then_inc(sem("sq_ready"), 1)
                    act.wait_ge(gemm_done, i * SLOTS + (T_GATE + s + 1))
                    act.activation(zg[:, bass.ds(i * SLOTS + s, 1), :], ps[:, s:s + 1, 0:T], ACT.Silu
                                   ).then_inc(sem("zg_ready"), 1)
                    if s < 2 or more:
                        high_after(i, s, T_GATE)
                    act.wait_ge(sem("sq_used"), i * SLOTS + (KT + s + 1))
                    act.wait_ge(sem("norm_free"), i * SLOTS + (s + 1))
                    act.activation(nrm[:, (s + 1) % 2, :], ps[:, 4 + (s + 1) % 2, 0:T], ACT.Sqrt, scale=scale,
                                   bias=bias).then_inc(sem("norm_sqrt"), 1)

            act.wait_ge(sem("cv_ready"), 2 * CT + 8)
            with act.Fori(0, 2) as i:
                gates(i, float(P), epsc[:, 1:2])
            with act.Fori(2, 3) as i:
                gates(i, 1.0, epsc[:, 0:1])
            gates(3, 1.0, epsc[:, 0:1], more=False)
            norms[0] += N_GATE
            sq_n[0] += N_GATE
            act.wait_ge(sem("dA_ready"), 1)
            act.activation(smp[:, 0:8], dAr[:, TP:T], ACT.Exp).then_inc(sem("smp_exp"), 1)

            act.wait_ge(sem("w_sub"), 1)
            act.wait_ge(sem("cso_stored"), 16)
            act.activation(Wt, Wt, ACT.Exp).then_inc(sem("w_exp"), 1)
            act.activation(LE1, BR[:, 0:24, TP - 1], ACT.Exp).then_inc(sem("w_exp"), 1)
            act.activation(nbe, cst2[:, 1, 16:24], ACT.Exp).then_inc(sem("w_exp"), 1)
            act.wait_ge(sem("bt_ps"), 1)
            act.copy(Bt.rearrange("p c n -> p (c n)"), ps[:, 7, :]).then_inc(sem("bt_ready"), 1)
            act.wait_ge(sem("m_sub"), 1)
            act.activation(Mb, Mb, ACT.Exp).then_inc(sem("m_exp"), 1)
            act.wait_ge(sem("h1_ps"), 1)
            act.copy(h1T.rearrange("p (g n) -> p g n", g=2), ps[:, 0:2, :]).then_inc(sem("h1_ready"), 1)
            act.wait_ge(sem("hf_ps"), 1)
            for j in range(2):
                act.copy(hso[:, 4 * j:4 * j + 4, :], ps[:, 2 + j, :].rearrange("p (a n) -> p a n", a=4)
                         ).then_inc(sem("hso_ready"), 1)
            act.wait_ge(sem("m_sub"), 2)
            act.activation(Mb, Mb, ACT.Exp).then_inc(sem("m_exp"), 1)
            act.wait_ge(sem("m_used"), 1)
            act.activation(Mb, BR[:, 0:HS, CH:TP], ACT.Exp).then_inc(sem("m_exp"), 1)

            act.wait_ge(sem("y_ps"), 16)
            act.wait_ge(sem("hf_ps"), 1)
            act.wait_ge(sem("norm_free"), 17)
            act.wait_ge(sem("bc_ps"), 4)
            act.copy(bcs[0:8], ps[0:8, 0, :]).then_inc(sem("bcs_ready"), 1)
            with act.Fori(0, 4) as i:
                act.wait_ge(sem("gdn_free"), i + 1)
                kt = cv[:, bass.ds(i * 2 + TK, 2), 0:TP]
                vt = cv[:, bass.ds(i * 2 + TV, 2), 0:TP]
                act.copy(kf.rearrange("p (h c) t -> p h (c t)", h=2), kt).then_inc(sem("kf_ready"), 1)
                act.copy(vf.rearrange("p (h c) t -> p h (c t)", h=2), vt).then_inc(sem("kf_ready"), 1)
                act.wait_ge(sem("dm_sub"), i + 1)
                act.activation(Dm, Dm, ACT.Exp).then_inc(sem("dm_exp"), 1)
                act.activation(qg, BR[:, bass.ds(i * 2 + 16, 2), CH:TP], ACT.Exp).then_inc(sem("qg_exp"), 1)
                def ada_copy(n):
                    act.wait_ge(gemm_done, i * 12 + (T_ADA2 + 4 * n))
                    if n > 1:
                        act.wait_ge(sem("ada_ps"), i * 3 + (N_ADA1 // SLOTS + n - 1))
                    act.copy(adasb, ps[:, 6, :]).then_inc(sem("ada_sb"), 1)

                for l in range(1, LV):
                    act.wait_ge(sem("x_ps"), i * LV + (l + 1))
                    if l > 1:
                        act.wait_ge(sem("tt_ps"), i * (LV - 1) + (l - 1))
                    act.copy(Xb.rearrange("p a t -> p (a t)"), ps[:, 0, :]).then_inc(sem("x_ready"), 1)
                    if l in (1, 4):
                        ada_copy((l + 2) // 3)
                vn4 = VN.rearrange("p (h c) t -> p h c t", h=2)
                act.wait_ge(sem("vn_ps"), i * 2 + 1)
                act.copy(vn4[:, :, 0, :], ps[:, 0, 0:256].rearrange("p (h t) -> p h t", h=2)
                         ).then_inc(sem("vn_ready"), 1)
                ada_copy(3)
                act.wait_ge(sem("s_ps"), i * 2 + 1)
                act.copy(S1.rearrange("p h t -> p (h t)"), ps[:, 1, 0:256]).then_inc(sem("s_ready"), 1)
                act.wait_ge(sem("vn_ps"), i * 2 + 2)
                act.copy(vn4[:, :, 1, :], ps[:, 0, 0:256].rearrange("p (h t) -> p h t", h=2)
                         ).then_inc(sem("vn_ready"), 1)

            def ada_rest(g):
                act.wait_ge(gemm_done, T_REST + SLOTS * (g + 1))
                act.wait_ge(sem("ada_ps"), (T_REST - T_ADA2 + N_ADA1) // SLOTS + g)
                act.copy(adasb, ps[:, 6, :]).then_inc(sem("ada_sb"), 1)

            ada_rest(0)
            act.wait_ge(sem("ygate_ready"), 1)
            for g in range(2):
                squares([cv[:, TX + 4 * g + j, :] for j in range(4)])
                root(1.0 / 512, epsc[:, 0:1])
            ada_rest(1)
            act.wait_ge(sem("vrow_ps"), 1)
            act.copy(vrow, ps[0:64, 3, 0:128]).then_inc(sem("vrow_ready"), 1)
            act.wait_ge(sem("o_ready"), 1)
            for h in range(HG):
                squares([cv[:, TQ + h, :]])
                if h % 4:
                    root(1.0 / P, epsc[:, 0:1])
                if h % 4 == 3:
                    root(1.0 / P, epsc[:, 0:1])
                    ada_rest(2 + h // 4)
            act.wait_ge(sem("mix_ready"), 1)
            act.copy(mixh[:, 0:8], cv[:, TX:TX + 8, :]).then_inc(sem("mixh_ready"), 1)
            act.wait_ge(sem("mix_ready"), 2)
            act.copy(mixh[:, 8:16], cv[:, TQ:TQ + 8, :]).then_inc(sem("mixh_ready"), 1)

            def high_next(i, s, t0):
                high((s + 1) % SLOTS, i * 16 + (t0 // SLOTS * 16 + 16 + 16 * ((s + 1) // SLOTS)),
                     i * SLOTS + (t0 + s))

            high(0, T_OUT // SLOTS * 16 + 16, None)
            with act.Fori(0, N_OUT // SLOTS) as i:
                for s in range(SLOTS):
                    high_next(i, s, T_OUT)
            act.wait_ge(sem("x1_done"), N_OUT + SLOTS)
            squares([xT[:, k, :] for k in range(KT)])
            root(1.0 / D, epsc[:, 0:1])
            act.wait_ge(sem("gst_stored"), 128)
            high_h(1, hTh)
            with act.Fori(0, N_Q // SLOTS) as i:
                for s in range(SLOTS):
                    high_next(i, s, T_Q)
                    act.wait_ge(gemm_done, i * SLOTS + (T_Q + s + 1))
                    act.wait_ge(sem("score_ps"), i * SLOTS + s + 1)
                    act.copy(qst[:, s, :], ps[:, s, 0:TP]).then_inc(sem("q_staged"), 1)
                    act.copy(qT[:, i * SLOTS + s, :], ps[:, s, 0:T]).then_inc(sem("q_ready"), 1)
            def finish(t):
                t0, n = TILES[t]
                c = cvv[0:64, 0:1] if t == 0 else cvv
                act.wait_ge(sem("cv_sub"), t + 1)
                act.activation(c, c, ACT.Exp).then_inc(sem("cv_exp"), 1)
                act.wait_ge(sem("tk_ps"), t + 1)
                for j, v in enumerate((i1T, i2T, gT)):
                    act.copy(v[:, t0:t0 + n], ps[:, TKB[t], j * 128:j * 128 + n]).then_inc(sem("tk_ready"), 1)

            def gate_copy(n, b, quarter, t0, bank=6):
                act.wait_ge(sem("g_ps"), n + 3)
                act.copy(G[:, bass.ds(quarter, QE), bass.ds(t0, GT)].rearrange("p a t -> p t a"),
                         ps[:, bank + b, 0:GT * QE].rearrange("p (t a) -> p t a", t=GT)).then_inc(sem("g_copied"), 1)

            def split(i, j):
                if j == 1:
                    act.wait_ge(sem("v_done"), i * KT + 1)
                elif j and j <= SLOTS + 1:
                    act.wait_ge(gemm_done, i * SLOTS + (T_U + j - 1))
                elif j:
                    act.wait_ge(sem("v_done"), i * KT + (4 * (j - SLOTS - 1) + 1))
                high(j % SLOTS, i * 32 + (T_U // SLOTS * 16 + 16 * (j // SLOTS) + 16), None)

            act.wait_ge(sem("x1_stored"), 16)
            finish(0)
            finish(1)
            with act.Fori(0, EARLY // 2) as i:
                for b in range(2):
                    gate_copy(i * 2 + b, b, 0, i * (2 * GT) + b * GT, 2)
            finish(2)
            with act.Fori(EARLY // 2, NG // 2) as i:
                for b in range(2):
                    gate_copy(i * 2 + b, b, 0, i * (2 * GT) + b * GT, 2)

            def expert_step(i, groups, g0, quarter, t0, end=False):
                for s in range(SLOTS):
                    split(i, s + 1)
                    act.wait_ge(gemm_done, i * SLOTS + (T_U + s + 1))
                    act.wait_ge(sem("coef_ready"), i * SLOTS + (s + 1))
                    act.activation(craw[:, s % 2, :], ps[:, s % 2, 0:T], ACT.Gelu).then_inc(sem("gelu_done"), 1)
                    if groups and s:
                        g = groups[s - 1]
                        gate_copy(g0 + g, g % 2, quarter, t0 + g * GT)
                for q in range(3 if end else 4):
                    split(i, SLOTS + q + 1)

            for q in range(3):
                if q:
                    act.wait_ge(sem("coef_ready"), q * QE + 2)
                with act.Fori(0, 4) as i2:
                    at = (i2 * 6 + (NG * (q + 1)), (1 - q % 2) * QE, i2 * (6 * GT))
                    expert_step(i2 * 2 + 8 * q, (0, 1, 2), *at)
                    expert_step(i2 * 2 + (8 * q + 1), (3, 4, 5), *at)
            with act.Fori(24, 31) as i:
                expert_step(i, None, None, None, None)
            expert_step(31, None, None, None, None, end=True)
            for j in range(0, KT, 4):
                act.wait_ge(sem("x2_ready"), j // 4 + 1)
                for k in range(j, j + 4):
                    square(xT[:, k, :])
            root_at.append(sq_n[0])
            root(1.0 / D, epsc[:, 0:1], bank=0)

        @block.vector
        def _(dve):
            gemm_done = sem("gemm_done")
            st = Steps(dve, sem("dve_steps"))
            norms = [0]
            link = st.link

            def tt(out, x, y, op):
                return dve.tensor_tensor(out, x, y, op)

            def ts(out, x, s1, s2, op0, op1=ALU.bypass):
                return dve.tensor_scalar(out, x, s1, s2, op0, op1)

            def stt(out, x, s, y, op0, op1):
                return dve.scalar_tensor_tensor(out=out, in0=x, scalar=s, in1=y, op0=op0, op1=op1)

            def inv_root():
                k = norms[0]
                norms[0] += 1
                dve.wait_ge(sem("norm_sqrt"), k + 1)
                link(dve.reciprocal(nrm[:, k % 2, :], nrm[:, k % 2, :]))
                return nrm[:, k % 2, :]

            def over(v, n, at=1):
                return v.unsqueeze(at).broadcast_to(list(v.shape[:at]) + [n] + list(v.shape[at:]))

            dve.memset(sT[:, :, NC:32], 0.0).then_inc(sem("s_zero"), 1)
            dve.sem_inc(sem("x1_done"), SLOTS)
            dve.sem_inc(sem("v_added"), 4)
            dve.memset(raw[:, :, 0:3], 0.0).then_inc(sem("raw_zero"), 1)
            dve.wait_ge(sem("ld_par"), 16)
            dve.wait_ge(sem("ld_const"), 16)

            def modulated(w, sh, sc, k, piece=None):
                link(stt(mod[:, sc:sc + KT, :], mod[:, sc:sc + KT, :], 1.0, over(w, NC, 2), ALU.add, ALU.mult))
                r = inv_root()
                for g in range(0, KT, 4):
                    link(tt(hT[:, g:g + 4], xT[:, g:g + 4], over(r, 4), ALU.mult))
                    for j in range(g, g + 4):
                        st.mark(ts(hT[:, j, 0:TP], hT[:, j, 0:TP], mod[:, sc + j, 0:1], mod[:, sh + j, 0:1],
                                   ALU.mult, ALU.add))
                    hs = hT[:, g:g + 4, TP:T]
                    link(tt(hs, hs, mod[:, sc + g:sc + g + 4, 1:NC], ALU.mult))
                    tt(hs, hs, mod[:, sh + g:sh + g + 4, 1:NC], ALU.add).then_inc(sem("h_ready"), 1)
                    if g and piece:
                        piece(g - 4)
                if piece:
                    piece(KT - 4)
                dve.wait_ge(sem("h_ready"), 4 * k + 4)
                dve.engine_nop().then_inc(sem("norm_free"), 1)

            dve.wait_ge(sem("ada_ps"), N_ADA1 // SLOTS)
            link(tt(mod[:, 0:32, :], ps[:, 7, 0:32 * NC].rearrange("p (n c) -> p n c", c=NC),
                    over(bada[:, 0:32], NC, 2), ALU.add))
            modulated(n1w, 0, 16, 0)

            dve.wait_ge(sem("small_done"), 1)
            link(ts(xbr, ps[0:32, 6, 0:T], rbias, None, ALU.add))
            stt(abr, xbr, -1.0, xbr, ALU.mult, ALU.max).then_inc(sem("abs_ready"), 1)
            dve.wait_ge(sem("exp_ready"), 1)
            link(ts(z1r, abr, 2.0, None, ALU.add))
            link(dve.reciprocal(z1r, z1r))
            link(tt(z1r, z1r, abr, ALU.mult))
            link(tt(z2r, z1r, z1r, ALU.mult))
            link(ts(polyr, z2r, 1.0 / 17, None, ALU.mult))
            for c in (15, 13, 11, 9, 7, 5, 3):
                link(stt(polyr, polyr, 1.0 / c, z2r, ALU.add, ALU.mult))
            link(stt(polyr, polyr, 1.0, z1r, ALU.add, ALU.mult))
            link(ts(polyr, polyr, 2.0, None, ALU.mult))
            link(stt(spr, xbr, 0.0, polyr, ALU.max, ALU.add))
            dve.wait_ge(sem("sg_ready"), 2)
            link(ts(dAr, spr, rbias2[:, 0:1], -1.0, ALU.mult, ALU.mult))
            link(dve.tensor_copy(smp[:, 8:16], spr[:, TP:T]))
            dve.tensor_copy(smp[:, 16:24], sgr[:, TP:T]).then_inc(sem("small_rows"), 1)
            dve.wait_ge(sem("small_rows"), 1)
            dve.sem_inc(sem("dA_ready"), 1)

            def low(n, slot):
                dve.wait_ge(sem("hi_ready"), n + 1)
                tt(wlo[:, slot % 2], wring[:, slot], whi_f[:, slot % 2], ALU.subtract).then_inc(sem("lo_ready"), 1)

            def low_h(k, high, j):
                dve.wait_ge(sem("hth_ready"), 4 * k + j // 4 + 1)
                tt(hTl[:, j:j + 4], hT[:, j:j + 4], high[:, j:j + 4], ALU.subtract).then_inc(sem("hl_ready"), 1)

            for j in range(0, KT, 4):
                low_h(0, h1h_f, j)
            low(0, 0)
            low(1, 1)
            with dve.Fori(0, N_CONV // SLOTS) as i:
                st.enter(i, 3 * SLOTS)
                for s in range(SLOTS):
                    w = lambda j: convw[:, bass.ds(i * (4 * SLOTS) + (4 * s + j), 1)]
                    dve.wait_ge(sem("raw_ready"), i * (3 * SLOTS) + 3 * (SLOTS + s + 1))
                    dve.wait_ge(sem("cv_ready"), i * (2 * SLOTS) + 2 * (s + 1))
                    link(ts(cac[:, s, :], raw[:, s, 0:CV], w(0), None, ALU.mult))
                    for j in (1, 2):
                        link(stt(cac[:, s, :], raw[:, s, j:j + CV], w(j), cac[:, s, :], ALU.mult, ALU.add))
                    stt(cac[:, s, :], raw[:, s, 3:3 + CV], w(3), cac[:, s, :], ALU.mult, ALU.add
                        ).then_inc(sem("conv_done"), 1)
                    low(i * SLOTS + (s + 2), (s + 2) % SLOTS)
            st.leave(N_CONV // SLOTS)

            def gates(i, more=True):
                for s in range(SLOTS):
                    if s < 2 or more:
                        low(i * SLOTS + (N_CONV + s + 2), (s + 2) % SLOTS)
                    r = nrm[:, (s + 1) % 2, :]
                    dve.wait_ge(sem("norm_sqrt"), i * SLOTS + (s + 2))
                    link(dve.reciprocal(r, r))
                    v = cv[:, bass.ds(i * SLOTS + s, 1), :]
                    tt(v, v, over(r, 1), ALU.mult).then_inc(sem("norm_free"), 1)

            with dve.Fori(0, N_GATE // SLOTS - 1) as i:
                st.enter(i, SLOTS)
                gates(i)
            st.leave(N_GATE // SLOTS - 1)
            gates(N_GATE // SLOTS - 1, more=False)
            norms[0] += N_GATE

            dve.wait_ge(sem("tok_ps"), 1)
            dve.tensor_copy(tok.rearrange("p a b -> p (a b)"), ps[:, 6, 0:192]).then_inc(sem("tok_ready"), 1)
            dve.wait_ge(sem("cs_ps"), 1)
            link(dve.tensor_copy(cst2.rearrange("p a b -> p (a b)"), ps[:, 7, 256:320]))
            dve.tensor_copy(csr, ps[0:32, 7, 0:TP]).then_inc(sem("cs_ready"), 1)
            dve.wait_ge(sem("cs_ready"), 1)

            dve.wait_ge(sem("cso_stored"), 16)
            for c in range(2):
                for j in range(2):
                    dve.wait_ge(sem("xt_ps"), 8 * c + 4 * j + 4)
                    st.mark(tt(xdt[:, c, j * 512:(j + 1) * 512].rearrange("p (h d) -> p h d", d=64),
                               ps[:, 2 * c + j, :].rearrange("p (h d) -> p h d", d=64),
                               over(tok[:, 2 + c, 8 * j:8 * j + 8], 64, 2), ALU.mult))
            st.settle()
            dve.sem_inc(sem("xdt_ready"), 1)
            dve.wait_ge(sem("ld_br"), 16)
            for c in range(2):
                last = tt(Wt[:, c, :], BR[:, 0:24, c * CH + CH - 1], cst2[:, c, 0:24], ALU.subtract)
                if c == 0:
                    link(last)
            last.then_inc(sem("w_sub"), 1)
            dve.wait_ge(sem("w_exp"), 3)
            link(tt(wf0, Wt[:, 0, :], LE1, ALU.mult))
            stt(nbe, nbe, -1.0, tok[:, 5, 24:32], ALU.mult, ALU.mult).then_inc(sem("wf_ready"), 1)

            def decay(c):
                link(tt(Mb, BR[:, 0:HS, c * CH:(c + 1) * CH], over(cst2[:, c, 0:HS], CH, 2), ALU.subtract))
                ts(Mb, Mb, 0.0, None, ALU.min).then_inc(sem("m_sub"), 1)

            decay(0)
            dve.wait_ge(sem("cb_ps"), 1)
            link(tt(cbm, ps[:, 6, :].rearrange("p (a t) -> p a t", a=4), over(tri, 4), ALU.mult))
            for c in range(2):
                dve.wait_ge(sem("m_exp"), c + 1)
                link(tt(Mb[:, 0:8, :], Mb[:, 0:8, :], over(cbm[:, 2 * c, :], 8), ALU.mult))
                tt(Mb[:, 8:16, :], Mb[:, 8:16, :], over(cbm[:, 2 * c + 1, :], 8), ALU.mult
                   ).then_inc(sem("m_ready"), 1)
                if c == 0:
                    for hp in range(8):
                        dve.wait_ge(sem("y_ps"), hp // 4 * 4 + 4)
                        yt = cv[:, TX + hp, 0:CH]
                        stt(yt, yt, dcol[:, hp:hp + 1], ps[:, 4 + hp // 4, (hp % 4) * 128:(hp % 4 + 1) * 128],
                            ALU.mult, ALU.add).then_inc(sem("y_evac"), 1)
                    decay(1)
            dve.wait_ge(sem("m_used"), 1)
            for hp in range(8):
                yt = cv[:, TX + hp, CH:TP]
                stt(yt, yt, dcol[:, hp:hp + 1], ps[:, 4 + hp // 4, (hp % 4) * 128:(hp % 4 + 1) * 128],
                    ALU.mult, ALU.add).then_inc(sem("y_evac"), 1)
            dve.wait_ge(sem("m_exp"), 3)
            for g in range(2):
                m = Mb[:, 8 * g:8 * g + 8, :]
                last = tt(m, m, over(cv[:, TC + g, CH:TP], 8), ALU.mult)
                if g == 0:
                    link(last)
            last.then_inc(sem("ce_ready"), 1)
            dve.wait_ge(sem("y_evac"), 16)
            for hp in range(8):
                dve.wait_ge(sem("y_ps"), hp // 4 * 4 + 12)
                yt = cv[:, TX + hp, CH:TP]
                tt(yt, yt, ps[:, 6 + hp // 4, (hp % 4) * 128:(hp % 4 + 1) * 128], ALU.add
                   ).then_inc(sem("y_evac"), 1)

            dve.wait_ge(sem("ld_sr"), 16)
            for q in range(2):
                rows = slice(64 * q, 64 * q + 64)
                for dst, src in ((Esel, SR[:, 0:HS, 0]), (dtsel, SR[:, 0:HS, 1])):
                    link(dve.tensor_copy(dst[rows], src[rows, q:HS:2, :]))
            link(tt(XD, cv[:, TX:TX + 8, TP:T], dtsel, ALU.mult))
            dve.sem_inc(sem("xd_ready"), 1)
            dve.sem_inc(sem("ysm_ready"), 1)

            dve.wait_ge(sem("norm_free"), 17)
            with dve.Fori(0, 4) as i:
                st.enter(i, GDN_STEPS)

                def sample_sum(c):
                    dve.wait_ge(sem("stm_ready"), i * 2 + (c + 1))
                    dve.tensor_reduce(ysm[:, bass.ds(i * 2 + c, 1), :].rearrange("p b t -> p (b t)"),
                                      stm.rearrange("p (t n) -> p t n", n=128), AX, ALU.add
                                      ).then_inc(sem("ysm_ready"), 1)

                dve.wait_ge(sem("gdn_free"), i + 1)
                d4 = Dm.rearrange("p (h c) t -> p h c t", h=2)
                for h in range(2):
                    st.mark(tt(Dm[:, 2 * h:2 * h + 2, :],
                               BR[:, i * 2 + (16 + h), :].rearrange("p (c t) -> p c t", c=2),
                               over(cst2[:, :, bass.ds(i * 2 + (16 + h), 1)].rearrange("p c o -> p (c o)"), CH, 2),
                               ALU.subtract))
                tt(kb.rearrange("p (h c) t -> p h (c t)", h=2), cv[:, bass.ds(i * 2 + TK, 2), 0:TP],
                   BR[:, bass.ds(i * 2 + 24, 2), :], ALU.mult).then_inc(sem("kb_ready"), 1)
                st.settle()
                ts(Dm, Dm, 0.0, None, ALU.min).then_inc(sem("dm_sub"), 1)
                dve.wait_ge(sem("dm_exp"), i + 1)
                link(tt(Dm, Dm, over(tri, 4), ALU.mult))
                dve.wait_ge(sem("kk_ps"), i + 1)
                link(tt(LT, Dm, ps[:, 0, :].rearrange("p (a t) -> p a t", a=4), ALU.mult))
                link(tt(Bm0, LT, over(lvl[:, 0, :], 4), ALU.mult))
                dve.sem_inc(sem("lt_ready"), 1)
                tt(Tt, over(ident, 4), Bm0, ALU.subtract).then_inc(sem("t_ready"), 1)
                tt(QK, Dm, ps[:, 1, :].rearrange("p (a t) -> p a t", a=4), ALU.mult).then_inc(sem("qk_ready"), 1)
                dve.wait_ge(sem("x_ps"), i * LV + 1)
                tt(Tm, over(ident, 4), ps[:, 0, :].rearrange("p (a t) -> p a t", a=4), ALU.subtract
                   ).then_inc(sem("t_ready"), 1)
                dve.wait_ge(sem("qg_exp"), i + 1)
                st.mark(tt(qg, qg, cv[:, bass.ds(i * 2 + TQ, 2), CH:TP], ALU.mult))
                dve.wait_ge(sem("vt_ps"), i + 1)
                r4 = Rv.rearrange("p (h c) t -> p h c t", h=2)
                k4 = kd.rearrange("p (h c) t -> p h c t", h=2)
                v4 = ps[:, 2, :].rearrange("p (h c t) -> p h c t", h=2, c=2)
                kt4 = ps[:, 3, :].rearrange("p (h c t) -> p h c t", h=2, c=2)
                dve.wait_ge(sem("kt_ps"), i + 1)
                for c in range(2):
                    last = tt(k4[:, :, c, :], kt4[:, :, c, :], over(Wt[:, c, bass.ds(i * 2 + 16, 2)], P, 2), ALU.mult)
                    st.mark(last)
                    last = tt(r4[:, :, c, :], v4[:, :, c, :], over(tok[:, 4 + c, bass.ds(i * 2 + 24, 2)], P, 2),
                              ALU.mult)
                    if c == 0:
                        last.then_inc(sem("rv0_ready"), 1)
                    else:
                        last.then_inc(sem("rv_ready"), 1)
                for l in range(1, LV):
                    if l < LV - 1:
                        dve.wait_ge(sem("tm_ps"), i * (LV - 2) + l)
                        tt(Tm, Tm, ps[:, 4, :].rearrange("p (a t) -> p a t", a=4), ALU.subtract
                           ).then_inc(sem("t_ready"), 1)
                    dve.wait_ge(sem("tt_ps"), i * (LV - 1) + l)
                    tt(Tt, Tt, ps[:, 1, :].rearrange("p (a t) -> p a t", a=4), ALU.subtract
                       ).then_inc(sem("t_ready"), 1)
                    if l == LV - 1:
                        dve.engine_nop().then_inc(sem("t_ready"), 1)
                    if l == 4:
                        sample_sum(0)
                dve.wait_ge(sem("ks_ps"), i + 1)
                for h in range(2):
                    last = stt(Rv[:, 2 * h + 1, :], ps[:, 0, 256 + h * 128:256 + (h + 1) * 128],
                               nbe[:, bass.ds(i * 2 + h, 1)], Rv[:, 2 * h + 1, :], ALU.mult, ALU.add)
                    if h == 0:
                        st.mark(last)
                last.then_inc(sem("rv_ready"), 1)
                dve.wait_ge(sem("o_ps"), i + 1)
                link(dve.tensor_copy(cv[:, bass.ds(i * 2 + TQ, 2), 0:TP],
                                     ps[:, 5, :].rearrange("p (h t) -> p h t", h=2)))
                sample_sum(1)
                dve.wait_ge(sem("ada_ps"), i * 3 + (N_ADA1 // SLOTS + 3))
                st.mark(tt(mod[:, bass.ds(i * 12 + 32, 12), :],
                           ps[:, 7, 0:12 * NC].rearrange("p (n c) -> p n c", c=NC),
                           over(bada[:, bass.ds(i * 12 + 32, 12)], NC, 2), ALU.add))
                dve.wait_ge(sem("s_ps"), i * 2 + 2)
                dve.wait_ge(sem("s2_free"), i + 1)
                for h in range(2):
                    last = stt(S2[:, h, :], S1[:, h, :], LE1[:, bass.ds(i * 2 + (16 + h), 1)],
                               ps[:, 1, h * 128:(h + 1) * 128], ALU.mult, ALU.add)
                    if h == 0:
                        st.mark(last)
                last.then_inc(sem("gdn_free"), 1)
            st.leave(4)

            dve.wait_ge(sem("ysm_ready"), TS + 1)
            xs = cv[:, TX:TX + 8, TP:T]
            link(tt(xs, xs, over(dcol, TS, 2), ALU.mult))
            link(tt(xs, xs, ysm.rearrange("p b t -> p t b"), ALU.add))
            link(tt(cv[:, TX:TX + 8, :], cv[:, TX:TX + 8, :], zg[:, 0:8, :], ALU.mult))
            dve.sem_inc(sem("ygate_ready"), 1)

            qs, ks, vs = (cv[:, t:t + 8, TP:T] for t in (TQ, TK, TV))
            eight = lambda v: v.rearrange("p (h b) -> p h b", b=TS)
            for c in range(2):
                dve.wait_ge(sem(f"sst_stored{c}"), 64)
            link(tt(eight(qkp), qs, ks, ALU.mult))
            dve.sem_inc(sem("qkp_ready"), 1)
            kq4 = kq.rearrange("p (h b) w -> p h b w", b=TS)
            link(dve.tensor_copy(kq4[:, :, :, 0], ks))
            link(dve.tensor_copy(kq4[:, :, :, 1], qs))
            dve.sem_inc(sem("kq_ready"), 1)
            for g in range(2):
                r = inv_root()
                for j in range(4):
                    t = 4 * g + j
                    v = cv[:, TX + t, :]
                    last = stt(v, v, ynw[:, t:t + 1], r, ALU.mult, ALU.mult)
                    if j < 3:
                        st.mark(last)
                last.then_inc(sem("norm_free"), 1)
            dve.wait_ge(sem("norm_free"), norms[0])
            dve.sem_inc(sem("mix_ready"), 1)
            dve.wait_ge(sem("skq_ps"), 1)
            dve.wait_ge(sem("qk_ps"), 1)
            skq = ps[:, 2, 0:128].rearrange("p (h b w) -> p h b w", b=TS, w=2)
            eg = SR[:, 16:24, 0, :]
            be = SR[:, 24:32, 2, :]
            link(tt(eight(vn), skq[:, :, :, 0], eg, ALU.mult))
            link(tt(eight(vn), vs, eight(vn), ALU.subtract))
            link(tt(eight(vn), eight(vn), be, ALU.mult))
            dve.sem_inc(sem("vns_ready"), 1)
            link(tt(eight(ksm), skq[:, :, :, 1], eg, ALU.mult))
            link(tt(vsm, vn, ps[:, 1, 0:64], ALU.mult))
            link(tt(qs, eight(ksm), eight(vsm), ALU.add))
            dve.sem_inc(sem("o_ready"), 1)
            for h in range(HG):
                r = inv_root()
                v = cv[:, TQ + h, :]
                stt(v, v, onw[:, 0:1], r, ALU.mult, ALU.mult).then_inc(sem("norm_free"), 1)
            dve.wait_ge(sem("norm_free"), norms[0])
            tt(cv[:, TQ:TQ + 8, :], cv[:, TQ:TQ + 8, :], zg[:, 8:16, :], ALU.mult).then_inc(sem("mix_ready"), 1)
            dve.wait_ge(sem("gst_scaled"), 2)
            dve.wait_ge(sem("ada_ps"), (N_ADA1 + N_ADA2) // SLOTS)
            for j, t in enumerate((TX, TQ)):
                dve.wait_ge(sem("mixh_ready"), j + 1)
                tt(mixl[:, 8 * j:8 * j + 8], cv[:, t:t + 8, :], mixh_f[:, 8 * j:8 * j + 8], ALU.subtract
                   ).then_inc(sem("mixl_ready"), 1)
            low(L_OUT, 0)

            dve.wait_ge(sem("ada_ps"), (N_ADA1 + N_ADA2) // SLOTS)
            link(tt(mod[:, 80:96, :], ps[:, 7, 0:16 * NC].rearrange("p (n c) -> p n c", c=NC),
                    over(bada[:, 80:96], NC, 2), ALU.add))

            G1 = 32
            for half in range(2):
                with dve.Fori(0, 2) as i:
                    st.enter(i, 2 * SLOTS)
                    for s in range(SLOTS):
                        n = i * SLOTS + (8 * half + s)
                        low(i * SLOTS + (L_OUT + 8 * half + s + 1), (s + 1) % SLOTS)
                        dve.wait_ge(gemm_done, i * SLOTS + (T_OUT + 8 * half + s + 1))
                        st.mark(stt(xT[:, n, 0:TP], ps[:, s, 0:TP], mod[:, n + G1, 0:1], xT[:, n, 0:TP],
                                    ALU.mult, ALU.add))
                        link(tt(gtmp[:, s, :], ps[:, s, TP:T], mod[:, n + G1, 1:NC], ALU.mult))
                        tt(xT[:, n, TP:T], xT[:, n, TP:T], gtmp[:, s, :], ALU.add).then_inc(sem("x1_done"), 1)
                        if s == 0:
                            dve.wait_ge(sem("ld_gvb"), i * 16 + (32 * half + 16))
                        for p in range(4):
                            pair = gst[half][:, i * 16 + (4 * s + p), :]
                            stt(pair, gvb[:, 4 * s + p, :],
                                cv[:, i * 2 + (TK + 4 * half + s // 2), TP + (4 * s + p) % 8:TP + (4 * s + p) % 8 + 1],
                                pair, ALU.mult, ALU.add).then_inc(sem("gst_ready"), 1)
                st.leave(2)
            dve.wait_ge(sem("x1_done"), N_OUT + SLOTS)
            dve.wait_ge(sem("gst_stored"), 128)
            modulated(n2w, 48, 64, 1, lambda j: low_h(1, hTh_f, j))
            def top16(items, between=()):
                between = list(between)

                def stage(ops):
                    for it in items:
                        for op in ops:
                            st.mark(op(*it))
                    if between:
                        between.pop(0)()
                    st.settle()

                stage([lambda x, v, i, w: dve.max(v[:, 0:8], x)])
                stage([lambda x, v, i, w: dve.max_index(i[:, 0:8], v[:, 0:8], x),
                       lambda x, v, i, w: dve.match_replace(w, v[:, 0:8], x, -3.0e38)])
                stage([lambda x, v, i, w: dve.max(v[:, 8:16], w)])
                stage([lambda x, v, i, w: dve.max_index(i[:, 8:16], v[:, 8:16], w)])

            def keys(j):
                dve.wait_ge(sem("score_ps"), j + 1 + SLOTS)
                top16([(ps[:, 4 + j % 4, half * P:(half + 1) * P], v[:, j, :], i[:, j, :],
                        work[:, (2 * (j % 4) + half) * P:(2 * (j % 4) + half + 1) * P])
                       for half, (v, i) in enumerate(((sv, siu), (sv_2, siu_2)))])
                dve.sem_inc(sem("score_used"), 1)

            dve.sem_inc(sem("score_used"), SLOTS)
            for j in range(N_Q):
                low(L_Q + j + 1, (j + 1) % SLOTS)
                if j >= 2:
                    keys(j - 2)
            keys(N_Q - 2)
            keys(N_Q - 1)

            dve.wait_ge(sem("x1_stored"), 16)
            link(dve.memset(Qs, 0.0))
            dve.wait_ge(sem("q_ready"), N_Q + SLOTS)
            for j in range(16):
                at = (j % 2) * 64 + (j // 2) * TS
                st.mark(dve.tensor_copy(Qs[:, j, at:at + TS], qT[:, j, TP:T]))
            st.settle()
            dve.sem_inc(sem("qs_ready"), 1)

            def candidates(t, n, heads, values, indices, between=()):
                link(tt(cand[0:n, 0:heads].rearrange("p h (a b) -> p h a b", b=16), over(values(0), 16, 3),
                        over(values(1), 16, 2), ALU.add))
                top16([(cand[0:n, h, :], cvv[0:n, h, :], ciu[0:n, h, :], work[0:n, h * 256:(h + 1) * 256])
                       for h in range(heads)], between)
                c, gs = cvv[0:n, 0:heads], gsum[0:n, 0:heads]
                link(dve.tensor_copy(gs, c[:, :, 0]))
                link(tt(c, c, over(gs, 16, 2), ALU.subtract))
                dve.sem_inc(sem("cv_sub"), 1)
                m = heads * 16
                for side, (op, by), dst in ((0, (ALU.logical_shift_right, 4), tkI1),
                                            (1, (ALU.bitwise_and, 15), tkI2)):
                    link(ts(rcu[0:n, 0:heads], ciu[0:n, 0:heads], by, None, op))
                    link(dve.tensor_copy(rcf[0:n, 0:heads], rcu[0:n, 0:heads]))
                    rflat = rcf[0:n, 0:heads].rearrange("p h k -> p (h k)")
                    link(tt(oh[0:n, 0:m], over(rflat, 16, 2), over(iota[0:n, 0:16], m), ALU.is_equal))
                    o4 = oh[0:n, 0:m].rearrange("p (h k) r -> p h k r", k=16)
                    link(tt(o4, o4, over(indices(side), 16, 2), ALU.mult))
                    link(dve.tensor_reduce(dst[0:n, 0:m], oh[0:n, 0:m], AX, ALU.add))
                dve.wait_ge(sem("cv_exp"), t + 1)
                link(dve.tensor_reduce(gs, c, AX, ALU.add))
                link(dve.reciprocal(gs, gs))
                link(tt(tkG[0:n, 0:m].rearrange("p (h k) -> p h k", k=16), c, over(gs, 16, 2), ALU.mult))

            dve.wait_ge(sem("score_ps"), N_Q + 1 + SLOTS)
            top16([(ps[:, 4, 0:128], sv_s[:, 0, :], siu_s[:, 0, :], work[:, 0:128])])
            link(dve.tensor_copy(sv_s[:, 1, :], siu_s[:, 0, :]))
            dve.sem_inc(sem("pair_ready"), 1)
            dve.wait_ge(sem("pair_ps"), 1)
            link(dve.tensor_copy(sv_s[0:64, 2:6, :].rearrange("p a k -> p (a k)"), ps[0:64, 5, 0:64]))
            candidates(0, 64, 1, lambda side: sv_s[0:64, 2 + 2 * side:3 + 2 * side, :],
                       lambda side: sv_s[0:64, 3 + 2 * side:4 + 2 * side, :])
            for j, v in enumerate((tkI1, tkI2, tkG)):
                st.mark(tt(oh[0:64, 8 * j:8 * j + 8, :], over(v[0:64, 0:16], 8), over(of_head[0:64], 16, 2), ALU.mult))
            st.settle()
            dve.sem_inc(sem("top_done"), 1)

            def prompt(t, values, indices, between=()):
                n = TILES[t][1]
                dve.wait_ge(sem("tk_ps"), t)
                link(dve.tensor_copy(sif[0:n], indices[0:n]))
                sv4 = values[0:n].rearrange("p (h s) k -> p h s k", s=2)
                si4 = sif[0:n].rearrange("p (h s) k -> p h s k", s=2)
                candidates(t, n, 8, lambda side: sv4[:, :, side, :], lambda side: si4[:, :, side, :], between)
                dve.sem_inc(sem("top_done"), 1)

            def gate_parts(t0, n, ready):
                dve.wait_ge(sem("tk_ready"), ready)
                for part in range(3):
                    link(dve.tensor_copy(gp[:, t0:t0 + n, part], gT[:, t0:t0 + n]))
                    if part < 2:
                        link(tt(gT[:, t0:t0 + n], gT[:, t0:t0 + n], gp[:, t0:t0 + n, part], ALU.subtract))
                dve.sem_inc(sem("gp_ready"), 1)

            def one_hots(n, b, quarter, t0):
                dve.wait_ge(sem("g_ps"), n + 1)
                tt(Soh[:, b], over(iota[:, quarter * QE:(quarter + 1) * QE], GT),
                   over(i2T[:, bass.ds(t0, GT)], QE, 2), ALU.is_equal).then_inc(sem("soh_ready"), 1)
                tt(Aoh[:, b], over(iota, GT), over(i1T[:, bass.ds(t0, GT)], P, 2), ALU.is_equal
                   ).then_inc(sem("aoh_ready"), 1)

            def early(*groups):
                def go():
                    for g in groups:
                        one_hots(g, g % 2, 0, g * GT)
                return go

            prompt(1, sv, siu)
            prompt(2, sv_2, siu_2, (lambda: gate_parts(0, P, 6), early(0, 1, 2), early(3, 4), early(5, 6, 7)))

            dve.memset(acc, 0.0).then_inc(sem("acc_zero"), 1)
            dve.wait_ge(sem("acc_zero"), 1)
            dve.sem_inc(sem("coef_ready"), 2)
            gate_parts(TP, TS, 3)
            gate_parts(P, P, 9)

            def split(i, j):
                low(i * (2 * SLOTS) + (L_E + j), j % SLOTS)

            with dve.Fori(EARLY // 2, NG // 2) as i:
                for b in range(2):
                    one_hots(i * 2 + b, b, 0, i * (2 * GT) + b * GT)

            def expert_step(i, groups, g0, quarter, t0, col, end=False):
                def oh(j):
                    if groups:
                        g = groups[j]
                        one_hots(g0 + g, g % 2, quarter + 1, t0 + g * GT)

                for s in range(SLOTS):
                    split(i, s + 1)
                    if s < 3:
                        oh(s)
                    c, g = craw[:, s % 2, :], G[:, col + s, :]
                    dve.wait_ge(sem("gelu_done"), i * SLOTS + (s + 3))
                    st.mark(tt(chi[:, s, :], c, g, ALU.mult))
                    link(tt(c, c, g, ALU.mult))
                    tt(clo[:, s, :], c, chi_f[:, s, :], ALU.subtract).then_inc(sem("coef_ready"), 1)
                for q in range(4):
                    if not (end and q == 3):
                        split(i, SLOTS + q + 1)
                    dve.wait_ge(sem("v_added"), i * KT + (4 * q + 4))
                    for d in range(4):
                        dve.wait_ge(sem("v_done"), i * KT + (4 * q + d + 2))
                        tt(acc[:, 4 * q + d, :], acc[:, 4 * q + d, :], ps[:, 2 + d, 0:T], ALU.add
                           ).then_inc(sem("v_added"), 1)
                    if end and q:
                        x2(q - 1)

            def x2(q):
                G2 = 80
                dve.wait_ge(sem("x1_back"), 16)
                dve.wait_ge(sem("v_added"), (N_U // SLOTS - 1) * KT + 4 * q + 8)
                for j in range(4 * q, 4 * q + 4):
                    st.mark(stt(xT[:, j, 0:TP], acc[:, j, 0:TP], mod[:, G2 + j, 0:1], xT[:, j, 0:TP],
                                ALU.mult, ALU.add))
                four = slice(4 * q, 4 * q + 4)
                link(tt(acc[:, four, TP:T], acc[:, four, TP:T], mod[:, G2 + 4 * q:G2 + 4 * q + 4, 1:NC], ALU.mult))
                tt(xT[:, four, TP:T], xT[:, four, TP:T], acc[:, four, TP:T], ALU.add).then_inc(sem("x2_ready"), 1)

            for q in range(4):
                dve.wait_ge(sem("g_copied"), NG * (q + 1) + 2)
                half = (q % 2) * QE
                if q < 3:
                    with dve.Fori(0, 4) as i2:
                        st.enter(i2, 16)
                        g0 = i2 * 6 + NG * (q + 1)
                        expert_step(i2 * 2 + 8 * q, (0, 1, 2), g0, q, i2 * (6 * GT), i2 * 8 + half)
                        expert_step(i2 * 2 + (8 * q + 1), (3, 4, 5), g0, q, i2 * (6 * GT), i2 * 8 + (half + 4))
                    st.leave(4)
                else:
                    with dve.Fori(0, 7) as i:
                        st.enter(i, 8)
                        expert_step(i + 24, None, None, None, None, i * 4 + half)
                    st.leave(7)
                    expert_step(31, None, None, None, None, 28 + half, end=True)
                    x2(3)

            r = inv_root()
            for j in range(KT):
                st.mark(stt(hT[:, j, :], xT[:, j, :], fnw[:, j:j + 1], r, ALU.mult, ALU.mult))
                if j % 4 == 3:
                    st.settle()
                    dve.sem_inc(sem("y_ready"), 1)

        @block.gpsimd
        def _(pool):
            def tt(out, x, y, op):
                return pool.tensor_tensor(out, x, y, op)

            def over(v, n, at=1):
                return v.unsqueeze(at).broadcast_to(list(v.shape[:at]) + [n] + list(v.shape[at:]))

            pst = Steps(pool, sem("pool_steps"))
            pool.sem_inc(sem("s2_free"), 1)
            pool.wait_ge(sem("smp_exp"), 1)
            pool.wait_ge(sem("cs_ready"), 1)
            pool.dma_start(a["rows_dram"][0:24, :], csr[0:24, :]).then_inc(sem("rows_out"), 16)
            pool.dma_start(a["rows_dram"][24:32, :], sgr[24:32, 0:TP]).then_inc(sem("rows_out"), 16)
            pool.dma_start(a["smp_dram"], smp[0:32]).then_inc(sem("rows_out"), 16)
            pool.wait_ge(sem("cso_ready"), 2 * CT)
            pool.dma_start(o["conv_out"], cso).then_inc(sem("cso_stored"), 16)
            pool.wait_ge(sem("rows_out"), 48)
            pool.wait_ge(sem("cv_ready"), 2 * CT + 8)
            pool.dma_start(BR, a["rows_dram"].partition_broadcast(P)).then_inc(sem("ld_br"), 16)
            pool.dma_start(SR.rearrange("p r k b -> p r (k b)"), a["smp_dram"].partition_broadcast(P)
                           ).then_inc(sem("ld_sr"), 16)
            pool.wait_ge(sem("xdt_ready"), 1)
            pool.wait_ge(sem("w_exp"), 3)
            pool.wait_ge(sem("cso_stored"), 16)
            x0, x1 = (xdt[:, c, :].rearrange("p (h d) -> p h d", d=64) for c in range(2))
            f0, f1 = (xwf[:, c, :].rearrange("p (h d) -> p h d", d=64) for c in range(2))
            tt(xw0, x0, over(Wt[:, 0, 0:HS], 64, 2), ALU.mult).then_inc(sem("xw_ready"), 1)
            tt(f1, x1, over(Wt[:, 1, 0:HS], 64, 2), ALU.mult).then_inc(sem("xw_ready"), 1)
            pool.wait_ge(sem("wf_ready"), 1)
            tt(f0, x0, over(wf0[:, 0:HS], 64, 2), ALU.mult).then_inc(sem("xw_ready"), 1)
            pool.wait_ge(sem("hso_ready"), 2)
            pool.dma_start(ssd_p, hso).then_inc(sem("hso_stored"), 16)
            pool.wait_ge(sem("y_evac"), 24)
            pool.wait_ge(sem("hso_stored"), 16)
            pool.wait_ge(sem("bcs_ready"), 1)
            pool.dma_start(a["bc_dram"], bcs[0:8].rearrange("p (j n) -> p j n", j=4)).then_inc(sem("bc_out"), 16)
            pool.wait_ge(sem("bc_out"), 16)
            pool.wait_ge(sem("xd_ready"), 1)
            with pool.Fori(0, 4) as i:
                pst.enter(i, 6)
                for c in range(2):
                    pool.dma_start(sst[:, c:c + 1].rearrange("p b (t n) -> p b t n", n=128),
                                   ssd_s_in[:, bass.ds(i * 2 + c, 1)]).then_inc(sem(f"ld_sst{c}"), 16)
                    pool.dma_start(BC[:, c:c + 1].rearrange("p b (j n) -> p (b j) n", n=128),
                                   a["bc_dram"][bass.ds(i * 2 + c, 1)].rearrange("b j n -> (b j) n"
                                                                                 ).partition_broadcast(P)
                                   ).then_inc(sem(f"ld_bc{c}"), 16)

                def level(l):
                    if l >= 2:
                        pool.wait_ge(sem("x_ps"), i * LV + (l - 1))
                        pool.wait_ge(sem("t_ready"), i * (2 * LV) + 1)
                    tt((Bm0, Bm1)[l % 2], LT, over(lvl[:, l, :], 4), ALU.mult).then_inc(sem("b_ready"), 1)

                def column(v, c):
                    return v[:, :, bass.ds(i * 2 + c, 1)].rearrange("p t o -> p (t o)")

                def g4(v):
                    return v.rearrange("p (g t n) -> p g t n", g=2, n=128)

                pool.wait_ge(sem("lt_ready"), i + 1)
                level(1)
                for c in range(2):
                    s3 = sst[:, c].rearrange("p (t n) -> p t n", n=128)
                    bt = BC[:, c].rearrange("p (j n) -> p j n", n=128)
                    pool.wait_ge(sem(f"ld_sst{c}"), i * 16 + 16)
                    pst.link(tt(s3, s3, over(column(Esel, c), 128, 2), ALU.mult))
                    level((2, 5)[c])
                    if c:
                        level(6)
                    pool.wait_ge(sem(f"ld_bc{c}"), i * 16 + 16)
                    pool.wait_ge(sem("ysm_ready"), i * 2 + (c + 1))
                    xd = column(XD, c).rearrange("p (g t) -> p g t", g=2)
                    pst.link(tt(g4(stm), over(bt[:, 0:2, :], 4, 2), over(xd, 128, 3), ALU.mult))
                    if c == 0:
                        level(3)
                    pst.link(tt(sst[:, c], sst[:, c], stm, ALU.add))
                    pool.sem_inc(sem("sst_new"), 1)
                    pool.dma_start(ssd_s_out[:, bass.ds(i * 2 + c, 1)],
                                   sst[:, c:c + 1].rearrange("p b (t n) -> p b t n", n=128)
                                   ).then_inc(sem(f"sst_stored{c}"), 16)
                    tt(g4(stm), g4(sst[:, c]), over(bt[:, 2:4, :], 4, 2), ALU.mult).then_inc(sem("stm_ready"), 1)
                    if c == 0:
                        level(4)
                pool.wait_ge(sem("gdn_free"), i + 2)
                pool.dma_start(gdn_p[:, bass.ds(i * 2, 2), :], S2).then_inc(sem("s2_stored"), 16)
                pool.wait_ge(sem("s2_stored"), i * 16 + 16)
                pool.sem_inc(sem("s2_free"), 1)
                pool.wait_ge(sem("stm_ready"), i * 2 + 2)
                for c in range(2):
                    pool.wait_ge(sem(f"sst_stored{c}"), i * 16 + 16)
            pst.leave(4)
            for h in range(8):
                pool.dma_start(gst[h // 4][:, 8 * (h % 4):8 * (h % 4) + 8, :], gdn_s_in[:, h]
                               ).then_inc(sem("ld_gst"), 16)
            pool.wait_ge(sem("skq_ps"), 1)
            for j in range(2):
                s4 = gst[j].rearrange("p (h b) v -> p h b v", b=TS)
                tt(s4, s4, over(SR[:, 16 + 4 * j:20 + 4 * j, 0, :], 128, 3), ALU.mult).then_inc(sem("gst_scaled"), 1)
            pool.wait_ge(sem("vrow_ready"), 1)
            pool.dma_start(a["v_dram"], vrow[0:64]).then_inc(sem("v_out"), 16)
            pool.wait_ge(sem("v_out"), 16)
            for j in range(4):
                if j:
                    pool.wait_ge(sem("gst_ready"), 16 * j)
                pool.dma_start(gvb, a["v_dram"][16 * j:16 * j + 16, :].partition_broadcast(P)
                               ).then_inc(sem("ld_gvb"), 16)
            for j in range(2):
                pool.wait_ge(sem("gst_ready"), 32 * j + 32)
                for h in range(4):
                    pool.dma_start(gdn_s_out[:, 4 * j + h], gst[j][:, 8 * h:8 * h + 8, :]
                                   ).then_inc(sem("gst_stored"), 16)
            pool.wait_ge(sem("x1_done"), N_OUT + SLOTS)
            pool.dma_start(a["x1_dram"], xT).then_inc(sem("x1_stored"), 16)
            pool.wait_ge(sem("gst_stored"), 128)
            pool.dma_start(sk, a["sub_keys"]).then_inc(sem("ld_sk"), 16)
            pool.wait_ge(sem("hso_stored"), 16)
            pool.wait_ge(sem("x1_stored"), 16)

            def gate_rows(n, b, t0):
                pool.wait_ge(sem("soh_ready"), n + 1)
                tt(Boh[:, b], over(Soh[:, b], 3, 2), over(gp[:, bass.ds(t0, GT), :], QE, 3), ALU.mult
                   ).then_inc(sem("boh_ready"), 1)

            pool.wait_ge(sem("tk_ready"), 6)
            pool.wait_ge(sem("gp_ready"), 1)
            with pool.Fori(0, EARLY // 2) as i:
                for b in range(2):
                    gate_rows(i * 2 + b, b, i * (2 * GT) + b * GT)
            pool.wait_ge(sem("gp_ready"), 3)
            with pool.Fori(EARLY // 2, NG // 2) as i:
                for b in range(2):
                    gate_rows(i * 2 + b, b, i * (2 * GT) + b * GT)
            for q in range(1, 4):
                with pool.Fori(0, NG // 2) as i:
                    for b in range(2):
                        gate_rows(i * 2 + (NG * q + b), b, i * (2 * GT) + b * GT)


def kernel(**inputs):
    import numpy as np
    import concourse.bacc as bacc
    from concourse.bass_utils import run_bass_kernel_spmd

    x = {k: np.asarray(v) for k, v in inputs.items()}
    f32 = np.float32

    def feat(v):
        return np.ascontiguousarray(v.reshape(v.shape[0], -1, P).transpose(2, 1, 0))

    def wtiles(w):
        return np.ascontiguousarray(w.reshape(KT, P, -1, P).transpose(2, 1, 0, 3))

    w_in = x["w_in"][0]
    z, xbc, dt, qkv, ar, br, gate = np.split(w_in, [1024, 2560, 2576, 5648, 5656, 5664], axis=1)
    conv_w = np.concatenate([x["gdn_conv_w"][0], x["ssd_conv_w"][0]], axis=1)
    cols = np.zeros((P, 2), f32)
    cols[0:24, 0] = np.concatenate([x["ssd_dt_bias"][0], x["gdn_dt_bias"][0]])
    cols[0:24, 1] = np.concatenate([x["ssd_A_log"][0], x["gdn_A_log"][0]])
    col = lambda v: v.reshape(-1, P).T
    params = np.concatenate([
        col(x["norm1_w"][0]), col(x["norm2_w"][0]), col(x["final_norm_w"]), col(x["b_ada"][0]),
        conv_w.reshape(4, CT, P).transpose(2, 1, 0).reshape(P, CT * 4),
        np.concatenate([np.zeros((P, 24), f32), col(x["ssd_conv_b"][0])], axis=1),
        col(np.repeat(x["ssd_D"][0], 64)), col(x["ssd_norm_w"][0]), col(x["gdn_norm_w"][0]), cols], axis=1)
    j, i = np.meshgrid(np.arange(P), np.arange(P), indexing="ij")
    levels = [((i // (2 * m) == j // (2 * m)) & (i // m % 2 == 1) & (j // m % 2 == 0)) for m in (1, 2, 4, 8, 16, 32, 64)]
    eps = np.zeros((P, 2), f32)
    eps[:, 0], eps[:, 1] = EPS, P * EPS
    consts = np.concatenate([np.eye(P), np.ones((P, P)), i >= j, i + 0.0] + levels + [
                                 eps, np.arange(P)[:, None] % 32 == np.arange(NC),
                                 np.arange(P)[:, None] // TS == np.arange(8), np.arange(P)[:, None] % TS == np.arange(TS)], axis=1).astype(f32)
    state = np.concatenate([x["state_gdn_conv"][0], x["state_ssd_conv"][0]], axis=2)
    u = x["peer_u"][0].reshape(P, P, KT, P)
    arrays = {
        "condT": feat(np.concatenate([x["c_prompt"], x["c_sample"]])),
        "xT": feat(np.concatenate([x["x_prompt"][0], x["x_sample"][:, 0]])),
        "consts": consts, "params": params,
        "w_ada": x["w_ada"][0].reshape(4, 4, P, 24, 512).transpose(3, 0, 2, 1, 4).reshape(96, P, KT, P),
        "w_small": np.concatenate([dt, ar, br], axis=1).reshape(KT, P, 32).transpose(1, 0, 2),
        "w_in": wtiles(np.concatenate([qkv, xbc, z, gate], axis=1)),
        "w_out": wtiles(x["w_out"][0]), "w_q": wtiles(x["peer_w_q"][0]),
        "conv_state": state.reshape(8, 3, CT, P).transpose(3, 2, 0, 1),
        "sub_keys": x["peer_sub_keys"][0].reshape(16, P, P).transpose(2, 0, 1),
        "peer_u": u.transpose(1, 3, 2, 0),
        "peer_v": x["peer_v"][0].reshape(P, 32, 4, 4, 512).transpose(1, 3, 0, 2, 4).reshape(P, P, KT, P),
        "state_ssd": x["state_ssd"][0], "state_gdn": x["state_gdn"][0],
    }
    outs = {"yT": (P, KT, T), "conv_out": (P, CT, 9, 3), "ssd_state_p": (HS, 64, 128), "gdn_state_p": (HG, P, P),
            "ssd_state_s": (TS, HS, 64, 128), "gdn_state_s": (TS, HG, P, P)}
    scratch = {"rows_dram": (32, TP), "smp_dram": (32, 24), "bc_dram": (TS, 4, 128), "v_dram": (64, 128),
               "x1_dram": (P, KT, T)}
    nc = bacc.Bacc("TRN2", target_bir_lowering=False, num_devices=1, dynamic_dma_scratch_size=4096)
    arrays = {f"in_{k}": np.ascontiguousarray(v) for k, v in arrays.items()}
    a = {k[3:]: nc.dram_tensor(k, v.shape, F32, kind="ExternalInput").ap() for k, v in arrays.items()}
    for k, shape in scratch.items():
        a[k] = nc.dram_tensor(k, shape, F32, kind="Internal").ap()
    o = {k: nc.dram_tensor(f"out_{k}", shape, F32, kind="ExternalOutput").ap() for k, shape in outs.items()}
    build(nc, a, o)
    r = run_bass_kernel_spmd(nc, [arrays], core_ids=[0]).results[0]
    y = r["out_yT"].transpose(2, 1, 0).reshape(T, D)
    conv = r["out_conv_out"].transpose(2, 3, 1, 0).reshape(9, 3, CT * P)
    gdn_c, ssd_c = conv[:, :, 0:3072], conv[:, :, 3072:]
    c = np.ascontiguousarray
    return (c(y[None, 0:TP]), c(y[TP:, None]), r["out_ssd_state_p"][None, None], c(ssd_c[None, 0:1]),
            r["out_gdn_state_p"][None, None], c(gdn_c[None, 0:1]), r["out_ssd_state_s"][None], c(ssd_c[None, 1:]),
            r["out_gdn_state_s"][None], c(gdn_c[None, 1:]))
```
